# Optimizing a Trainium2 kernel written in Bass

```python
import math
import jax, jax.numpy as jnp
from jax import lax
import numpy as np

D_MODEL = 2048
BATCH = 1
SEQ = 512
DEPTH = 1
DEC_BATCH = 8
DEC_SEQ = 8
PAST_LEN = 1024
PAGE_SIZE = 128

N_HEADS = 8
HEAD_DIM = 64
V_DIM = 2 * HEAD_DIM
QK_COLS = N_HEADS * 2 * HEAD_DIM
ATTN_WIDTH = N_HEADS * V_DIM
Q_BLOCK = 128
SUBLN_EPS = 1e-5
MASK_VALUE = -1e30
POOL_WINDOWS = (2, 4, 8, 16)
N_POOL_GROUPS = len(POOL_WINDOWS)
POOL_WIDTH = D_MODEL // 2
POOL_GROUP_DIM = POOL_WIDTH // N_POOL_GROUPS
POOL_STATE = max(POOL_WINDOWS) - 1
N_BRANCHES = 2
GATE_COLS = N_BRANCHES * D_MODEL
IN_COLS = 2 * QK_COLS + ATTN_WIDTH + POOL_WIDTH + GATE_COLS
PEER_HEADS = 8
PEER_KEYS = 128
PEER_EXPERTS = PEER_KEYS * PEER_KEYS
PEER_HALF = 128
PEER_QDIM = 2 * PEER_HALF
PEER_TOPK = 16
PEER_BLOCK = 128
NORM_EPS = 1e-6

kernel_name = "diffattn_pool_peer_hybrid_step"

def rms_norm(x, g, eps):
    xf = x.astype(jnp.float32)
    y = xf * lax.rsqrt(jnp.mean(xf * xf, axis=-1, keepdims=True) + eps)
    return (y * g.astype(jnp.float32)).astype(x.dtype)

def diff_lambda(lq1, lk1, lq2, lk2, lam_init):
    f = jnp.float32
    return (jnp.exp(jnp.sum(lq1.astype(f) * lk1.astype(f)))
            - jnp.exp(jnp.sum(lq2.astype(f) * lk2.astype(f))) + lam_init)

def project_in(xn, w_in, b_gate):
    B, T, _ = xn.shape
    z = xn @ w_in
    q, k, v, p, gl = jnp.split(z, [QK_COLS, 2 * QK_COLS, 2 * QK_COLS + ATTN_WIDTH,
                                   2 * QK_COLS + ATTN_WIDTH + POOL_WIDTH], axis=-1)
    q = q.reshape(B, T, N_HEADS, 2, HEAD_DIM)
    k = k.reshape(B, T, N_HEADS, 2, HEAD_DIM)
    v = v.reshape(B, T, N_HEADS, V_DIM)
    gl = (gl + b_gate).reshape(B, T, N_BRANCHES, D_MODEL)
    return q, k, v, p, gl

def diff_attention_block(q, k, v, q_pos, k_pos, lam):
    s = jnp.einsum('bqhcd,bkhcd->bhcqk', q, k).astype(jnp.float32) * (HEAD_DIM ** -0.5)
    mask = k_pos[None, :] <= q_pos[:, None]
    s = jnp.where(mask, s, MASK_VALUE)
    p = jax.nn.softmax(s, axis=-1)
    a = p[:, :, 0] - lam * p[:, :, 1]
    return jnp.einsum('bhqk,bkhe->bqhe', a.astype(v.dtype), v)

def prompt_attention(q, k, v, lam):
    B, T = q.shape[:2]
    nb = T // Q_BLOCK
    pos = jnp.arange(T, dtype=jnp.int32)
    qb = jnp.moveaxis(q.reshape(B, nb, Q_BLOCK, N_HEADS, 2, HEAD_DIM), 1, 0)
    pb = pos.reshape(nb, Q_BLOCK)
    ob = lax.map(lambda a: diff_attention_block(a[0], k, v, a[1], pos, lam), (qb, pb))
    return jnp.moveaxis(ob, 0, 1).reshape(B, T, N_HEADS, V_DIM)

def sample_attention(q, k, v, lam, past_k, past_v, page_table):
    DB, T = q.shape[:2]
    past_len = page_table.shape[1] * PAGE_SIZE
    kp = past_k[page_table].reshape(DB, past_len, N_HEADS, 2, HEAD_DIM)
    vp = past_v[page_table].reshape(DB, past_len, N_HEADS, V_DIM)
    k_all = jnp.concatenate([kp, k], axis=1)
    v_all = jnp.concatenate([vp, v], axis=1)
    q_pos = past_len + jnp.arange(T, dtype=jnp.int32)
    k_pos = jnp.arange(past_len + T, dtype=jnp.int32)
    return diff_attention_block(q, k_all, v_all, q_pos, k_pos, lam)

def pool_branch(p_new, p_prev, start_pos, pool_w, pool_scale):
    B, T, _ = p_new.shape
    P = p_prev.shape[1]
    ext = jnp.concatenate([p_prev, p_new], axis=1)
    cs = jnp.concatenate([jnp.zeros((B, 1, POOL_WIDTH), jnp.float32),
                          jnp.cumsum(ext.astype(jnp.float32), axis=1)], axis=1)
    end = cs[:, P + 1:]
    pos = start_pos + jnp.arange(T, dtype=jnp.int32)
    outs = []
    for g, w in enumerate(POOL_WINDOWS):
        sl = slice(g * POOL_GROUP_DIM, (g + 1) * POOL_GROUP_DIM)
        win_sum = end[..., sl] - cs[:, P + 1 - w:P + 1 - w + T, sl]
        count = jnp.minimum(pos + 1, w).astype(jnp.float32)
        outs.append(win_sum / count[None, :, None])
    pooled = jnp.concatenate(outs, axis=-1)
    d = (pooled - p_new.astype(jnp.float32)).reshape(B, T, N_POOL_GROUPS, POOL_GROUP_DIM)
    mixed = jnp.einsum('btgc,gcd->btgd', d, pool_w.astype(jnp.float32)).reshape(B, T, POOL_WIDTH)
    out = (mixed * pool_scale.astype(jnp.float32)).astype(p_new.dtype)
    return out, ext[:, -P:]

def peer_block(h, w_q, sub_keys, u, v):
    N = h.shape[0]
    q = (h @ w_q).reshape(N, PEER_HEADS, 2, PEER_HALF)
    s = jnp.einsum('nhcd,hckd->nhck', q, sub_keys).astype(jnp.float32)
    sv, si = lax.top_k(s, PEER_TOPK)
    cand = (sv[:, :, 0, :, None] + sv[:, :, 1, None, :]).reshape(N, PEER_HEADS, PEER_TOPK * PEER_TOPK)
    cidx = (si[:, :, 0, :, None] * PEER_KEYS + si[:, :, 1, None, :]).reshape(N, PEER_HEADS, PEER_TOPK * PEER_TOPK)
    top_s, top_p = lax.top_k(cand, PEER_TOPK)
    experts = jnp.take_along_axis(cidx, top_p, axis=-1)
    gate = jax.nn.softmax(top_s, axis=-1)
    act = jax.nn.gelu(jnp.einsum('nd,nhkd->nhk', h, u[experts]).astype(jnp.float32), approximate=False)
    return jnp.einsum('nhk,nhkd->nd', (gate * act).astype(h.dtype), v[experts])

def peer_ffn(h, w_q, sub_keys, u, v):
    B, T, D = h.shape
    N = B * T
    nb = -(-N // PEER_BLOCK)
    hf = jnp.pad(h.reshape(N, D), ((0, nb * PEER_BLOCK - N), (0, 0)))
    out = lax.map(lambda hb: peer_block(hb, w_q, sub_keys, u, v), hf.reshape(nb, PEER_BLOCK, D))
    return out.reshape(nb * PEER_BLOCK, D)[:N].reshape(B, T, D)

def layer_step(x, attend, pool_prev, start_pos, lam, lam_init, norm1_g, w_in, b_gate, subln_g,
               w_attn_branch, pool_w, pool_scale, w_pool_branch, w_out, norm2_g,
               w_peer_q, peer_sub_keys, peer_u, peer_v):
    B, T, _ = x.shape
    xn = rms_norm(x, norm1_g, NORM_EPS)
    q, k, v, p, gl = project_in(xn, w_in, b_gate)
    o = attend(q, k, v, lam)
    o = rms_norm(o, subln_g, SUBLN_EPS) * (1.0 - lam_init)
    a_out = o.reshape(B, T, ATTN_WIDTH) @ w_attn_branch
    pool_o, pool_state = pool_branch(p, pool_prev, start_pos, pool_w, pool_scale)
    b_out = pool_o @ w_pool_branch
    gates = jax.nn.sigmoid(gl.astype(jnp.float32))
    merged = (gates[:, :, 0] * a_out.astype(jnp.float32)
              + gates[:, :, 1] * b_out.astype(jnp.float32)).astype(x.dtype)
    h = x + merged @ w_out
    y = h + peer_ffn(rms_norm(h, norm2_g, NORM_EPS), w_peer_q, peer_sub_keys, peer_u, peer_v)
    return y, k, v, pool_state

def setup_inputs(seed: int = 0) -> dict:
    key = jax.random.key(seed)
    ks = jax.random.split(key, 32)
    n_pages = PAST_LEN // PAGE_SIZE
    n_phys = (DEC_BATCH * n_pages * 5) // 4
    nrm = jax.random.normal
    f = jnp.float32
    page_table = jax.random.permutation(ks[0], n_phys)[:DEC_BATCH * n_pages].reshape(DEC_BATCH, n_pages).astype(jnp.int32)
    return {
        'x_prompt': nrm(ks[1], (BATCH, SEQ, D_MODEL), f),
        'x_sample': nrm(ks[2], (DEC_BATCH, DEC_SEQ, D_MODEL), f),
        'cache_k': nrm(ks[3], (DEPTH, n_phys, PAGE_SIZE, N_HEADS, 2, HEAD_DIM), f),
        'cache_v': nrm(ks[4], (DEPTH, n_phys, PAGE_SIZE, N_HEADS, V_DIM), f),
        'state_pool': nrm(ks[5], (DEPTH, DEC_BATCH, POOL_STATE, POOL_WIDTH), f),
        'page_table': page_table,
        'norm1_g': 1.0 + 0.01 * nrm(ks[6], (DEPTH, D_MODEL), f),
        'w_in': nrm(ks[7], (DEPTH, D_MODEL, IN_COLS), f) * D_MODEL ** -0.5,
        'b_gate': 0.1 * nrm(ks[8], (DEPTH, GATE_COLS), f),
        'lambda_q1': 0.1 * nrm(ks[9], (DEPTH, HEAD_DIM), f),
        'lambda_k1': 0.1 * nrm(ks[10], (DEPTH, HEAD_DIM), f),
        'lambda_q2': 0.1 * nrm(ks[11], (DEPTH, HEAD_DIM), f),
        'lambda_k2': 0.1 * nrm(ks[12], (DEPTH, HEAD_DIM), f),
        'subln_g': 1.0 + 0.01 * nrm(ks[13], (DEPTH, V_DIM), f),
        'w_attn_branch': nrm(ks[14], (DEPTH, ATTN_WIDTH, D_MODEL), f) * ATTN_WIDTH ** -0.5,
        'pool_w': nrm(ks[15], (DEPTH, N_POOL_GROUPS, POOL_GROUP_DIM, POOL_GROUP_DIM), f) * POOL_GROUP_DIM ** -0.5,
        'pool_scale': 1.0 + 0.1 * nrm(ks[16], (DEPTH, POOL_WIDTH), f),
        'w_pool_branch': nrm(ks[17], (DEPTH, POOL_WIDTH, D_MODEL), f) * POOL_WIDTH ** -0.5,
        'w_out': nrm(ks[18], (DEPTH, D_MODEL, D_MODEL), f) * D_MODEL ** -0.5,
        'norm2_g': 1.0 + 0.01 * nrm(ks[19], (DEPTH, D_MODEL), f),
        'w_peer_q': nrm(ks[20], (DEPTH, D_MODEL, PEER_HEADS * PEER_QDIM), f) * D_MODEL ** -0.5,
        'peer_sub_keys': nrm(ks[21], (DEPTH, PEER_HEADS, 2, PEER_KEYS, PEER_HALF), f) * PEER_HALF ** -0.5,
        'peer_u': nrm(ks[22], (DEPTH, PEER_EXPERTS, D_MODEL), f) * D_MODEL ** -0.5,
        'peer_v': 0.5 * nrm(ks[23], (DEPTH, PEER_EXPERTS, D_MODEL), f),
        'norm_f_g': 1.0 + 0.01 * nrm(ks[24], (D_MODEL,), f),
    }

def reference(x_prompt, x_sample, cache_k, cache_v, state_pool, page_table, norm1_g, w_in, b_gate,
              lambda_q1, lambda_k1, lambda_q2, lambda_k2, subln_g, w_attn_branch, pool_w, pool_scale,
              w_pool_branch, w_out, norm2_g, w_peer_q, peer_sub_keys, peer_u, peer_v, norm_f_g):
    yp, ys = x_prompt, x_sample
    past_len = page_table.shape[1] * PAGE_SIZE
    kp_rows, vp_rows, pp_states, ks_rows, vs_rows, ps_states = [], [], [], [], [], []
    for l in range(DEPTH):
        lam_init = 0.8 - 0.6 * math.exp(-0.3 * l)
        lam = diff_lambda(lambda_q1[l], lambda_k1[l], lambda_q2[l], lambda_k2[l], lam_init)
        weights = (norm1_g[l], w_in[l], b_gate[l], subln_g[l], w_attn_branch[l], pool_w[l], pool_scale[l],
                   w_pool_branch[l], w_out[l], norm2_g[l], w_peer_q[l], peer_sub_keys[l], peer_u[l], peer_v[l])
        pool0 = jnp.zeros((yp.shape[0], POOL_STATE, POOL_WIDTH), yp.dtype)
        yp, kp, vp, pp = layer_step(yp, prompt_attention, pool0, 0, lam, lam_init, *weights)
        ck, cv = cache_k[l], cache_v[l]
        attend_s = lambda q, k, v, lm: sample_attention(q, k, v, lm, ck, cv, page_table)
        ys, kss, vss, pss = layer_step(ys, attend_s, state_pool[l], past_len, lam, lam_init, *weights)
        kp_rows.append(kp); vp_rows.append(vp); pp_states.append(pp)
        ks_rows.append(kss); vs_rows.append(vss); ps_states.append(pss)
    yp = rms_norm(yp, norm_f_g, NORM_EPS)
    ys = rms_norm(ys, norm_f_g, NORM_EPS)
    return (yp, ys, jnp.stack(kp_rows), jnp.stack(vp_rows), jnp.stack(pp_states),
            jnp.stack(ks_rows), jnp.stack(vs_rows), jnp.stack(ps_states))


_drawn_inputs = setup_inputs


def setup_inputs(seed=0):
    import zlib

    import numpy as np

    out = dict(_drawn_inputs(seed))
    spreads = {}
    factors = {'lambda_q1': 3.037,
     'lambda_k1': 5.6,
     'subln_g': 45.905,
     'norm_f_g': 181.613,
     'norm2_g': 18.287,
     'pool_scale': 4.317}
    for name, (base, spread) in spreads.items():
        noise = np.random.default_rng([zlib.crc32(name.encode()), seed]).standard_normal(out[name].shape)
        drawn = base * np.exp(spread * noise) if base else spread * noise
        out[name] = __import__('jax').numpy.asarray(drawn.astype(out[name].dtype))
    for name, factor in factors.items():
        out[name] = (out[name] * factor).astype(out[name].dtype)
    return out
```

```python
import math

import numpy as np
import concourse.bass as bass
from concourse import mybir
from contextlib import ExitStack

F = mybir.dt.float32
R = mybir.dt.float32r
I32 = mybir.dt.int32
U32 = mybir.dt.uint32
ALU = mybir.AluOpType
ACT = mybir.ActivationFunctionType
AX = mybir.AxisListType

P = 128
D = 2048
KD = D // P
SEQ, DB, DT = 512, 8, 8
NS = DB * DT
T = SEQ + NS
TH = T // 2
TB = 5
H, HD, VD = 8, 64, 128
PAGES = 8
POOLW, PSTATE = 1024, 15
WINDOWS = (2, 4, 8, 16)
PH, PK, TOPK = 8, 128, 16
NEG = -1e30
SUBLN_EPS, NORM_EPS = 1e-5, 1e-6
LAM_INIT = 0.8 - 0.6 * math.exp(0.0)

T_Q, T_K, T_V, T_P, T_G = 0, 8, 16, 24, 32
N_IN = 64
N_BR, N_OUT, N_PQ = 16, 16, 16
G_BR = N_IN
G_OUT = G_BR + N_BR
G_PQ = G_OUT + N_OUT
G_U = G_PQ + N_PQ
N_W = G_U
N_U = PK
NTOK_G = 16
GB = 64


def tokens(tb):
    return P if tb < TB - 1 else NS


def hybrid_step(nc, x_prompt, x_sample, cache_k, cache_v, state_pool, page_table, norm1_g, w_in, b_gate,
                lambda_q1, lambda_k1, lambda_q2, lambda_k2, subln_g, w_attn_branch, pool_w, pool_scale,
                w_pool_branch, w_out, norm2_g, w_peer_q, peer_sub_keys, peer_u, peer_v, norm_f_g,
                y_prompt, y_sample, k_prompt, v_prompt, pool_prompt, k_sample, v_sample, pool_sample):
    ctx = ExitStack()
    with ctx:
        ctx.enter_context(nc.allow_non_contiguous_dma("columns of gains and biases"))
        BASE = (nc.sbuf_base + 63) // 64 * 64
        U = KD * T * 4
        A_ACT, A_MAIN = 0, 2 * U
        A_RING = 3 * U
        A_CONST = A_RING + 6 * KD * P * 4
        A_X = A_CONST + 4352

        class Region:
            def __init__(self, at, end):
                self.at, self.end = BASE + at, BASE + end

            def __call__(self, name, shape, dt=F):
                size = int(np.prod(shape[1:])) * 4
                t = nc.alloc_sbuf_tensor_at(name, shape, dt, offset=self.at)
                self.at += (size + 31) // 32 * 32
                assert self.at <= self.end, (name, self.at - self.end)
                return t

        END = nc.sbuf_usable_end // 32 * 32 - BASE
        r = Region(A_ACT, A_MAIN)
        act_hi = r("act_hi", [P, KD, T], R)
        act_lo = r("act_lo", [P, KD, T], R)
        main = Region(A_MAIN, A_RING)("main", [P, KD, T])
        r = Region(A_RING, A_CONST)
        w_raw = [r(f"w_raw{s}", [P, KD, P]) for s in range(2)]
        w_hi = [r(f"w_hi{s}", [P, KD, P], R) for s in range(2)]
        w_lo = [r(f"w_lo{s}", [P, KD, P], R) for s in range(2)]
        r = Region(A_CONST, A_X)
        ident = r("ident", [P, P])
        ones = r("ones", [P, P])
        mask_diag = r("mask_diag", [P, P])
        mask_new = r("mask_new", [P, 120])
        iota_f = r("iota_f", [P, P])
        iota_i = r("iota_i", [P, P], I32)
        g1c, g2c, gfc = r("g1c", [P, KD]), r("g2c", [P, KD]), r("gfc", [P, KD])
        subgc = r("subgc", [P, 1])
        subgc8 = r("subgc8", [P, 1])
        pscale_c = r("pscale_c", [P, 8])
        bgate_c = r("bgate_c", [P, 32])
        cinv = r("cinv", [P, 4, 16])
        page_i = r("page_i", [P, DB * PAGES], I32)
        page_rows = r("page_rows", [P, DB * PAGES], U32)
        col_i = r("col_i", [P, 4], I32)
        col_f = r("col_f", [P, 8])
        lam_v = r("lam_v", [P, 4])
        lam_c = r("lam_c", [P, 2])
        r = Region(A_X, END)
        tmp = r("tmp", [P, 2, T])
        rstd = r("rstd", [P, T])
        v_nat = r("v_nat", [P, TB, H * VD])
        pT = r("pT", [P, 8, T])
        k_stage = r("k_stage", [P, TB, P])
        r = Region(A_X, END)
        r("tmp_", [P, 3, T])
        x_in = r("x_in", [P, 2, D])
        lam_raw = Region(A_ACT, A_MAIN)("lam_raw", [P, 5, HD])
        r = Region(A_ACT, A_MAIN)
        qd = r("qd", [P, 8 * 144])
        K_RING = 3
        k_page = [r(f"k_page{s}", [P, H * P]) for s in range(K_RING)]
        kT_page = [r(f"kT_page{s}", [P, H, P]) for s in range(2)]
        sp_ = r("sp_", [P, 1024 + NS])
        s_aT = r("s_aT", [P, PAGES, NS])
        s_aTn = r("s_aTn", [NS, NS])
        s_stat = r("s_stat", [P, 8])
        shared_at = r.at - BASE
        v_page = [r(f"v_page{s}", [P, H * VD]) for s in range(PAGES)]
        r = Region(shared_at, A_MAIN)
        pp = [r(f"pp{s}", [P, 2, SEQ]) for s in range(2)]
        pa_buf = [r(f"pa{s}", [P, SEQ]) for s in range(2)]
        paT = [r(f"paT{s}", [P, 4, P]) for s in range(2)]
        p_stat = r("p_stat", [P, 2, 8])
        r = Region(shared_at, A_MAIN)
        SEG = PSTATE + DT
        EXL = PSTATE + SEQ + DB * SEG
        ex = [r(f"ex{s}", [P, 2, EXL]) for s in range(2)]
        st_rows = r("st_rows", [P, POOLW])
        stT = r("stT", [P, 8, DB * PSTATE])
        pool_rows = r("pool_rows", [NS, 2, POOLW])
        pw = Region(A_MAIN + U // 2, A_RING)("pw", [P, 2, 256])
        r = Region(A_X, END)
        r("tmp__", [P, 3, T])
        back = r("back", [P, 4, T])
        mtmp = r("mtmp", [P, 2, T])
        r = Region(A_X, END)
        r("tmp___", [P, 2, T])
        iaT = r("iaT", [P, T])
        ibT = r("ibT", [P, T])
        gT = r("gT", [P, T])
        gTh = r("gTh", [P, T], R)
        x2 = r.at - BASE
        q_ev = r("q_ev", [P, 2, T])
        sk_raw = r("sk_raw", [P, 2, P])
        skT = r("skT", [P, 2, P])
        s_ev = r("s_ev", [P, 2, TB, PK])
        sv = r("sv", [P, TB, 16, 16])
        si = r("si", [P, TB, 16, 16], U32)
        r = Region(A_RING, A_CONST)
        si_f = r("si_f", [P, 16, 16])
        cand = r("cand", [P, PH, 256])
        ts = r("ts", [P, PH, TOPK])
        tp = r("tp", [P, PH, TOPK], U32)
        tpa = r("tpa", [P, 2, PH * TOPK], U32)
        tpf = r("tpf", [P, 2, PH * TOPK])
        oh = r("oh", [P, PH * TOPK, 16])
        ohv = r("ohv", [P, PH * TOPK, 16])
        sel = r("sel", [P, 3, PH * TOPK])
        ssum = r("ssum", [P, 2, PH])
        r = Region(A_RING, A_CONST)
        oi = [r(f"oi{s}", [P, NTOK_G, PK], R) for s in range(2)]
        jh = [r(f"jh{s}", [P, NTOK_G, PK], R) for s in range(2)]
        jl = [r(f"jl{s}", [P, NTOK_G, PK], R) for s in range(2)]
        gmat = Region(x2, END)("gmat", [P, PK, GB])
        r = Region(A_ACT, A_MAIN)
        v_hi = [r(f"v_hi{s}", [P, D], R) for s in range(4)]
        v_lo = [r(f"v_lo{s}", [P, D], R) for s in range(4)]
        r = Region(A_RING, A_CONST)
        v_raw = [r(f"v_raw{s}", [P, D]) for s in range(2)]
        wx_hi = [r(f"wx_hi{s}", [P, T], R) for s in range(4)]
        wx_lo = [r(f"wx_lo{s}", [P, T], R) for s in range(4)]
        r = Region(A_X, END)
        a_back = [r(f"a_back{s}", [P, T]) for s in range(2)]
        g_back = [r(f"g_back{s}", [P, T // GB, GB]) for s in range(2)]
        wx = [r(f"wx{s}", [P, T]) for s in range(2)]
        y_rows = Region(A_ACT, A_MAIN)("y_rows", [P, TB, D])

        pair = [ctx.enter_context(nc.psum_tensor(f"pair{i}", [P, 2, 512], F)) for i in range(4)]

        def halves(n):
            return pair[n][:, :, 0:TH]

        def as_halves(t):
            return t.rearrange("p (a t) -> p a t", a=2)

        xT_dram = nc.dram_tensor("xT_dram", [KD, P, T], F).ap()
        gate_dram = nc.dram_tensor("gate_dram", [32, P, T], F).ap()
        gmat_dram = nc.dram_tensor("gmat_dram", [T // GB, P, PK, GB], F).ap()
        gelu_dram = nc.dram_tensor("gelu_dram", [N_U, P, T], F).ap()
        ck = cache_k.rearrange("l n s h c d -> (l n s) (h c d)")
        cv = cache_v.rearrange("l n s h e -> (l n s) (h e)")
        u_tiles = peer_u.rearrange("l (i j) d -> (l i) j d", j=PK)
        v_tiles = peer_v.rearrange("l (i j) d -> (l i) j d", j=PK)

        def sem(name):
            return ctx.enter_context(nc.semaphore(name))

        const_in = sem("const_in")
        pool_const = sem("pool_const")
        vec_const = sem("vec_const")
        lam_exp, lam_dots = sem("lam_exp"), sem("lam_dots")
        chain = sem("chain")
        x_loaded = [sem(f"x_loaded{s}") for s in range(2)]
        xt_mm, xt_ev_act, xt_ev_dve = sem("xt_mm"), sem("xt_ev_act"), sem("xt_ev_dve")
        xT_saved = sem("xT_saved")
        raw_in = [sem(f"raw_in{s}") for s in range(2)]
        hi_done, lo_done, tile_done = sem("hi_done"), sem("lo_done"), sem("tile_done")
        out_act, out_dve = sem("out_act"), sem("out_dve")
        nat_mm, nat_ev = sem("nat_mm"), sem("nat_ev")
        k_out, v_out = sem("k_out"), sem("v_out")
        gate_out = [sem(f"gate_out{s}") for s in range(2)]
        pool_in, pool_t_mm, pool_t_ev = sem("pool_in"), sem("pool_t_mm"), sem("pool_t_ev")
        pool_d = sem("pool_d")
        pool_out = sem("pool_out")
        pw_in, pw_mm, pw_val, pw_hi, pw_ev = (sem(n) for n in ("pw_in", "pw_mm", "pw_val", "pw_hi", "pw_ev"))
        pa_s, pa_max, pa_exp, pa_a, pa_tmm, pa_tev, pa_o, pa_oev = (
            sem(n) for n in ("pa_s", "pa_max", "pa_exp", "pa_a", "pa_tmm", "pa_tev", "pa_o", "pa_oev"))
        kp_in = [sem(f"kp_in{s}") for s in range(K_RING)]
        vp_in = [sem(f"vp_in{s}") for s in range(PAGES)]
        sa_qd, sa_tmm, sa_tev_a, sa_tev_d, sa_s, sa_max, sa_exp, sa_p, sa_ptmm, sa_cp, sa_aT, sa_o, sa_oev = (
            sem(n) for n in ("sa_qd", "sa_tmm", "sa_tev_a", "sa_tev_d", "sa_s", "sa_max", "sa_exp", "sa_p",
                             "sa_ptmm", "sa_cp", "sa_aT", "sa_o", "sa_oev"))
        NORMS = ("n1", "sub", "n2", "nf")
        sq_done, sq_used, n_var, n_sqrt, n_val, n_hi, n_lo = (
            {k: sem(f"{n}_{k}") for k in NORMS} for n in ("sq_done", "sq_used", "n_var", "n_sqrt", "n_val", "n_hi", "n_lo"))
        back_in = [sem(f"back_in{s}") for s in range(2)]
        merged_sum, mg_hi, mg_lo = sem("merged_sum"), sem("mg_hi"), sem("mg_lo")
        rows_in = sem("rows_in")
        sk_in = [sem(f"sk_in{s}") for s in range(2)]
        sk_tmm, sk_tev, q_evd, sc_mm, sc_ev, top_done = (
            sem(n) for n in ("sk_tmm", "sk_tev", "q_evd", "sc_mm", "sc_ev", "top_done"))
        gx_in, gx_exp, sel_done, sel_tmm, sel_tev, idx_done = (
            sem(n) for n in ("gx_in", "gx_exp", "sel_done", "sel_tmm", "sel_tev", "idx_done"))
        oh_v, oh_p, gm_mm, gm_ev, gm_ev_d, gm_out = (
            sem(n) for n in ("oh_v", "oh_p", "gm_mm", "gm_ev", "gm_ev_d", "gm_out"))
        u_in = [sem(f"u_in{s}") for s in range(2)]
        u_tmm, u_hi, u_lo, a_done, a_gelu = (sem(n) for n in ("u_tmm", "u_hi", "u_lo", "a_done", "a_gelu"))
        a_out = [sem(f"a_out{s}") for s in range(2)]
        v_in = [sem(f"v_in{s}") for s in range(2)]
        ag_in = [sem(f"ag_in{s}") for s in range(2)]
        v_hid, v_lod, wx_val, wx_hid, wx_lod, vt_done, acc_ps, acc_done = (
            sem(n) for n in ("v_hid", "v_lod", "wx_val", "wx_hid", "wx_lod", "vt_done", "acc_ps", "acc_done"))
        yt_mm, yt_ev, y_out = sem("yt_mm"), sem("yt_ev"), sem("y_out")

        block = ctx.enter_context(nc.Block())

        def col_view(a, n):
            return a.rearrange("l (k p) -> p (l k)", p=P) if len(a.shape) == 2 else a.rearrange("(k p) -> p k", p=P)

        def ring_source(g):
            if g < G_BR:
                return [(w_in[0, :, g * P:(g + 1) * P].rearrange("(k p) c -> p k c", p=P), 0, KD)]
            if g < G_OUT:
                c = slice((g - G_BR) * P, (g - G_BR + 1) * P)
                return [(w_attn_branch[0, :, c].rearrange("(k p) c -> p k c", p=P), 0, 8),
                        (w_pool_branch[0, :, c].rearrange("(k p) c -> p k c", p=P), 8, 8)]
            w, g = (w_out, g - G_OUT) if g < G_PQ else (w_peer_q, g - G_PQ)
            return [(w[0, :, g * P:(g + 1) * P].rearrange("(k p) c -> p k c", p=P), 0, KD)]

        def raw_count(g):
            n = sum(2 if G_BR <= m < G_OUT else 1 for m in range(g % 2, g + 1, 2))
            return 16 * n

        OUT_ACT = [t for t in range(N_IN) if t < T_K or t >= T_G]
        OUT_DVE = [t for t in range(N_IN) if T_K <= t < T_G]

        def wait_w_in_out(eng, t):
            if t in OUT_ACT:
                eng.wait_ge(out_act, OUT_ACT.index(t) + 1)
            else:
                eng.wait_ge(out_dve, OUT_DVE.index(t) + 1)



        def split_waits_norm(eng, key, done):
            eng.wait_ge(n_hi[key], done)
            eng.wait_ge(n_lo[key], done)

        @block.sync
        def _(sp):
            for s in range(2):
                sp.dma_start(x_in[:, s, :], x_prompt[0, s * P:(s + 1) * P, :]).then_inc(x_loaded[s], 16)

            def load_tile(g):
                if g >= 2:
                    sp.wait_ge(lo_done, g - 1)
                for src, k0, n in ring_source(g):
                    sp.dma_start(w_raw[g % 2][:, k0:k0 + n, :], src).then_inc(raw_in[g % 2], 16)

            for i, v in enumerate((lambda_q1, lambda_k1, lambda_q2, lambda_k2)):
                sp.dma_start(lam_raw[:, i, :], v.broadcast_to([P, HD])).then_inc(const_in, 16)
            for dst, src in ((g1c, norm1_g), (g2c, norm2_g), (gfc, norm_f_g), (subgc, subln_g),
                             (pscale_c, pool_scale), (bgate_c, b_gate)):
                sp.dma_start(dst[:, :], col_view(src, P)).then_inc(const_in, 16)
            sp.dma_start(page_i[:, :], page_table.rearrange("b g -> (b g)").unsqueeze(0)
                         .broadcast_to([P, DB * PAGES])).then_inc(const_in, 16)
            load_tile(0)
            load_tile(1)
            for tb in range(2, TB):
                sp.wait_ge(xt_mm, tb - 1)
                src = x_prompt[0, tb * P:(tb + 1) * P, :] if tb < 4 else x_sample.rearrange("b t d -> (b t) d")
                sp.dma_start(x_in[0:tokens(tb), tb % 2, :], src).then_inc(x_loaded[tb % 2], 16)
            for g in range(2, G_U):
                load_tile(g)
            sp.wait_ge(gm_mm, T // NTOK_G)
            for s in range(2):
                sp.dma_start(w_raw[s][:, :, :].rearrange("p k c -> p (k c)"), u_tiles[:, s, :]).then_inc(u_in[s], 16)
            with sp.Fori(1, N_U // 2) as hh:
                for s in range(2):
                    sp.wait_ge(u_tmm, hh * 2 + (s - 1))
                    sp.dma_start(w_raw[s][:, :, :].rearrange("p k c -> p (k c)"),
                                 u_tiles[:, bass.ds(hh * 2 + s, 1), :].rearrange("p a d -> p (a d)")
                                 ).then_inc(u_in[s], 16)

            def load_v(n, i):
                s = i % 2
                def one(ap, m):
                    return ap[:, m, :] if isinstance(m, int) else ap[:, bass.ds(m, 1), :].rearrange("p a d -> p (a d)")
                sp.dma_start(v_raw[s][:, :], one(v_tiles, n)).then_inc(v_in[s], 16)
                sp.dma_start(a_back[s][:, :], one(gelu_dram.rearrange("j i t -> i j t"), n)).then_inc(ag_in[s], 16)
                g = gmat_dram.rearrange("b i j t -> i b j t")
                g = g[:, :, n, :] if isinstance(n, int) else g[:, :, bass.ds(n, 1), :].rearrange("i b j t -> i b (j t)")
                sp.dma_start(g_back[s][:, :, :], g).then_inc(ag_in[s], 16)

            sp.wait_ge(a_done, N_U)
            for s in range(2):
                sp.wait_ge(a_out[s], 16 * N_U // 2)
            sp.wait_ge(gm_out, 16 * (T // GB))
            for i in range(4):
                if i >= 2:
                    sp.wait_ge(v_lod, i - 1)
                    sp.wait_ge(wx_val, i - 1)
                load_v(i, i)
            with sp.Fori(1, N_U // 4) as q:
                for i in range(4):
                    sp.wait_ge(v_lod, q * 4 + (i - 1))
                    sp.wait_ge(wx_val, q * 4 + (i - 1))
                    load_v(q * 4 + i, i)
            sp.wait_ge(yt_ev, 2 * KD)
            sp.dma_start(y_prompt[0].rearrange("(b p) d -> p b d", p=P), y_rows[:, 0:4, :]).then_inc(y_out, 16)
            sp.dma_start(y_sample.rearrange("b t d -> (b t) d"), y_rows[0:NS, 4, :]).then_inc(y_out, 16)
            sp.wait_ge(y_out, 32)

        @block.gpsimd
        def _(pool):
            g = nc.gpsimd
            g.memset(ident[:, :], 0.0).then_inc(pool_const, 1)
            g.memset(ones[:, :], 1.0).then_inc(pool_const, 1)
            g.memset(mask_diag[:, :], 0.0).then_inc(pool_const, 1)
            g.iota(iota_i[:, :], pattern=[[1, P]], base=0, channel_multiplier=0).then_inc(pool_const, 1)
            g.iota(col_i[:, 0:1], pattern=[[1, 1]], base=0, channel_multiplier=1).then_inc(pool_const, 1)
            pool.wait_ge(pool_const, 5)
            g.affine_select(out=ident[:, :], in_=ident[:, :], compare_op=ALU.not_equal, fill=1.0, base=0,
                            pattern=[[-1, P]], channel_multiplier=1).then_inc(pool_const, 1)
            g.affine_select(out=mask_diag[:, :], in_=mask_diag[:, :], compare_op=ALU.is_ge, fill=NEG, base=0,
                            pattern=[[-1, P]], channel_multiplier=1).then_inc(pool_const, 1)
            pool.wait_ge(vec_const, 1)
            g.affine_select(out=mask_new[:, :], in_=mask_new[:, :], compare_op=ALU.is_ge, fill=NEG, base=-56,
                            pattern=[[1, 120]], channel_multiplier=0).then_inc(pool_const, 1)
            pool.wait_ge(xt_ev_act, TB)
            pool.wait_ge(xt_ev_dve, TB)
            pool.dma_start(xT_dram.rearrange("k p t -> p k t"), main[:, :, :]).then_inc(xT_saved, 16)
            for h in range(H):
                pool.wait_ge(nat_ev, 2 * (h + 1))
                pool.dma_start(k_prompt[0, 0].rearrange("(b p) h c d -> p b h (c d)", p=P)[:, :, h, :],
                               k_stage[:, 0:4, :]).then_inc(k_out, 16)
                pool.dma_start(k_sample[0].rearrange("b t h c d -> (b t) h (c d)")[:, h, :],
                               k_stage[0:NS, 4, :]).then_inc(k_out, 16)
            pool.wait_ge(nat_ev, 32)
            pool.dma_start(v_prompt[0, 0].rearrange("(b p) h e -> p b (h e)", p=P), v_nat[:, 0:4, :]).then_inc(v_out, 16)
            pool.dma_start(v_sample[0].rearrange("b t h e -> (b t) (h e)"), v_nat[0:NS, 4, :]).then_inc(v_out, 16)
            for n in range(32):
                pool.wait_ge(out_act, 8 + n + 1)
                pool.dma_start(gate_dram[n], tmp[:, n % 2, :]).then_inc(gate_out[n % 2], 16)
            pool.wait_ge(tile_done, N_IN)
            pool.dma_start(st_rows[0:DB * PSTATE, :], state_pool.rearrange("l b s c -> (l b s) c")).then_inc(pool_in, 16)
            pool.dma_start(pool_sample[0, :, 0:PSTATE - DT, :], state_pool[0, :, DT:PSTATE, :]).then_inc(pool_out, 16)
            pool.wait_ge(pool_t_ev, 3)
            pool.dma_start(pool_prompt[0, 0], pool_rows[0:PSTATE, 0, :]).then_inc(pool_out, 16)
            for b in range(DB):
                pool.dma_start(pool_sample[0, b, PSTATE - DT:PSTATE, :],
                               pool_rows[b * DT:(b + 1) * DT, 1, :]).then_inc(pool_out, 16)

            def gather(dst, cache, n, s):
                pool.indirect_dma_start(out=dst[:, :], out_offset=None, in_=cache,
                                        in_offset=bass.IndirectOffsetOnAxis(ap=page_rows[:, n:n + 1], axis=0)
                                        ).then_inc(s, 16)

            for n in range(K_RING):
                gather(k_page[n], ck, n, kp_in[n])
            pool.wait_ge(pool_out, 16 * (2 + DB))
            pool.wait_ge(pool_d, 4)
            pool.wait_ge(pa_oev, 4 * H)
            for b in range(DB):
                for g_ in range(PAGES):
                    n = b * PAGES + g_
                    if b:
                        pool.wait_ge(sa_o, b)
                    gather(v_page[g_], cv, n, vp_in[g_])
                    if n + K_RING < DB * PAGES:
                        pool.wait_ge(sa_tmm, n + 1)
                        gather(k_page[n % K_RING], ck, n + K_RING, kp_in[n % K_RING])
            pool.wait_ge(sa_oev, DB)
            for g_ in range(4):
                if g_:
                    pool.wait_ge(pw_mm, 2 * g_)
                pool.dma_start(pw[:, :, :], pool_w[0, g_].rearrange("(k p) d -> p k d", p=P)).then_inc(pw_in, 16)
            for s in range(2):
                pool.wait_ge(gate_out[s], 16 * 16)
            pool.wait_ge(pw_ev, 8)
            for n in range(N_BR):
                if n >= 2:
                    pool.wait_ge(merged_sum, n - 1)
                pool.dma_start(back[:, n % 2, :], gate_dram[n]).then_inc(back_in[n % 2], 16)
                pool.dma_start(back[:, 2 + n % 2, :], gate_dram[KD + n]).then_inc(back_in[n % 2], 16)
            pool.wait_ge(xT_saved, 16)
            for m in range(N_OUT):
                if m < 2:
                    pool.wait_ge(merged_sum, N_BR - 1 + m)
                else:
                    pool.wait_ge(out_dve, 24 + m - 1)
                pool.dma_start(back[:, m % 2, :], xT_dram[m]).then_inc(back_in[m % 2], 16)
            pool.wait_ge(out_dve, 24 + N_OUT)
            for t in range(N_PQ):
                if t >= 2:
                    pool.wait_ge(sk_tmm, t - 1)
                pool.dma_start(sk_raw[:, t % 2, :], peer_sub_keys[0, t // 2, t % 2]).then_inc(sk_in[t % 2], 16)
            pool.wait_ge(idx_done, 1)
            for q in range(T // NTOK_G):
                if q >= 2:
                    pool.wait_ge(gm_mm, q - 1)
                for n in range(NTOK_G):
                    t = q * NTOK_G + n
                    i = g.tensor_scalar(jl[q % 2][:, n, :], iota_f[:, :], ibT[:, t:t + 1], gT[:, t:t + 1],
                                        ALU.is_equal, ALU.mult)
                i.then_inc(oh_p, 1)
                if (q + 1) % (GB // NTOK_G) == 0:
                    b = q // (GB // NTOK_G)
                    pool.wait_ge(gm_ev, q + 1)
                    pool.wait_ge(gm_ev_d, q + 1)
                    pool.dma_start(gmat_dram[b], gmat[:, :, :]).then_inc(gm_out, 16)
            with pool.Fori(0, N_U // 2) as hh:
                for s in range(2):
                    pool.wait_ge(a_gelu, hh * 2 + (s + 1))
                    pool.dma_start(gelu_dram[bass.ds(hh * 2 + s, 1)].rearrange("a p t -> p (a t)"),
                                   tmp[:, s, :]).then_inc(a_out[s], 16)

            def value_tile(n, i, first):
                s = i % 2
                if not first or i >= 2:
                    pool.wait_ge(wx_lod, n - 1)
                pool.wait_ge(ag_in[s], 32 * (i // 2) + (n - i) * 16 + 32)
                g.tensor_tensor(wx[s][:, :], a_back[s][:, :], g_back[s][:, :, :].rearrange("p b t -> p (b t)"),
                                ALU.mult).then_inc(wx_val, 1)
                pool.wait_ge(v_hid, n + 1)
                g.tensor_tensor(v_lo[i][:, :], v_raw[s][:, :], v_hi[i][:, :].bitcast(F), ALU.subtract).then_inc(v_lod, 1)

            for i in range(4):
                value_tile(i, i, True)
            with pool.Fori(1, N_U // 4) as q:
                for i in range(4):
                    value_tile(q * 4 + i, i, False)
            pool.wait_ge(k_out, 32 * H)
            pool.wait_ge(v_out, 32)

        @block.scalar
        def _(act):
            a = nc.scalar
            for tb in range(TB):
                act.wait_ge(xt_mm, tb + 1)
                w = tokens(tb)
                a.copy(main[:, 0:8, tb * P:tb * P + w],
                       pair[2 * (tb % 2)][:, :, :].rearrange("p a (k t) -> p (a k) t", t=P)[:, :, 0:w]).then_inc(xt_ev_act, 1)

            def split_hi(g):
                act.wait_ge(raw_in[g % 2], raw_count(g))
                if g >= 2:
                    act.wait_ge(tile_done, g - 1)
                a.copy(w_hi[g % 2][:, :, :], w_raw[g % 2][:, :, :]).then_inc(hi_done, 1)

            split_hi(0)
            split_hi(1)
            act.wait_ge(lam_dots, 1)
            a.activation(lam_v[:, 2:4], lam_v[:, 0:2], ACT.Exp).then_inc(lam_exp, 1)

            def squares(key, k0, n, first=0):
                for i in range(n):
                    c = first + i
                    if c >= 2:
                        act.wait_ge(sq_used[key], c - 1)
                    a.activation(tmp[:, c % 2, :], main[:, k0 + i, :], ACT.Square).then_inc(sq_done[key], 1)

            def root(key, n):
                act.wait_ge(n_var[key], n)
                a.activation(rstd[:, :], rstd[:, :], ACT.Sqrt).then_inc(n_sqrt[key], 1)

            def norm_hi(key, dst, c):
                act.wait_ge(n_val[key], c + 1)
                a.copy(act_hi[:, dst, :], tmp[:, c % 2, :]).then_inc(n_hi[key], 1)

            act.wait_ge(xt_ev_act, TB)
            act.wait_ge(xt_ev_dve, TB)
            squares("n1", 0, KD)
            root("n1", 1)
            for k in range(KD):
                norm_hi("n1", k, k)
            for t in range(N_IN):
                act.wait_ge(tile_done, t + 1)
                split_hi(t + 2)
                if T_K <= t - 2 < T_P:
                    i = t - 2 - T_K
                    act.wait_ge(nat_mm, i + 1)
                    if i == 0:
                        act.wait_ge(xt_mm, TB)
                    if i < 8:
                        if i:
                            act.wait_ge(k_out, 32 * i)
                        dst, c = k_stage, 0
                    else:
                        dst, c = v_nat, (i - 8) * P
                    a.copy(dst[:, 0:4, c:c + P], pair[2][:, 0, :].rearrange("p (b c) -> p b c", c=P)).then_inc(nat_ev, 1)
                    a.copy(dst[0:NS, 4, c:c + P], pair[2][0:NS, 1, 0:P]).then_inc(nat_ev, 1)
                if t < T_K:
                    if t == 0:
                        act.wait_ge(xT_saved, 16)
                        act.wait_ge(n_lo["n1"], KD)
                    a.mul(as_halves(main[:, t, :]), halves(t % 2), HD ** -0.5).then_inc(out_act, 1)
                elif t >= T_G:
                    n = t - T_G
                    if n < 2:
                        act.wait_ge(nat_mm, 16)
                    else:
                        act.wait_ge(gate_out[n % 2], 16 * (n // 2))
                    a.activation(as_halves(tmp[:, n % 2, :]), halves(t % 2), ACT.Sigmoid,
                                 bias=bgate_c[:, n:n + 1]).then_inc(out_act, 1)
            act.wait_ge(pool_t_mm, 1)
            a.copy(stT[:, :, :], pair[0][:, :, :].rearrange("p a (k t) -> p (a k) t", t=P)[:, :, 0:DB * PSTATE]).then_inc(pool_t_ev, 1)
            act.wait_ge(pool_t_mm, 2)
            a.copy(pool_rows[0:PSTATE, 0, :], pair[1][0:PSTATE, :, :].rearrange("p a c -> p (a c)")).then_inc(pool_t_ev, 1)
            act.wait_ge(pool_t_mm, 3)
            a.copy(pool_rows[0:NS, 1, :], pair[2][0:NS, :, :].rearrange("p a c -> p (a c)")).then_inc(pool_t_ev, 1)
            act.wait_ge(pool_out, 16 * (2 + DB))
            act.wait_ge(pool_d, 4)

            def take_aT(u):
                nk = u % 4 + 1
                act.wait_ge(pa_tmm, u + 1)
                if u >= 2:
                    act.wait_ge(pa_o, u - 1)
                a.copy(paT[u % 2][:, 0:nk, :],
                       pair[2][:, u % 2, 0:nk * P].rearrange("p (k q) -> p k q", q=P)).then_inc(pa_tev, 1)

            for u in range(4 * H):
                nk = (u % 4 + 1) * P
                act.wait_ge(pa_max, u + 1)
                if u >= 2:
                    act.wait_ge(pa_a, u - 1)
                for c in range(2):
                    a.activation(pp[u % 2][:, c, 0:nk], pair[u % 2][:, c, 0:nk], ACT.Exp,
                                 bias=p_stat[:, u % 2, 2 + c:3 + c],
                                 accum_out=p_stat[:, u % 2, 4 + c:5 + c]).then_inc(pa_exp, 1)
                if u:
                    take_aT(u - 1)
            take_aT(4 * H - 1)

            for b in range(DB):
                for g in range(PAGES):
                    n, s = b * PAGES + g, b * (PAGES + 1) + g
                    act.wait_ge(sa_tmm, n + 1)
                    if n >= 2:
                        act.wait_ge(sa_s, n - 1)
                    a.copy(kT_page[n % 2][:, 0:4, :], pair[s % 2][:, 0, :].rearrange("p (h k) -> p h k", k=P)).then_inc(sa_tev_a, 1)
                act.wait_ge(sa_max, b + 1)
                if b:
                    act.wait_ge(sa_ptmm, b)
                a.activation(sp_[:, 0:1024], pair[2][:, :, :].rearrange("p a k -> p (a k)"), ACT.Exp,
                             bias=s_stat[:, 3:4], accum_out=s_stat[:, 4:5]).then_inc(sa_exp, 1)
                a.activation(sp_[:, 1024:1024 + NS], pair[3][:, 0, 0:NS], ACT.Exp,
                             bias=s_stat[:, 3:4], accum_out=s_stat[:, 5:6]).then_inc(sa_exp, 1)
                act.wait_ge(sa_ptmm, b + 1)
                if b:
                    act.wait_ge(sa_o, b)
                s = b * (PAGES + 1) + PAGES
                pt = pair[s % 2][:, :, :].rearrange("p a (g h c t) -> p (a g) h c t", h=H, c=2, t=DT)
                for bank in range(2):
                    half = pair[s % 2][:, bank, :].rearrange("p (g c t) -> p g c t", c=2, t=DT)
                    a.copy(s_aT[:, 4 * bank:4 * bank + 4, :].rearrange("p g (h t) -> p (g h) t", t=DT),
                           half[:, :, 0, :]).then_inc(sa_cp, 1)
                a.copy(s_aTn[:, :].rearrange("p (h t) -> p h t", t=DT),
                       pair[3][0:NS, 0, P:2 * P].rearrange("p (h c t) -> p h c t", c=2, t=DT)[:, :, 0, :]).then_inc(sa_cp, 1)
            act.wait_ge(sa_oev, DB)
            act.wait_ge(pa_oev, 4 * H)
            squares("sub", 0, 1)
            for h in range(H):
                if h + 1 < H:
                    act.wait_ge(sq_used["sub"], h + 1)
                    act.wait_ge(n_lo["sub"], h) if h else None
                root("sub", h + 1)
                norm_hi("sub", h, h)
                if h + 1 < H:
                    act.wait_ge(n_lo["sub"], h + 1)
                    squares("sub", h + 1, 1, first=h + 1)
            for i in range(8):
                act.wait_ge(pw_mm, i + 1)
                if i < 2:
                    split = None
                    act.wait_ge(n_lo["sub"], H)
                else:
                    act.wait_ge(pw_ev, i - 1)
                a.mul(as_halves(tmp[:, i % 2, :]), halves(i % 2), pscale_c[:, i:i + 1]).then_inc(pw_val, 1)
                act.wait_ge(pw_val, i + 1)
                a.copy(act_hi[:, 8 + i, :], tmp[:, i % 2, :]).then_inc(pw_hi, 1)
            for d in range(N_BR):
                act.wait_ge(tile_done, G_BR + d + 1)
                split_hi(G_BR + d + 2)
            for k in range(KD):
                act.wait_ge(merged_sum, k + 1)
                a.copy(act_hi[:, k, :], main[:, k, :]).then_inc(mg_hi, 1)
            for m in range(N_OUT):
                act.wait_ge(tile_done, G_OUT + m + 1)
                split_hi(G_OUT + m + 2)
            act.wait_ge(out_dve, 24 + N_OUT)
            squares("n2", 0, KD)
            root("n2", 1)
            for k in range(KD):
                norm_hi("n2", k, k)

            def take_scores(t):
                act.wait_ge(sc_mm, t + 1)
                if t >= 2:
                    act.wait_ge(top_done, t - 1)
                ps = pair[2 + t % 2]
                a.copy(s_ev[:, t % 2, 0:4, :], ps[:, 0, :].rearrange("p (b k) -> p b k", k=P)).then_inc(sc_ev, 1)
                a.copy(s_ev[0:NS, t % 2, 4, :], ps[0:NS, 1, 0:P]).then_inc(sc_ev, 1)

            for t in range(N_PQ):
                act.wait_ge(tile_done, G_PQ + t + 1)
                if G_PQ + t + 2 < G_U:
                    split_hi(G_PQ + t + 2)
                act.wait_ge(sk_tmm, t + 1)
                if t >= 2:
                    act.wait_ge(sc_mm, t - 1)
                a.copy(skT[:, t % 2, :], pair[2 + t % 2][:, 1, P:2 * P]).then_inc(sk_tev, 1)
                if t:
                    take_scores(t - 1)
            take_scores(N_PQ - 1)
            for tb in range(TB):
                w = tokens(tb)
                act.wait_ge(gx_in, tb + 1)
                a.activation(sel[0:w, 2, :], sel[0:w, 2, :], ACT.Exp).then_inc(gx_exp, 1)
                act.wait_ge(sel_tmm, tb + 1)
                for i, dst in enumerate((iaT, ibT, gT)):
                    a.copy(dst[:, tb * P:tb * P + w], pair[0][:, 0, i * P:i * P + w]).then_inc(sel_tev, 1)
            for q in range(T // NTOK_G):
                act.wait_ge(gm_mm, q + 1)
                if q % 4 == 0 and q:
                    act.wait_ge(gm_out, 16 * (q // 4))
                t0 = q % 4 * NTOK_G
                a.copy(gmat[:, :, t0:t0 + 8],
                       pair[2 * (q % 2)][:, :, :].rearrange("p a (t j) -> p j (a t)", j=PK)).then_inc(gm_ev, 1)

            def u_high(n, s, first):
                act.wait_ge(u_tmm, n + 1)
                if not first:
                    act.wait_ge(a_done, n - 1)
                for i in range(2):
                    a.copy(w_hi[s][:, 8 * i:8 * i + 8, :],
                           pair[2 + i][:, :, :].rearrange("p a (k e) -> p (a k) e", e=P)).then_inc(u_hi, 1)

            def gelu(n, s, first):
                act.wait_ge(a_done, n + 1)
                if not first:
                    act.wait_ge(a_out[s], (n - s) * 8)
                a.activation(as_halves(tmp[:, s, :]), halves(s), ACT.Gelu).then_inc(a_gelu, 1)

            u_high(0, 0, True)
            u_high(1, 1, True)
            gelu(0, 0, True)
            u_high(2, 0, False)
            gelu(1, 1, True)
            with act.Fori(1, N_U // 2 - 1) as hh:
                for s in range(2):
                    u_high(hh * 2 + (s + 1), 1 - s, False)
                    gelu(hh * 2 + s, s, False)
            u_high(N_U - 1, 1, False)
            gelu(N_U - 2, 0, False)
            gelu(N_U - 1, 1, False)

            def value_high(n, i, first):
                s = i % 2
                act.wait_ge(v_in[s], 16 * (i // 2) + (n - i) * 8 + 16)
                if not first:
                    act.wait_ge(acc_ps, (n - i) * 8 + 16 * (i // 2) - 16)
                a.copy(v_hi[i][:, :], v_raw[s][:, :]).then_inc(v_hid, 1)
                act.wait_ge(wx_val, n + 1)
                a.copy(wx_hi[i][:, :], wx[s][:, :]).then_inc(wx_hid, 1)

            for i in range(4):
                value_high(i, i, True)
            with act.Fori(1, N_U // 4) as q:
                for i in range(4):
                    value_high(q * 4 + i, i, False)
            act.wait_ge(acc_done, N_U // 2 * KD)
            squares("nf", 0, KD)
            root("nf", 1)
            for k in range(KD):
                act.wait_ge(yt_mm, k + 1)
                ps = pair[2 + k % 2]
                c = slice(k * P, (k + 1) * P)
                a.copy(y_rows[:, 0:4, c], ps[:, 0, :].rearrange("p (b c) -> p b c", c=P)).then_inc(yt_ev, 1)
                a.copy(y_rows[0:NS, 4, c], ps[0:NS, 1, 0:P]).then_inc(yt_ev, 1)

        @block.vector
        def _(dve):
            v = nc.vector
            count = [0]

            def link(*ops):
                for op in ops:
                    op.then_inc(chain, 1)
                count[0] += len(ops)
                dve.wait_ge(chain, count[0])

            dve.wait_ge(pool_const, 7)
            link(v.tensor_copy(iota_f[:, :], iota_i[:, :]),
                 v.tensor_copy(col_f[:, 0:1], col_i[:, 0:1]),
                 v.tensor_single_scalar(col_i[:, 1:2], col_i[:, 0:1], 7, ALU.bitwise_and),
                 v.tensor_single_scalar(col_i[:, 2:3], col_i[:, 0:1], 3, ALU.logical_shift_right))
            link(v.tensor_single_scalar(col_i[:, 3:4], col_i[:, 2:3], 1, ALU.bitwise_and))
            link(v.tensor_copy(col_f[:, 1:3], col_i[:, 1:4:2]))
            link(v.tensor_scalar_add(col_f[:, 3:4], col_f[:, 1:2], 56.0))
            v.tensor_scalar(mask_new[:, :], iota_f[:, 0:120], col_f[:, 3:4], NEG, ALU.is_gt, ALU.mult).then_inc(vec_const, 1)
            for g, w in enumerate(WINDOWS):
                link(v.tensor_scalar(cinv[:, g, :], iota_f[:, 0:16], 1.0, float(w), ALU.add, ALU.min))
            link(v.reciprocal(cinv[:, :, :], cinv[:, :, :]))
            dve.wait_ge(const_in, 16 * 11)
            v.tensor_scalar(page_rows[:, :], page_i[:, :], float(P), col_f[:, 0:1], ALU.mult, ALU.add).then_inc(vec_const, 1)
            v.tensor_scalar_mul(subgc8[:, :], subgc[:, :], 1.0 - LAM_INIT).then_inc(vec_const, 1)
            for i in range(2):
                op = v.tensor_tensor_reduce(out=lam_raw[:, 4, :], in0=lam_raw[:, 2 * i, :], in1=lam_raw[:, 2 * i + 1, :],
                                            scale=1.0, scalar=0.0, op0=ALU.mult, op1=ALU.add, accum_out=lam_v[:, i:i + 1])
                if i:
                    op.then_inc(lam_dots, 1)
                else:
                    link(op)
            for tb in range(TB):
                dve.wait_ge(xt_mm, tb + 1)
                w = tokens(tb)
                v.tensor_copy(main[:, 8:16, tb * P:tb * P + w],
                              pair[2 * (tb % 2) + 1][:, :, :].rearrange("p a (k t) -> p (a k) t", t=P)[:, :, 0:w]).then_inc(xt_ev_dve, 1)
            dve.wait_ge(lam_exp, 1)
            link(v.tensor_scalar_add(lam_c[:, 0:1], lam_v[:, 2:3], LAM_INIT))
            link(v.tensor_sub(lam_c[:, 0:1], lam_c[:, 0:1], lam_v[:, 3:4]))
            link(v.tensor_scalar_mul(lam_c[:, 1:2], lam_c[:, 0:1], -1.0),
                 v.tensor_scalar_add(col_f[:, 4:5], lam_c[:, 0:1], 1.0))
            link(v.tensor_mul(col_f[:, 5:6], col_f[:, 4:5], col_f[:, 2:3]))
            link(v.tensor_scalar(col_f[:, 6:7], col_f[:, 5:6], -1.0, 1.0, ALU.mult, ALU.add))

            def split_lo(g):
                dve.wait_ge(hi_done, g + 1)
                v.tensor_sub(w_lo[g % 2][:, :, :], w_raw[g % 2][:, :, :], w_hi[g % 2][:, :, :].bitcast(F)).then_inc(lo_done, 1)

            def variance(key, n, ps, width, eps):
                dve.wait_ge(sq_used[key], n)
                v.tensor_scalar(as_halves(rstd[:, :]), halves(ps), 1.0 / width, eps, ALU.mult, ALU.add).then_inc(n_var[key], 1)

            def inverse(key, n):
                dve.wait_ge(n_sqrt[key], n)
                link(v.reciprocal(rstd[:, :], rstd[:, :]))

            def norm_value(key, src, gain, c):
                if c >= 2:
                    dve.wait_ge(n_lo[key], c - 1)
                v.scalar_tensor_tensor(tmp[:, c % 2, :], main[:, src, :], gain, rstd[:, :], ALU.mult, ALU.mult).then_inc(n_val[key], 1)

            def norm_lo(key, dst, c):
                dve.wait_ge(n_hi[key], c + 1)
                v.tensor_sub(act_lo[:, dst, :], tmp[:, c % 2, :], act_hi[:, dst, :].bitcast(F)).then_inc(n_lo[key], 1)

            def norm_all(key, gains, eps):
                variance(key, KD, 0, D, eps)
                inverse(key, 1)
                for k in range(KD):
                    norm_value(key, k, gains[:, k:k + 1], k)
                    if k:
                        norm_lo(key, k - 1, k - 1)
                norm_lo(key, KD - 1, KD - 1)

            split_lo(0)
            split_lo(1)
            norm_all("n1", g1c, NORM_EPS)
            for t in range(N_IN):
                dve.wait_ge(tile_done, t + 1)
                split_lo(t + 2)
                if T_K <= t < T_V:
                    v.tensor_copy(as_halves(main[:, 8 + t - T_K, :]), halves(t % 2)).then_inc(out_dve, 1)
                elif T_V <= t < T_P:
                    i = t - T_V
                    if i >= 2:
                        dve.wait_ge(nat_mm, 8 + i - 1)
                    v.tensor_copy(as_halves(tmp[:, i % 2, :]), halves(t % 2)).then_inc(out_dve, 1)
                elif T_P <= t < T_G:
                    v.tensor_copy(as_halves(pT[:, t - T_P, :]), halves(t % 2)).then_inc(out_dve, 1)
            dve.wait_ge(tile_done, N_IN)
            dve.wait_ge(out_dve, 24)
            dve.wait_ge(pool_t_ev, 3)
            L0 = PSTATE + SEQ
            for g, w in enumerate(WINDOWS):
                e, f = ex
                def new(b):
                    return b[:, :, L0:].rearrange("p k (s x) -> p k s x", x=SEG)
                p2 = pT[:, 2 * g:2 * g + 2, :]
                ops = [v.memset(e[:, :, 0:PSTATE], 0.0), v.tensor_copy(e[:, :, PSTATE:L0], p2[:, :, 0:SEQ])]
                for k in range(2):
                    ops += [v.tensor_copy(new(e)[:, k, :, 0:PSTATE],
                                          stT[:, 2 * g + k, :].rearrange("p (s x) -> p s x", x=PSTATE)),
                            v.tensor_copy(new(e)[:, k, :, PSTATE:], p2[:, k, SEQ:].rearrange("p (s x) -> p s x", x=DT))]
                link(*ops)
                step = 1
                while step < w:
                    link(v.tensor_copy(f[:, :, 0:step], e[:, :, 0:step]),
                         v.tensor_add(f[:, :, step:], e[:, :, step:], e[:, :, 0:EXL - step]))
                    e, f = f, e
                    step *= 2
                for k in range(2):
                    link(v.tensor_mul(f[:, k, 0:16], e[:, k, PSTATE:PSTATE + 16], cinv[:, g, :]))
                    link(v.tensor_sub(f[:, k, 0:16], f[:, k, 0:16], p2[:, k, 0:16]))
                    link(v.scalar_tensor_tensor(p2[:, k, 0:SEQ], e[:, k, PSTATE:L0], 1.0 / w, p2[:, k, 0:SEQ], ALU.mult, ALU.subtract),
                         v.scalar_tensor_tensor(p2[:, k, SEQ:].rearrange("p (s x) -> p s x", x=DT), new(e)[:, k, :, PSTATE:],
                                                1.0 / w, p2[:, k, SEQ:].rearrange("p (s x) -> p s x", x=DT), ALU.mult, ALU.subtract))
                    link(v.tensor_copy(p2[:, k, 0:16], f[:, k, 0:16]))
                v.nop() if False else None
                v.tensor_copy(col_f[:, 7:8], col_f[:, 0:1]).then_inc(pool_d, 1)
            dve.wait_ge(pool_out, 16 * (2 + DB))
            dve.wait_ge(pool_d, 4)

            def row_max(u):
                nk = (u % 4 + 1) * P
                dve.wait_ge(pa_s, u + 1)
                ps, st = pair[u % 2], p_stat[:, u % 2, :]
                link(*[v.tensor_add(ps[:, c, nk - P:nk], ps[:, c, nk - P:nk], mask_diag[:, :]) for c in range(2)])
                if u >= 2:
                    dve.wait_ge(pa_a, u - 1)
                link(v.tensor_reduce(out=st[:, 0:2], in_=ps[:, :, 0:nk], axis=AX.X, op=ALU.max))
                v.tensor_scalar_mul(st[:, 2:4], st[:, 0:2], -1.0).then_inc(pa_max, 1)

            def weights(u):
                nk = (u % 4 + 1) * P
                s, st = pp[u % 2], p_stat[:, u % 2, :]
                dve.wait_ge(pa_exp, 2 * (u + 1))
                link(v.reciprocal(st[:, 6:8], st[:, 4:6]))
                if u >= 2:
                    dve.wait_ge(pa_tmm, u - 1)
                link(v.tensor_scalar_mul(pa_buf[u % 2][:, 0:nk], s[:, 0, 0:nk], st[:, 6:7]),
                     v.tensor_mul(st[:, 7:8], st[:, 7:8], lam_c[:, 1:2]))
                v.scalar_tensor_tensor(pa_buf[u % 2][:, 0:nk], s[:, 1, 0:nk], st[:, 7:8], pa_buf[u % 2][:, 0:nk],
                                       ALU.mult, ALU.add).then_inc(pa_a, 1)

            def take_o(u):
                h, qb = divmod(u, 4)
                dve.wait_ge(pa_o, u + 1)
                v.tensor_copy(main[:, h, qb * P:(qb + 1) * P], pair[3][:, u % 2, 0:P]).then_inc(pa_oev, 1)

            for u in range(4 * H + 2):
                if u < 4 * H:
                    row_max(u)
                if 1 <= u <= 4 * H:
                    weights(u - 1)
                if u >= 2:
                    take_o(u - 2)

            dve.wait_ge(pool_const, 8)
            link(v.memset(qd[:, :], 0.0))
            for b in range(DB):
                if b:
                    dve.wait_ge(sa_s, PAGES * b + b)
                for c in range(2):
                    r_ = slice(c * HD, (c + 1) * HD)
                    v.tensor_copy(qd[r_, :].rearrange("p (h x) -> p h x", x=144)[:, :, c * DT:(c + 1) * DT],
                                  main[r_, 0:H, SEQ + b * DT:SEQ + (b + 1) * DT]).then_inc(sa_qd, 1)
                for g in range(PAGES):
                    n, s = b * PAGES + g, b * (PAGES + 1) + g
                    dve.wait_ge(sa_tmm, n + 1)
                    if n >= 2:
                        dve.wait_ge(sa_s, (n - 2) + (n - 2) // PAGES + 1)
                    v.tensor_copy(kT_page[n % 2][:, 4:8, :], pair[s % 2][:, 1, :].rearrange("p (h k) -> p h k", k=P)).then_inc(sa_tev_d, 1)
                dve.wait_ge(sa_s, (PAGES + 1) * (b + 1))
                if b:
                    dve.wait_ge(sa_exp, 2 * b)
                link(v.tensor_add(pair[3][:, 0, 0:NS], pair[3][:, 0, 0:NS], mask_new[:, 56 - 8 * b:56 - 8 * b + NS]))
                link(v.tensor_reduce(out=s_stat[:, 0:1], in_=pair[2][:, :, :], axis=AX.XY, op=ALU.max),
                     v.tensor_reduce(out=s_stat[:, 1:2], in_=pair[3][:, 0, 0:NS], axis=AX.X, op=ALU.max))
                link(v.tensor_max(s_stat[:, 2:3], s_stat[:, 0:1], s_stat[:, 1:2]))
                v.tensor_scalar_mul(s_stat[:, 3:4], s_stat[:, 2:3], -1.0).then_inc(sa_max, 1)
                dve.wait_ge(sa_exp, 2 * (b + 1))
                link(v.tensor_add(s_stat[:, 6:7], s_stat[:, 4:5], s_stat[:, 5:6]))
                link(v.reciprocal(s_stat[:, 6:7], s_stat[:, 6:7]))
                link(v.tensor_mul(s_stat[:, 7:8], s_stat[:, 6:7], col_f[:, 6:7]))
                v.tensor_scalar_mul(sp_[:, :], sp_[:, :], s_stat[:, 7:8]).then_inc(sa_p, 1)
                dve.wait_ge(sa_cp, 3 * (b + 1))
                s = b * (PAGES + 1) + PAGES
                for bank in range(2):
                    half = pair[s % 2][:, bank, :].rearrange("p (g c t) -> p g c t", c=2, t=DT)
                    o = s_aT[:, 4 * bank:4 * bank + 4, :].rearrange("p g (h t) -> p (g h) t", t=DT)
                    v.tensor_add(o, half[:, :, 1, :], o).then_inc(sa_aT, 1)
                o = s_aTn[:, :].rearrange("p (h t) -> p h t", t=DT)
                v.tensor_add(o, pair[3][0:NS, 0, P:2 * P].rearrange("p (h c t) -> p h c t", c=2, t=DT)[:, :, 1, :], o).then_inc(sa_aT, 1)
                dve.wait_ge(sa_o, b + 1)
                v.tensor_copy(main[:, 0:H, SEQ + b * DT:SEQ + (b + 1) * DT],
                              pair[3][:, 1, 0:NS].rearrange("p (h t) -> p h t", t=DT)).then_inc(sa_oev, 1)
            dve.wait_ge(sa_oev, DB)
            for h in range(H):
                variance("sub", h + 1, h % 2, VD, SUBLN_EPS)
                inverse("sub", h + 1)
                norm_value("sub", h, subgc8[:, :], h)
                norm_lo("sub", h, h)
            for i in range(8):
                dve.wait_ge(pw_hi, i + 1)
                v.tensor_sub(act_lo[:, 8 + i, :], tmp[:, i % 2, :], act_hi[:, 8 + i, :].bitcast(F)).then_inc(pw_ev, 1)
            dve.wait_ge(pw_ev, 8)
            for d in range(N_BR):
                dve.wait_ge(tile_done, G_BR + d + 1)
                split_lo(G_BR + d + 2)
                dve.wait_ge(back_in[d % 2], 32 * (d // 2 + 1))
                if d:
                    dve.wait_ge(merged_sum, d)
                pa_, pb_ = (0, 1) if d % 2 == 0 else (2, 3)
                link(v.tensor_mul(as_halves(mtmp[:, 0, :]), halves(pa_), as_halves(back[:, d % 2, :])),
                     v.tensor_mul(as_halves(mtmp[:, 1, :]), halves(pb_), as_halves(back[:, 2 + d % 2, :])))
                v.tensor_add(main[:, d, :], mtmp[:, 0, :], mtmp[:, 1, :]).then_inc(merged_sum, 1)
            for k in range(KD):
                dve.wait_ge(mg_hi, k + 1)
                v.tensor_sub(act_lo[:, k, :], main[:, k, :], act_hi[:, k, :].bitcast(F)).then_inc(mg_lo, 1)
            dve.wait_ge(mg_lo, KD)
            for m in range(N_OUT):
                dve.wait_ge(tile_done, G_OUT + m + 1)
                split_lo(G_OUT + m + 2)
                dve.wait_ge(back_in[m % 2], 32 * (N_BR // 2) + 16 * (m // 2 + 1))
                v.tensor_add(as_halves(main[:, m, :]), halves(m % 2), as_halves(back[:, m % 2, :])).then_inc(out_dve, 1)
            norm_all("n2", g2c, NORM_EPS)

            def best(t):
                dve.wait_ge(sc_ev, 2 * (t + 1))
                s = t % 2
                rows = [(tb, tokens(tb)) for tb in range(TB)]
                link(*[v.max(out=sv[0:w, tb, t, 0:8], in_=s_ev[0:w, s, tb, :]) for tb, w in rows])
                link(*[v.max_index(out=si[0:w, tb, t, 0:8], in_max=sv[0:w, tb, t, 0:8], in_values=s_ev[0:w, s, tb, :]) for tb, w in rows])
                link(*[v.match_replace(out=s_ev[0:w, s, tb, :], in_to_replace=sv[0:w, tb, t, 0:8],
                                       in_values=s_ev[0:w, s, tb, :], imm_value=-3e38) for tb, w in rows])
                link(*[v.max(out=sv[0:w, tb, t, 8:16], in_=s_ev[0:w, s, tb, :]) for tb, w in rows])
                for tb, w in rows:
                    op = v.max_index(out=si[0:w, tb, t, 8:16], in_max=sv[0:w, tb, t, 8:16], in_values=s_ev[0:w, s, tb, :])
                op.then_inc(top_done, 1)

            for t in range(N_PQ):
                dve.wait_ge(tile_done, G_PQ + t + 1)
                if G_PQ + t + 2 < G_U:
                    split_lo(G_PQ + t + 2)
                if t >= 2:
                    dve.wait_ge(sc_mm, t - 1)
                v.tensor_copy(as_halves(q_ev[:, t % 2, :]), halves(t % 2)).then_inc(q_evd, 1)
                if t:
                    best(t - 1)
            best(N_PQ - 1)
            dve.wait_ge(top_done, N_PQ)

            for tb in range(TB):
                w = tokens(tb)
                svh = sv[0:w, tb, :, :].rearrange("p (h c) a -> p h c a", c=2)
                full = [w, PH, TOPK, TOPK]
                link(v.tensor_copy(si_f[0:w], si[0:w, tb, :, :]),
                     v.tensor_tensor(cand[0:w].rearrange("p h (a b) -> p h a b", b=TOPK),
                                     svh[:, :, 0, :].unsqueeze(3).broadcast_to(full),
                                     svh[:, :, 1, :].unsqueeze(2).broadcast_to(full), ALU.add))
                link(*[v.max(out=ts[0:w, h, 0:8], in_=cand[0:w, h, :]) for h in range(PH)])
                link(*[v.max_index(out=tp[0:w, h, 0:8], in_max=ts[0:w, h, 0:8], in_values=cand[0:w, h, :]) for h in range(PH)])
                link(*[v.match_replace(out=cand[0:w, h, :], in_to_replace=ts[0:w, h, 0:8], in_values=cand[0:w, h, :],
                                       imm_value=-3e38) for h in range(PH)])
                link(*[v.max(out=ts[0:w, h, 8:16], in_=cand[0:w, h, :]) for h in range(PH)])
                link(*[v.max_index(out=tp[0:w, h, 8:16], in_max=ts[0:w, h, 8:16], in_values=cand[0:w, h, :]) for h in range(PH)])
                tpw = tp[0:w].rearrange("p h k -> p (h k)")
                link(v.tensor_single_scalar(tpa[0:w, 0, :], tpw, 4, ALU.logical_shift_right),
                     v.tensor_single_scalar(tpa[0:w, 1, :], tpw, 15, ALU.bitwise_and))
                link(v.tensor_copy(tpf[0:w], tpa[0:w]))
                for c in range(2):
                    link(v.tensor_tensor(oh[0:w], tpf[0:w, c, :].unsqueeze(2).broadcast_to([w, PH * TOPK, 16]),
                                         iota_f[0:w, 0:16].unsqueeze(1).broadcast_to([w, PH * TOPK, 16]), ALU.is_equal))
                    sih = si_f[0:w].rearrange("p (h c) a -> p h c a", c=2)[:, :, c, :]
                    link(v.tensor_tensor(ohv[0:w].rearrange("p (h k) a -> p h k a", k=TOPK),
                                         oh[0:w].rearrange("p (h k) a -> p h k a", k=TOPK),
                                         sih.unsqueeze(2).broadcast_to(full), ALU.mult))
                    if c == 0 and tb:
                        dve.wait_ge(sel_tmm, tb)
                    link(v.tensor_reduce(out=sel[0:w, c, :], in_=ohv[0:w], axis=AX.X, op=ALU.add))
                sel2 = sel[0:w, 2, :].rearrange("p (h k) -> p h k", k=TOPK)
                v.tensor_tensor(sel2, ts[0:w], ts[0:w, :, 0:1].broadcast_to([w, PH, TOPK]), ALU.subtract).then_inc(gx_in, 1)
                dve.wait_ge(gx_exp, tb + 1)
                link(v.tensor_reduce(out=ssum[0:w, 0, :], in_=sel2, axis=AX.X, op=ALU.add))
                link(v.reciprocal(ssum[0:w, 1, :], ssum[0:w, 0, :]))
                v.tensor_tensor(sel2, sel2, ssum[0:w, 1, :].unsqueeze(2).broadcast_to([w, PH, TOPK]), ALU.mult).then_inc(sel_done, 1)
            dve.wait_ge(sel_tev, 3 * TB)
            link(v.tensor_copy(gTh[:, :], gT[:, :]))
            v.tensor_sub(gT[:, :], gT[:, :], gTh[:, :].bitcast(F)).then_inc(idx_done, 1)
            dve.wait_ge(idx_done, 1)

            def take_g(q):
                dve.wait_ge(gm_mm, q + 1)
                if q % 4 == 0 and q:
                    dve.wait_ge(gm_out, 16 * (q // 4))
                t0 = q % 4 * NTOK_G + 8
                v.tensor_copy(gmat[:, :, t0:t0 + 8],
                              pair[2 * (q % 2) + 1][:, :, :].rearrange("p a (t j) -> p j (a t)", j=PK)).then_inc(gm_ev_d, 1)

            for q in range(T // NTOK_G):
                if q >= 2:
                    dve.wait_ge(gm_mm, q - 1)
                for n in range(NTOK_G):
                    t = q * NTOK_G + n
                    v.tensor_scalar(oi[q % 2][:, n, :], iota_f[:, :], iaT[:, t:t + 1], None, ALU.is_equal)
                    i = v.tensor_scalar(jh[q % 2][:, n, :], iota_f[:, :], ibT[:, t:t + 1], gTh[:, t:t + 1].bitcast(F),
                                        ALU.is_equal, ALU.mult)
                i.then_inc(oh_v, 1)
                if q:
                    take_g(q - 1)
            take_g(T // NTOK_G - 1)

            def u_low(n, s):
                for i in range(2):
                    dve.wait_ge(u_hi, n * 2 + (i + 1))
                    v.tensor_sub(w_lo[s][:, 8 * i:8 * i + 8, :],
                                 pair[2 + i][:, :, :].rearrange("p a (k e) -> p (a k) e", e=P),
                                 w_hi[s][:, 8 * i:8 * i + 8, :].bitcast(F)).then_inc(u_lo, 1)

            with dve.Fori(0, N_U // 2) as hh:
                for s in range(2):
                    u_low(hh * 2 + s, s)

            def value_pair(n, i, first):
                for m in range(2):
                    dve.wait_ge(wx_hid, n + (m + 1))
                    v.tensor_sub(wx_lo[i + m][:, :], wx[(i + m) % 2][:, :], wx_hi[i + m][:, :].bitcast(F)).then_inc(wx_lod, 1)

            def take_sums(at):
                for d in range(KD):
                    dve.wait_ge(acc_ps, at + (d + 1))
                    v.tensor_add(as_halves(main[:, d, :]), halves(d % 4), as_halves(main[:, d, :])).then_inc(acc_done, 1)

            value_pair(0, 0, True)
            value_pair(2, 2, True)
            take_sums(0)
            with dve.Fori(1, N_U // 4) as q:
                value_pair(q * 4, 0, False)
                take_sums(q * 32 - 16)
                value_pair(q * 4 + 2, 2, False)
                take_sums(q * 32)
            take_sums(N_U // 2 * KD - KD)
            variance("nf", KD, 0, D, NORM_EPS)
            inverse("nf", 1)
            for k in range(KD):
                if k >= 2:
                    dve.wait_ge(yt_mm, k - 1)
                v.scalar_tensor_tensor(tmp[:, k % 2, :], main[:, k, :], gfc[:, k:k + 1], rstd[:, :], ALU.mult, ALU.mult).then_inc(n_val["nf"], 1)

        @block.tensor
        def _(pe):
            m_ = nc.tensor.matmul

            def tr(out, in_):
                n = in_.shape[0]
                return nc.tensor.transpose(out, in_, ident[0:n, 0:n])

            pe.wait_ge(pool_const, 7)
            for tb in range(TB):
                pe.wait_ge(x_loaded[tb % 2], 16 * (tb // 2 + 1))
                if tb >= 2:
                    pe.wait_ge(xt_ev_act, tb - 1)
                    pe.wait_ge(xt_ev_dve, tb - 1)
                w = tokens(tb)
                for k in range(KD):
                    ps = pair[2 * (tb % 2) + k // 8]
                    i = tr(ps[:, k // 4 % 2, (k % 4) * P:(k % 4) * P + w], x_in[0:w, tb % 2, k * P:(k + 1) * P])
                i.then_inc(xt_mm, 1)

            def sum_squares(key, c0, n, ps):
                for i in range(n):
                    pe.wait_ge(sq_done[key], c0 + i + 1)
                    for hf in range(2):
                        op = m_(pair[ps][:, hf, 0:TH], ones[:, :], tmp[:, (c0 + i) % 2, hf * TH:(hf + 1) * TH],
                                start=(i == 0), stop=(i == n - 1))
                    op.then_inc(sq_used[key], 1)

            def tile(whi, wlo, out, ks=range(KD), wait=None):
                ks = list(ks)
                for k in ks:
                    if wait:
                        wait(k)
                    for i, (w, x) in enumerate(((whi, act_hi), (whi, act_lo), (wlo, act_hi))):
                        for hf in range(2):
                            op = m_(pair[out][:, hf, 0:TH], w[:, k, :], x[:, k, hf * TH:(hf + 1) * TH],
                                    start=(k == ks[0] and i == 0), stop=(k == ks[-1] and i == 2))
                return op

            pe.wait_ge(xt_ev_act, TB)
            pe.wait_ge(xt_ev_dve, TB)
            sum_squares("n1", 0, KD, 0)

            def to_rows(i):
                if i < 8:
                    pe.wait_ge(out_dve, i + 1)
                    src = main[:, 8 + i, :]
                else:
                    pe.wait_ge(out_dve, i + 1)
                    src = tmp[:, i % 2, :]
                if i:
                    pe.wait_ge(nat_ev, 2 * i)
                for tb in range(TB):
                    w = tokens(tb)
                    op = tr(pair[2][0:w, tb // 4, (tb % 4) * P:(tb % 4 + 1) * P], src[:, tb * P:tb * P + w])
                op.then_inc(nat_mm, 1)

            for t in range(N_IN):
                pe.wait_ge(lo_done, t + 1)
                if t >= 2:
                    wait_w_in_out(pe, t - 2)
                if t == 0:
                    pe.wait_ge(n_var["n1"], 1)
                tile(w_hi[t % 2], w_lo[t % 2], t % 2,
                     wait=(lambda k: pe.wait_ge(n_lo["n1"], k + 1)) if t == 0 else None).then_inc(tile_done, 1)
                if T_K <= t - 1 < T_P:
                    to_rows(t - 1 - T_K)
            pe.wait_ge(out_act, 40)
            pe.wait_ge(nat_ev, 32)
            pe.wait_ge(pool_in, 16)
            n = DB * PSTATE
            for k in range(8):
                op = tr(pair[0][:, k // 4, (k % 4) * P:(k % 4) * P + n], st_rows[0:n, k * P:(k + 1) * P])
            op.then_inc(pool_t_mm, 1)
            for k in range(8):
                op = tr(pair[1][0:PSTATE, k // 4, (k % 4) * P:(k % 4 + 1) * P], pT[:, k, SEQ - PSTATE:SEQ])
            op.then_inc(pool_t_mm, 1)
            for k in range(8):
                op = tr(pair[2][0:NS, k // 4, (k % 4) * P:(k % 4 + 1) * P], pT[:, k, SEQ:T])
            op.then_inc(pool_t_mm, 1)
            pe.wait_ge(pool_t_ev, 3)

            def scores(u):
                h, qb = divmod(u, 4)
                nk = (qb + 1) * P
                if u >= 2:
                    pe.wait_ge(pa_exp, 2 * (u - 1))
                for c in range(2):
                    r_ = slice(c * HD, (c + 1) * HD)
                    op = m_(pair[u % 2][:, c, 0:nk], main[r_, h, qb * P:(qb + 1) * P], main[r_, 8 + h, 0:nk],
                            start=True, stop=True)
                op.then_inc(pa_s, 1)

            def turn(u):
                nk = u % 4 + 1
                pe.wait_ge(pa_a, u + 1)
                if u >= 2:
                    pe.wait_ge(pa_tev, u - 1)
                for k in range(nk):
                    op = tr(pair[2][:, u % 2, k * P:(k + 1) * P], pa_buf[u % 2][:, k * P:(k + 1) * P])
                op.then_inc(pa_tmm, 1)

            def output(u):
                h, nk = u // 4, u % 4 + 1
                pe.wait_ge(pa_tev, u + 1)
                if u >= 2:
                    pe.wait_ge(pa_oev, u - 1)
                for k in range(nk):
                    op = m_(pair[3][:, u % 2, 0:P], v_nat[:, k, h * VD:(h + 1) * VD], paT[u % 2][:, k, :],
                            start=(k == 0), stop=(k == nk - 1))
                op.then_inc(pa_o, 1)

            scores(0)
            for u in range(4 * H):
                if u + 1 < 4 * H:
                    scores(u + 1)
                turn(u)
                if u:
                    output(u - 1)
            output(4 * H - 1)

            pe.wait_ge(pa_oev, 4 * H)

            def page_T(n):
                b, g = divmod(n, PAGES)
                s = b * (PAGES + 1) + g
                pe.wait_ge(kp_in[n % K_RING], 16 * (n // K_RING + 1))
                if n >= 2:
                    pe.wait_ge(sa_tev_a, n - 1)
                    pe.wait_ge(sa_tev_d, n - 1)
                if b and g < 2:
                    pe.wait_ge(sa_aT, 3 * b)
                for h in range(H):
                    op = tr(pair[s % 2][:, h // 4, (h % 4) * P:(h % 4 + 1) * P], k_page[n % K_RING][:, h * P:(h + 1) * P])
                op.then_inc(sa_tmm, 1)

            page_T(0)
            for b in range(DB):
                pe.wait_ge(sa_qd, 2 * (b + 1))
                if b:
                    pe.wait_ge(sa_exp, 2 * b)
                for g in range(PAGES):
                    n = b * PAGES + g
                    if g + 1 < PAGES:
                        page_T(n + 1)
                    pe.wait_ge(sa_tev_a, n + 1)
                    pe.wait_ge(sa_tev_d, n + 1)
                    for h in range(H):
                        op = m_(pair[2][:, g // 4, (g % 4) * P:(g % 4 + 1) * P], qd[:, h * P:(h + 1) * P],
                                kT_page[n % 2][:, h, :], start=(h == 0), stop=(h == H - 1))
                    op.then_inc(sa_s, 1)
                if b:
                    pe.wait_ge(sa_aT, 3 * b)
                for h in range(H):
                    op = m_(pair[3][:, 0, 0:NS], qd[:, h * P:(h + 1) * P], main[:, 8 + h, SEQ:T],
                            start=(h == 0), stop=(h == H - 1))
                op.then_inc(sa_s, 1)
                s = b * (PAGES + 1) + PAGES
                pe.wait_ge(sa_p, b + 1)
                for g in range(PAGES):
                    tr(pair[s % 2][:, g // 4, (g % 4) * P:(g % 4 + 1) * P], sp_[:, g * P:(g + 1) * P])
                tr(pair[3][0:NS, 0, P:2 * P], sp_[:, 1024:1024 + NS]).then_inc(sa_ptmm, 1)
                if (b + 1) < DB:
                    page_T((b + 1) * PAGES)
                pe.wait_ge(sa_aT, 3 * (b + 1))
                if b:
                    pe.wait_ge(sa_oev, b)
                for g in range(PAGES):
                    pe.wait_ge(vp_in[g], 16 * (b + 1))
                for h in range(H):
                    for g in range(PAGES):
                        m_(pair[3][:, 1, h * DT:(h + 1) * DT], v_page[g][:, h * VD:(h + 1) * VD],
                           s_aT[:, g, h * DT:(h + 1) * DT], start=(g == 0), stop=False)
                    op = m_(pair[3][:, 1, h * DT:(h + 1) * DT], v_nat[0:NS, 4, h * VD:(h + 1) * VD],
                            s_aTn[:, h * DT:(h + 1) * DT], start=False, stop=True)
                op.then_inc(sa_o, 1)
            for h in range(H):
                if h >= 2:
                    pe.wait_ge(n_var["sub"], h - 1)
                sum_squares("sub", h, 1, h % 2)
            pe.wait_ge(n_var["sub"], H)
            for g in range(4):
                pe.wait_ge(pw_in, 16 * (g + 1))
                for o in range(2):
                    i = 2 * g + o
                    if i >= 2:
                        pe.wait_ge(pw_val, i - 1)
                    for k in range(2):
                        for hf in range(2):
                            op = m_(pair[i % 2][:, hf, 0:TH], pw[:, k, o * P:(o + 1) * P],
                                    pT[:, 2 * g + k, hf * TH:(hf + 1) * TH], start=(k == 0), stop=(k == 1))
                    op.then_inc(pw_mm, 1)
            pe.wait_ge(pw_ev, 8)
            for d in range(N_BR):
                g = G_BR + d
                pe.wait_ge(lo_done, g + 1)
                if d >= 2:
                    pe.wait_ge(merged_sum, d - 1)
                o = 0 if d % 2 == 0 else 2
                tile(w_hi[g % 2], w_lo[g % 2], o, range(8))
                tile(w_hi[g % 2], w_lo[g % 2], o + 1, range(8, 16)).then_inc(tile_done, 1)
            for t in range(N_OUT):
                g = G_OUT + t
                pe.wait_ge(lo_done, g + 1)
                if t >= 2:
                    pe.wait_ge(out_dve, 24 + t - 1)
                tile(w_hi[g % 2], w_lo[g % 2], t % 2,
                     wait=(lambda k: pe.wait_ge(mg_lo, k + 1)) if t == 0 else None).then_inc(tile_done, 1)
            pe.wait_ge(out_dve, 24 + N_OUT)
            sum_squares("n2", 0, KD, 0)
            pe.wait_ge(n_var["n2"], 1)

            def key_scores(t):
                pe.wait_ge(q_evd, t + 1)
                pe.wait_ge(sk_tev, t + 1)
                if t >= 2:
                    pe.wait_ge(sc_ev, 2 * (t - 1))
                for tb in range(TB):
                    w = tokens(tb)
                    op = m_(pair[2 + t % 2][0:w, tb // 4, (tb % 4) * P:(tb % 4 + 1) * P],
                            q_ev[:, t % 2, tb * P:tb * P + w], skT[:, t % 2, :], start=True, stop=True)
                op.then_inc(sc_mm, 1)

            for t in range(N_PQ):
                g = G_PQ + t
                pe.wait_ge(lo_done, g + 1)
                if t >= 2:
                    pe.wait_ge(q_evd, t - 1)
                tile(w_hi[g % 2], w_lo[g % 2], t % 2,
                     wait=(lambda k: pe.wait_ge(n_lo["n2"], k + 1)) if t == 0 else None).then_inc(tile_done, 1)
                pe.wait_ge(sk_in[t % 2], 16 * (t // 2 + 1))
                if t >= 2:
                    pe.wait_ge(sc_ev, 2 * (t - 1))
                tr(pair[2 + t % 2][:, 1, P:2 * P], sk_raw[:, t % 2, :]).then_inc(sk_tmm, 1)
                if t:
                    key_scores(t - 1)
            key_scores(N_PQ - 1)
            pe.wait_ge(q_evd, N_PQ)
            for tb in range(TB):
                w = tokens(tb)
                pe.wait_ge(sel_done, tb + 1)
                if tb:
                    pe.wait_ge(sel_tev, 3 * tb)
                for i in range(3):
                    op = tr(pair[0][:, 0, i * P:i * P + w], sel[0:w, i, :])
                op.then_inc(sel_tmm, 1)
            pe.wait_ge(sel_tev, 3 * TB)
            for q in range(T // NTOK_G):
                pe.wait_ge(oh_v, q + 1)
                pe.wait_ge(oh_p, q + 1)
                if q >= 2:
                    pe.wait_ge(gm_ev, q - 1)
                    pe.wait_ge(gm_ev_d, q - 1)
                for n in range(NTOK_G):
                    out = pair[2 * (q % 2) + n // 8][:, n // 4 % 2, (n % 4) * PK:(n % 4 + 1) * PK]
                    m_(out, oi[q % 2][:, n, :], jh[q % 2][:, n, :], start=True, stop=False)
                    op = m_(out, oi[q % 2][:, n, :], jl[q % 2][:, n, :], start=False, stop=True)
                op.then_inc(gm_mm, 1)
            pe.wait_ge(gm_ev, T // NTOK_G)
            pe.wait_ge(gm_ev_d, T // NTOK_G)

            def turn_u(n, s, first):
                pe.wait_ge(u_in[s], (n - s) * 8 + 16)
                if not first:
                    pe.wait_ge(u_lo, n * 2)
                raw = w_raw[s][:, :, :].rearrange("p k c -> p (k c)")
                for k in range(KD):
                    op = tr(pair[2 + k // 8][:, k // 4 % 2, (k % 4) * P:(k % 4 + 1) * P], raw[:, k * P:(k + 1) * P])
                op.then_inc(u_tmm, 1)

            def expert_tile(n, s, first):
                pe.wait_ge(u_lo, n * 2 + 2)
                if not first:
                    pe.wait_ge(a_gelu, n - 1)
                tile(w_hi[s], w_lo[s], s).then_inc(a_done, 1)

            turn_u(0, 0, True)
            turn_u(1, 1, False)
            expert_tile(0, 0, True)
            turn_u(2, 0, False)
            expert_tile(1, 1, True)
            with pe.Fori(1, N_U // 2 - 1) as hh:
                for s in range(2):
                    turn_u(hh * 2 + (s + 1), 1 - s, False)
                    expert_tile(hh * 2 + s, s, False)
            turn_u(N_U - 1, 1, False)
            expert_tile(N_U - 2, 0, False)
            expert_tile(N_U - 1, 1, False)
            pe.wait_ge(a_gelu, N_U)

            def value_sums(n, i, at, first):
                pe.wait_ge(v_lod, n + 2)
                pe.wait_ge(wx_lod, n + 2)
                for d in range(KD):
                    if not first or d >= 4:
                        pe.wait_ge(acc_done, at + (d - 3))
                    c = slice(d * P, (d + 1) * P)
                    terms = [(w[m], x[m]) for m in (i, i + 1) for w, x in ((v_hi, wx_hi), (v_hi, wx_lo), (v_lo, wx_hi))]
                    for j, (w, x) in enumerate(terms):
                        for hf in range(2):
                            op = m_(pair[d % 4][:, hf, 0:TH], w[:, c], x[:, hf * TH:(hf + 1) * TH],
                                    start=(j == 0), stop=(j == 5))
                    op.then_inc(acc_ps, 1)

            value_sums(0, 0, 0, True)
            value_sums(2, 2, KD, False)
            with pe.Fori(1, N_U // 4) as q:
                value_sums(q * 4, 0, q * 32, False)
                value_sums(q * 4 + 2, 2, q * 32 + 16, False)
            pe.wait_ge(acc_done, N_U // 2 * KD)
            sum_squares("nf", 0, KD, 0)
            for k in range(KD):
                pe.wait_ge(n_val["nf"], k + 1)
                if k >= 2:
                    pe.wait_ge(yt_ev, 2 * (k - 1))
                for tb in range(TB):
                    w = tokens(tb)
                    op = tr(pair[2 + k % 2][0:w, tb // 4, (tb % 4) * P:(tb % 4 + 1) * P], tmp[:, k % 2, tb * P:tb * P + w])
                op.then_inc(yt_mm, 1)


_INS = ["x_prompt", "x_sample", "cache_k", "cache_v", "state_pool", "page_table", "norm1_g", "w_in", "b_gate",
        "lambda_q1", "lambda_k1", "lambda_q2", "lambda_k2", "subln_g", "w_attn_branch", "pool_w", "pool_scale",
        "w_pool_branch", "w_out", "norm2_g", "w_peer_q", "peer_sub_keys", "peer_u", "peer_v", "norm_f_g"]
_OUTS = [(1, SEQ, D), (DB, DT, D), (1, 1, SEQ, H, 2, HD), (1, 1, SEQ, H, VD), (1, 1, PSTATE, POOLW),
         (1, DB, DT, H, 2, HD), (1, DB, DT, H, VD), (1, DB, PSTATE, POOLW)]


def kernel(**inputs):
    import numpy as _np
    import concourse.bacc as _bacc
    from concourse import mybir as _mybir
    from concourse.bass_utils import run_bass_kernel_spmd as _run

    nc = _bacc.Bacc("TRN2", target_bir_lowering=False, num_devices=1)
    arrays, args = {}, []
    for name in _INS:
        a = _np.ascontiguousarray(inputs[name])
        arrays[f"in_{name}_dram"] = a
        args.append(nc.dram_tensor(f"in_{name}_dram", a.shape, _mybir.dt.from_np(a.dtype), kind="ExternalInput").ap())
    for i, shape in enumerate(_OUTS):
        args.append(nc.dram_tensor(f"out_{i}_dram", shape, _mybir.dt.float32, kind="ExternalOutput").ap())
    hybrid_step(nc, *args)
    r = _run(nc, [arrays], core_ids=[0])
    return tuple(r.results[0][f"out_{i}_dram"] for i in range(len(_OUTS)))
```

```python
import math

import numpy as np
import concourse.bass as bass
from concourse import mybir
from contextlib import ExitStack

F = mybir.dt.float32
R = mybir.dt.float32r
I32 = mybir.dt.int32
U32 = mybir.dt.uint32
ALU = mybir.AluOpType
ACT = mybir.ActivationFunctionType
AX = mybir.AxisListType

P = 128
D = 2048
KD = D // P
SEQ, DB, DT = 512, 8, 8
NS = DB * DT
T = SEQ + NS
TH = T // 2
TB = 5
H, HD, VD = 8, 64, 128
PAGES = 8
POOLW, PSTATE = 1024, 15
WINDOWS = (2, 4, 8, 16)
PH, PK, TOPK = 8, 128, 16
NEG = -1e30
SUBLN_EPS, NORM_EPS = 1e-5, 1e-6
LAM_INIT = 0.8 - 0.6 * math.exp(0.0)

T_Q, T_K, T_V, T_P, T_G = 0, 8, 16, 24, 32
N_IN = 64
N_BR, N_OUT, N_PQ = 16, 16, 16
G_BR = N_IN
G_OUT = G_BR + N_BR
G_PQ = G_OUT + N_OUT
G_U = G_PQ + N_PQ
N_W = G_U
N_U = PK
NTOK_G = 8
SEL_TILES = 6
G_FIRST = SEL_TILES * TB
N_G = T // NTOK_G
GB = 64


def tokens(tb):
    return P if tb < TB - 1 else NS


def hybrid_step(nc, x_prompt, x_sample, cache_k, cache_v, state_pool, page_table, norm1_g, w_in, b_gate,
                lambda_q1, lambda_k1, lambda_q2, lambda_k2, subln_g, w_attn_branch, pool_w, pool_scale,
                w_pool_branch, w_out, norm2_g, w_peer_q, peer_sub_keys, peer_u, peer_v, norm_f_g,
                y_prompt, y_sample, k_prompt, v_prompt, pool_prompt, k_sample, v_sample, pool_sample):
    ctx = ExitStack()
    with ctx:
        ctx.enter_context(nc.allow_non_contiguous_dma("columns of gains and biases"))
        BASE = (nc.sbuf_base + 63) // 64 * 64
        U = KD * T * 4
        A_ACT, A_MAIN = 0, 2 * U
        A_RING = 3 * U
        A_CONST = A_RING + 6 * KD * P * 4
        A_X = A_CONST + 4352

        class Region:
            def __init__(self, at, end):
                self.at, self.end = BASE + at, BASE + end

            def __call__(self, name, shape, dt=F):
                size = int(np.prod(shape[1:])) * 4
                t = nc.alloc_sbuf_tensor_at(name, shape, dt, offset=self.at)
                self.at += (size + 31) // 32 * 32
                assert self.at <= self.end, (name, self.at - self.end)
                return t

        END = nc.sbuf_usable_end // 32 * 32 - BASE
        r = Region(A_ACT, A_MAIN)
        act_hi = r("act_hi", [P, KD, T], R)
        act_lo = r("act_lo", [P, KD, T], R)
        main = Region(A_MAIN, A_RING)("main", [P, KD, T])
        r = Region(A_RING, A_CONST)
        w_raw = [r(f"w_raw{s}", [P, KD, P]) for s in range(2)]
        w_hi = [r(f"w_hi{s}", [P, KD, P], R) for s in range(2)]
        w_lo = [r(f"w_lo{s}", [P, KD, P], R) for s in range(2)]
        r = Region(A_CONST, A_X)
        ident = r("ident", [P, P])
        ones = r("ones", [P, P])
        mask_diag = r("mask_diag", [P, P])
        mask_new = r("mask_new", [P, 120])
        iota_f = r("iota_f", [P, P])
        iota_i = r("iota_i", [P, P], I32)
        g1c, g2c, gfc = r("g1c", [P, KD]), r("g2c", [P, KD]), r("gfc", [P, KD])
        subgc = r("subgc", [P, 1])
        subgc8 = r("subgc8", [P, 1])
        pscale_c = r("pscale_c", [P, 8])
        bgate_c = r("bgate_c", [P, 32])
        cinv = r("cinv", [P, 4, 16])
        page_i = r("page_i", [P, DB * PAGES], I32)
        page_rows = r("page_rows", [P, DB * PAGES], U32)
        col_i = r("col_i", [P, 4], I32)
        col_f = r("col_f", [P, 8])
        lam_v = r("lam_v", [P, 4])
        lam_c = r("lam_c", [P, 2])
        r = Region(A_X, END)
        tmp = r("tmp", [P, 2, T])
        rstd = r("rstd", [P, T])
        v_nat = r("v_nat", [P, TB, H * VD])
        pT = r("pT", [P, 8, T])
        k_stage = r("k_stage", [P, TB, P])
        r = Region(A_X, END)
        r("tmp_", [P, 3, T])
        x_in = r("x_in", [P, 2, D])
        lam_raw = Region(A_ACT, A_MAIN)("lam_raw", [P, 5, HD])
        r = Region(A_ACT, A_MAIN)
        qd = r("qd", [P, 8 * 144])
        K_RING = 3
        k_page = [r(f"k_page{s}", [P, H * P]) for s in range(K_RING)]
        kT_page = [r(f"kT_page{s}", [P, H, P]) for s in range(2)]
        sp_ = r("sp_", [P, 1024 + NS])
        s_aT = r("s_aT", [P, PAGES, NS])
        s_aTn = r("s_aTn", [NS, NS])
        s_stat = r("s_stat", [P, 8])
        shared_at = r.at - BASE
        v_page = [r(f"v_page{s}", [P, H * VD]) for s in range(PAGES)]
        r = Region(shared_at, A_MAIN)
        pp = [r(f"pp{s}", [P, 2, SEQ]) for s in range(2)]
        pa_buf = [r(f"pa{s}", [P, SEQ]) for s in range(2)]
        paT = [r(f"paT{s}", [P, 4, P]) for s in range(2)]
        p_stat = r("p_stat", [P, 2, 8])
        r = Region(shared_at, A_MAIN)
        SEG = PSTATE + DT
        EXL = PSTATE + SEQ + DB * SEG
        ex = [r(f"ex{s}", [P, 2, EXL]) for s in range(2)]
        st_rows = r("st_rows", [P, POOLW])
        stT = r("stT", [P, 8, DB * PSTATE])
        pool_rows = r("pool_rows", [NS, 2, POOLW])
        pw = Region(A_MAIN + U // 2, A_RING)("pw", [P, 2, 256])
        r = Region(A_X, END)
        r("tmp__", [P, 3, T])
        back = r("back", [P, 4, T])
        mtmp = r("mtmp", [P, 2, T])
        r = Region(A_X, END)
        r("tmp___", [P, 2, T])
        iaT = r("iaT", [P, T])
        ibT = r("ibT", [P, T])
        gT = r("gT", [P, T])
        gTh = r("gTh", [P, T], R)
        x2 = r.at - BASE
        sv = r("sv", [P, TB, 16, 16])
        si = r("si", [P, TB, 16, 16], U32)
        q_ev = r("q_ev", [P, 2, T])
        sk_raw = r("sk_raw", [P, 2, P])
        skT = r("skT", [P, 2, P])
        s_ev = r("s_ev", [P, 2, TB, PK])
        r = Region(x2, END)
        r("keep_sv", [P, 2, TB, 16, 16])
        si_f = r("si_f", [P, 16, 16])
        cand = r("cand", [P, PH, 256])
        ts = r("ts", [P, PH, TOPK])
        tp = r("tp", [P, PH, TOPK], U32)
        tpa = r("tpa", [P, 2, PH * TOPK], U32)
        tpf = r("tpf", [P, 2, PH * TOPK])
        oh = r("oh", [P, PH * TOPK, 16])
        sel = r("sel", [P, 3, PH * TOPK])
        ssum = r("ssum", [P, 2, PH])
        r = Region(x2, END)
        oi = [r(f"oi{s}", [P, NTOK_G, PK], R) for s in range(2)]
        jh = [r(f"jh{s}", [P, NTOK_G, PK], R) for s in range(2)]
        jl = [r(f"jl{s}", [P, NTOK_G, PK], R) for s in range(2)]
        gmat = Region(A_MAIN, A_RING)("gmat", [P, PK, GB])
        r = Region(A_ACT, A_MAIN)
        v_hi = [r(f"v_hi{s}", [P, D], R) for s in range(4)]
        v_lo = [r(f"v_lo{s}", [P, D], R) for s in range(4)]
        r = Region(A_RING, A_CONST)
        v_raw = [r(f"v_raw{s}", [P, D]) for s in range(2)]
        wx_hi = [r(f"wx_hi{s}", [P, T], R) for s in range(4)]
        wx_lo = [r(f"wx_lo{s}", [P, T], R) for s in range(4)]
        r = Region(A_X, END)
        a_back = [r(f"a_back{s}", [P, T]) for s in range(2)]
        g_back = [r(f"g_back{s}", [P, T // GB, GB]) for s in range(2)]
        wx = [r(f"wx{s}", [P, T]) for s in range(2)]
        y_rows = Region(A_ACT, A_MAIN)("y_rows", [P, TB, D])

        pair = [ctx.enter_context(nc.psum_tensor(f"pair{i}", [P, 2, 512], F)) for i in range(4)]

        def halves(n):
            return pair[n][:, :, 0:TH]

        def as_halves(t):
            return t.rearrange("p (a t) -> p a t", a=2)

        xT_dram = nc.dram_tensor("xT_dram", [KD, P, T], F).ap()
        hT_dram = nc.dram_tensor("hT_dram", [KD, P, T], F).ap()
        gate_dram = nc.dram_tensor("gate_dram", [32, P, T], F).ap()
        gmat_dram = nc.dram_tensor("gmat_dram", [T // GB, P, PK, GB], F).ap()
        gelu_dram = nc.dram_tensor("gelu_dram", [N_U, P, T], F).ap()
        ck = cache_k.rearrange("l n s h c d -> (l n s) (h c d)")
        cv = cache_v.rearrange("l n s h e -> (l n s) (h e)")
        u_tiles = peer_u.rearrange("l (i j) d -> (l i) j d", j=PK)
        v_tiles = peer_v.rearrange("l (i j) d -> (l i) j d", j=PK)

        def sem(name):
            return ctx.enter_context(nc.semaphore(name))

        const_in = sem("const_in")
        pool_const = sem("pool_const")
        vec_const = sem("vec_const")
        lam_exp, lam_dots = sem("lam_exp"), sem("lam_dots")
        chain = sem("chain")
        x_loaded = [sem(f"x_loaded{s}") for s in range(2)]
        xt_mm, xt_ev_act, xt_ev_dve = sem("xt_mm"), sem("xt_ev_act"), sem("xt_ev_dve")
        xT_saved = sem("xT_saved")
        raw_in = [sem(f"raw_in{s}") for s in range(2)]
        hi_done, lo_done, tile_done = sem("hi_done"), sem("lo_done"), sem("tile_done")
        out_act, out_dve = sem("out_act"), sem("out_dve")
        nat_mm, nat_ev = sem("nat_mm"), sem("nat_ev")
        k_out, v_out = sem("k_out"), sem("v_out")
        gate_out = [sem(f"gate_out{s}") for s in range(2)]
        pool_in, pool_t_mm, pool_t_ev = sem("pool_in"), sem("pool_t_mm"), sem("pool_t_ev")
        pool_d = sem("pool_d")
        pool_out = sem("pool_out")
        pw_in, pw_mm, pw_val, pw_hi, pw_ev = (sem(n) for n in ("pw_in", "pw_mm", "pw_val", "pw_hi", "pw_ev"))
        pa_s, pa_max, pa_exp, pa_a, pa_tmm, pa_tev, pa_o, pa_oev = (
            sem(n) for n in ("pa_s", "pa_max", "pa_exp", "pa_a", "pa_tmm", "pa_tev", "pa_o", "pa_oev"))
        kp_in = [sem(f"kp_in{s}") for s in range(K_RING)]
        vp_in = [sem(f"vp_in{s}") for s in range(PAGES)]
        sa_qd, sa_tmm, sa_tev_a, sa_tev_d, sa_s, sa_max, sa_exp, sa_p, sa_ptmm, sa_cp, sa_aT, sa_o, sa_oev = (
            sem(n) for n in ("sa_qd", "sa_tmm", "sa_tev_a", "sa_tev_d", "sa_s", "sa_max", "sa_exp", "sa_p",
                             "sa_ptmm", "sa_cp", "sa_aT", "sa_o", "sa_oev"))
        NORMS = ("n1", "sub", "n2", "nf")
        sq_done, sq_used, n_var, n_sqrt, n_val, n_hi, n_lo = (
            {k: sem(f"{n}_{k}") for k in NORMS} for n in ("sq_done", "sq_used", "n_var", "n_sqrt", "n_val", "n_hi", "n_lo"))
        back_in = [sem(f"back_in{s}") for s in range(2)]
        merged_sum, mg_hi, mg_lo = sem("merged_sum"), sem("mg_hi"), sem("mg_lo")
        rows_in = sem("rows_in")
        sk_in = [sem(f"sk_in{s}") for s in range(2)]
        sk_tmm, sk_tev, q_evd, sc_mm, sc_ev, top_done = (
            sem(n) for n in ("sk_tmm", "sk_tev", "q_evd", "sc_mm", "sc_ev", "top_done"))
        gx_in, gx_exp, sel_done, sel_tmm, sel_tev, idx_done = (
            sem(n) for n in ("gx_in", "gx_exp", "sel_done", "sel_tmm", "sel_tev", "idx_done"))
        hT_saved, hT_back = sem("hT_saved"), sem("hT_back")
        oh_v, gm_mm, gm_ev, gm_out = (sem(n) for n in ("oh_v", "gm_mm", "gm_ev", "gm_out"))
        u_in = [sem(f"u_in{s}") for s in range(2)]
        u_tmm, u_hi, u_lo, a_done, a_gelu = (sem(n) for n in ("u_tmm", "u_hi", "u_lo", "a_done", "a_gelu"))
        a_out = [sem(f"a_out{s}") for s in range(2)]
        v_in = [sem(f"v_in{s}") for s in range(2)]
        ag_in = [sem(f"ag_in{s}") for s in range(2)]
        v_hid, v_lod, wx_val, wx_hid, wx_lod, vt_done, acc_ps, acc_done = (
            sem(n) for n in ("v_hid", "v_lod", "wx_val", "wx_hid", "wx_lod", "vt_done", "acc_ps", "acc_done"))
        yt_mm, yt_ev, y_out = sem("yt_mm"), sem("yt_ev"), sem("y_out")

        block = ctx.enter_context(nc.Block())

        def col_view(a, n):
            return a.rearrange("l (k p) -> p (l k)", p=P) if len(a.shape) == 2 else a.rearrange("(k p) -> p k", p=P)

        def ring_source(g):
            if g < G_BR:
                return [(w_in[0, :, g * P:(g + 1) * P].rearrange("(k p) c -> p k c", p=P), 0, KD)]
            if g < G_OUT:
                c = slice((g - G_BR) * P, (g - G_BR + 1) * P)
                return [(w_attn_branch[0, :, c].rearrange("(k p) c -> p k c", p=P), 0, 8),
                        (w_pool_branch[0, :, c].rearrange("(k p) c -> p k c", p=P), 8, 8)]
            w, g = (w_out, g - G_OUT) if g < G_PQ else (w_peer_q, g - G_PQ)
            return [(w[0, :, g * P:(g + 1) * P].rearrange("(k p) c -> p k c", p=P), 0, KD)]

        def raw_count(g):
            n = sum(2 if G_BR <= m < G_OUT else 1 for m in range(g % 2, g + 1, 2))
            return 16 * n

        OUT_ACT = [t for t in range(N_IN) if t < T_K or t >= T_G]
        OUT_DVE = [t for t in range(N_IN) if T_K <= t < T_G]

        def wait_w_in_out(eng, t):
            if t in OUT_ACT:
                eng.wait_ge(out_act, OUT_ACT.index(t) + 1)
            else:
                eng.wait_ge(out_dve, OUT_DVE.index(t) + 1)



        def split_waits_norm(eng, key, done):
            eng.wait_ge(n_hi[key], done)
            eng.wait_ge(n_lo[key], done)

        @block.sync
        def _(sp):
            for s in range(2):
                sp.dma_start(x_in[:, s, :], x_prompt[0, s * P:(s + 1) * P, :]).then_inc(x_loaded[s], 16)

            def load_tile(g):
                if g >= 2:
                    sp.wait_ge(lo_done, g - 1)
                for src, k0, n in ring_source(g):
                    sp.dma_start(w_raw[g % 2][:, k0:k0 + n, :], src).then_inc(raw_in[g % 2], 16)

            for i, v in enumerate((lambda_q1, lambda_k1, lambda_q2, lambda_k2)):
                sp.dma_start(lam_raw[:, i, :], v.broadcast_to([P, HD])).then_inc(const_in, 16)
            for dst, src in ((g1c, norm1_g), (g2c, norm2_g), (gfc, norm_f_g), (subgc, subln_g),
                             (pscale_c, pool_scale), (bgate_c, b_gate)):
                sp.dma_start(dst[:, :], col_view(src, P)).then_inc(const_in, 16)
            sp.dma_start(page_i[:, :], page_table.rearrange("b g -> (b g)").unsqueeze(0)
                         .broadcast_to([P, DB * PAGES])).then_inc(const_in, 16)
            load_tile(0)
            load_tile(1)
            for tb in range(2, TB):
                sp.wait_ge(xt_mm, tb - 1)
                src = x_prompt[0, tb * P:(tb + 1) * P, :] if tb < 4 else x_sample.rearrange("b t d -> (b t) d")
                sp.dma_start(x_in[0:tokens(tb), tb % 2, :], src).then_inc(x_loaded[tb % 2], 16)
            for g in range(2, G_U):
                load_tile(g)
            def load_u(n, s):
                src = u_tiles[:, n, :] if isinstance(n, int) else u_tiles[:, bass.ds(n, 1), :].rearrange("p a d -> p (a d)")
                sp.dma_start(w_raw[s][:, :, :].rearrange("p k c -> p (k c)"), src).then_inc(u_in[s], 16)

            def store_gelu(n, s):
                sp.wait_ge(a_gelu, n + 1)
                dst = gelu_dram[n] if isinstance(n, int) else gelu_dram[bass.ds(n, 1)].rearrange("a p t -> p (a t)")
                sp.dma_start(dst, tmp[:, s, :]).then_inc(a_out[s], 16)

            sp.wait_ge(lo_done, N_W)
            load_u(0, 0)
            load_u(1, 1)
            for n in range(2, 4):
                sp.wait_ge(u_tmm, 2 * (n - 1))
                load_u(n, n % 2)
                if n == 3:
                    store_gelu(0, 0)
            with sp.Fori(2, N_U // 2) as hh:
                for s in range(2):
                    sp.wait_ge(u_tmm, hh * 4 + 2 * (s - 1))
                    load_u(hh * 2 + s, s)
                    store_gelu(hh * 2 + (s - 3), 1 - s)
            for n in range(N_U - 3, N_U):
                store_gelu(n, n % 2)

            def load_v(n, i):
                s = i % 2
                def one(ap, m):
                    return ap[:, m, :] if isinstance(m, int) else ap[:, bass.ds(m, 1), :].rearrange("p a d -> p (a d)")
                sp.dma_start(v_raw[s][:, :], one(v_tiles, n)).then_inc(v_in[s], 16)
                sp.dma_start(a_back[s][:, :], one(gelu_dram.rearrange("j i t -> i j t"), n)).then_inc(ag_in[s], 16)
                g = gmat_dram.rearrange("b i j t -> i b j t")
                g = g[:, :, n, :] if isinstance(n, int) else g[:, :, bass.ds(n, 1), :].rearrange("i b j t -> i b (j t)")
                sp.dma_start(g_back[s][:, :, :], g).then_inc(ag_in[s], 16)

            sp.wait_ge(a_done, N_U)
            for s in range(2):
                sp.wait_ge(a_out[s], 16 * N_U // 2)
            sp.wait_ge(gm_out, 16 * (T // GB))
            for i in range(4):
                if i == 2:
                    sp.wait_ge(hT_saved, 16)
                    sp.dma_start(main[:, :, :], hT_dram.rearrange("k p t -> p k t")).then_inc(hT_back, 16)
                if i >= 2:
                    sp.wait_ge(v_lod, i - 1)
                    sp.wait_ge(wx_val, i - 1)
                load_v(i, i)
            with sp.Fori(1, N_U // 4) as q:
                for i in range(4):
                    sp.wait_ge(v_lod, q * 4 + (i - 1))
                    sp.wait_ge(wx_val, q * 4 + (i - 1))
                    load_v(q * 4 + i, i)
            sp.wait_ge(yt_ev, 2 * KD)
            sp.dma_start(y_prompt[0].rearrange("(b p) d -> p b d", p=P), y_rows[:, 0:4, :]).then_inc(y_out, 16)
            sp.dma_start(y_sample.rearrange("b t d -> (b t) d"), y_rows[0:NS, 4, :]).then_inc(y_out, 16)
            sp.wait_ge(y_out, 32)

        @block.gpsimd
        def _(pool):
            g = nc.gpsimd
            g.memset(ident[:, :], 0.0).then_inc(pool_const, 1)
            g.memset(ones[:, :], 1.0).then_inc(pool_const, 1)
            g.memset(mask_diag[:, :], 0.0).then_inc(pool_const, 1)
            g.iota(iota_i[:, :], pattern=[[1, P]], base=0, channel_multiplier=0).then_inc(pool_const, 1)
            g.iota(col_i[:, 0:1], pattern=[[1, 1]], base=0, channel_multiplier=1).then_inc(pool_const, 1)
            pool.wait_ge(pool_const, 5)
            g.affine_select(out=ident[:, :], in_=ident[:, :], compare_op=ALU.not_equal, fill=1.0, base=0,
                            pattern=[[-1, P]], channel_multiplier=1).then_inc(pool_const, 1)
            g.affine_select(out=mask_diag[:, :], in_=mask_diag[:, :], compare_op=ALU.is_ge, fill=NEG, base=0,
                            pattern=[[-1, P]], channel_multiplier=1).then_inc(pool_const, 1)
            pool.wait_ge(vec_const, 1)
            g.affine_select(out=mask_new[:, :], in_=mask_new[:, :], compare_op=ALU.is_ge, fill=NEG, base=-56,
                            pattern=[[1, 120]], channel_multiplier=0).then_inc(pool_const, 1)
            pool.wait_ge(xt_ev_act, TB)
            pool.wait_ge(xt_ev_dve, TB)
            pool.dma_start(xT_dram.rearrange("k p t -> p k t"), main[:, :, :]).then_inc(xT_saved, 16)
            for h in range(H):
                pool.wait_ge(nat_ev, 2 * (h + 1))
                pool.dma_start(k_prompt[0, 0].rearrange("(b p) h c d -> p b h (c d)", p=P)[:, :, h, :],
                               k_stage[:, 0:4, :]).then_inc(k_out, 16)
                pool.dma_start(k_sample[0].rearrange("b t h c d -> (b t) h (c d)")[:, h, :],
                               k_stage[0:NS, 4, :]).then_inc(k_out, 16)
            pool.wait_ge(nat_ev, 32)
            pool.dma_start(v_prompt[0, 0].rearrange("(b p) h e -> p b (h e)", p=P), v_nat[:, 0:4, :]).then_inc(v_out, 16)
            pool.dma_start(v_sample[0].rearrange("b t h e -> (b t) (h e)"), v_nat[0:NS, 4, :]).then_inc(v_out, 16)
            for n in range(32):
                pool.wait_ge(out_act, 8 + n + 1)
                pool.dma_start(gate_dram[n], tmp[:, n % 2, :]).then_inc(gate_out[n % 2], 16)
            pool.wait_ge(tile_done, N_IN)
            pool.dma_start(st_rows[0:DB * PSTATE, :], state_pool.rearrange("l b s c -> (l b s) c")).then_inc(pool_in, 16)
            pool.dma_start(pool_sample[0, :, 0:PSTATE - DT, :], state_pool[0, :, DT:PSTATE, :]).then_inc(pool_out, 16)
            pool.wait_ge(pool_t_ev, 3)
            pool.dma_start(pool_prompt[0, 0], pool_rows[0:PSTATE, 0, :]).then_inc(pool_out, 16)
            for b in range(DB):
                pool.dma_start(pool_sample[0, b, PSTATE - DT:PSTATE, :],
                               pool_rows[b * DT:(b + 1) * DT, 1, :]).then_inc(pool_out, 16)

            def gather(dst, cache, n, s):
                pool.indirect_dma_start(out=dst[:, :], out_offset=None, in_=cache,
                                        in_offset=bass.IndirectOffsetOnAxis(ap=page_rows[:, n:n + 1], axis=0)
                                        ).then_inc(s, 16)

            for n in range(K_RING):
                gather(k_page[n], ck, n, kp_in[n])
            pool.wait_ge(pool_out, 16 * (2 + DB))
            pool.wait_ge(pool_d, 4)
            pool.wait_ge(pa_oev, 4 * H)
            for b in range(DB):
                for g_ in range(PAGES):
                    n = b * PAGES + g_
                    if b:
                        pool.wait_ge(sa_o, b)
                    gather(v_page[g_], cv, n, vp_in[g_])
                    if n + K_RING < DB * PAGES:
                        pool.wait_ge(sa_tmm, n + 1)
                        gather(k_page[n % K_RING], ck, n + K_RING, kp_in[n % K_RING])
            pool.wait_ge(sa_oev, DB)
            for g_ in range(4):
                if g_:
                    pool.wait_ge(pw_mm, 2 * g_)
                pool.dma_start(pw[:, :, :], pool_w[0, g_].rearrange("(k p) d -> p k d", p=P)).then_inc(pw_in, 16)
            for s in range(2):
                pool.wait_ge(gate_out[s], 16 * 16)
            pool.wait_ge(pw_ev, 8)
            for n in range(N_BR):
                if n >= 2:
                    pool.wait_ge(merged_sum, n - 1)
                pool.dma_start(back[:, n % 2, :], gate_dram[n]).then_inc(back_in[n % 2], 16)
                pool.dma_start(back[:, 2 + n % 2, :], gate_dram[KD + n]).then_inc(back_in[n % 2], 16)
            pool.wait_ge(xT_saved, 16)
            for m in range(N_OUT):
                if m < 2:
                    pool.wait_ge(merged_sum, N_BR - 1 + m)
                else:
                    pool.wait_ge(out_dve, 24 + m - 1)
                pool.dma_start(back[:, m % 2, :], xT_dram[m]).then_inc(back_in[m % 2], 16)
            pool.wait_ge(out_dve, 24 + N_OUT)
            for t in range(N_PQ):
                if t >= 2:
                    pool.wait_ge(sk_tmm, t - 1)
                pool.dma_start(sk_raw[:, t % 2, :], peer_sub_keys[0, t // 2, t % 2]).then_inc(sk_in[t % 2], 16)
            pool.wait_ge(n_lo["n2"], KD)
            pool.dma_start(hT_dram.rearrange("k p t -> p k t"), main[:, :, :]).then_inc(hT_saved, 16)
            for b in range(T // GB):
                pool.wait_ge(gm_ev, (b + 1) * (GB // NTOK_G))
                pool.dma_start(gmat_dram[b], gmat[:, :, :]).then_inc(gm_out, 16)
            def value_tile(n, i, first):
                s = i % 2
                if not first or i >= 2:
                    pool.wait_ge(wx_lod, n - 1)
                pool.wait_ge(ag_in[s], 32 * (i // 2) + (n - i) * 16 + 32)
                g.tensor_tensor(wx[s][:, :], a_back[s][:, :], g_back[s][:, :, :].rearrange("p b t -> p (b t)"),
                                ALU.mult).then_inc(wx_val, 1)
                pool.wait_ge(v_hid, n + 1)
                g.tensor_tensor(v_lo[i][:, :], v_raw[s][:, :], v_hi[i][:, :].bitcast(F), ALU.subtract).then_inc(v_lod, 1)

            for i in range(4):
                value_tile(i, i, True)
            with pool.Fori(1, N_U // 4) as q:
                for i in range(4):
                    value_tile(q * 4 + i, i, False)
            pool.wait_ge(k_out, 32 * H)
            pool.wait_ge(v_out, 32)

        @block.scalar
        def _(act):
            a = nc.scalar
            for tb in range(TB):
                act.wait_ge(xt_mm, tb + 1)
                w = tokens(tb)
                a.copy(main[:, 0:8, tb * P:tb * P + w],
                       pair[2 * (tb % 2)][:, :, :].rearrange("p a (k t) -> p (a k) t", t=P)[:, :, 0:w]).then_inc(xt_ev_act, 1)

            def split_hi(g):
                act.wait_ge(raw_in[g % 2], raw_count(g))
                if g >= 2:
                    act.wait_ge(tile_done, g - 1)
                a.copy(w_hi[g % 2][:, :, :], w_raw[g % 2][:, :, :]).then_inc(hi_done, 1)

            split_hi(0)
            split_hi(1)
            act.wait_ge(lam_dots, 1)
            a.activation(lam_v[:, 2:4], lam_v[:, 0:2], ACT.Exp).then_inc(lam_exp, 1)

            def squares(key, k0, n, first=0):
                for i in range(n):
                    c = first + i
                    if c >= 2:
                        act.wait_ge(sq_used[key], c - 1)
                    a.activation(tmp[:, c % 2, :], main[:, k0 + i, :], ACT.Square).then_inc(sq_done[key], 1)

            def root(key, n):
                act.wait_ge(n_var[key], n)
                a.activation(rstd[:, :], rstd[:, :], ACT.Sqrt).then_inc(n_sqrt[key], 1)

            def norm_hi(key, dst, c):
                act.wait_ge(n_val[key], c + 1)
                a.copy(act_hi[:, dst, :], tmp[:, c % 2, :]).then_inc(n_hi[key], 1)

            act.wait_ge(xt_ev_act, TB)
            act.wait_ge(xt_ev_dve, TB)
            squares("n1", 0, KD)
            root("n1", 1)
            for k in range(KD):
                norm_hi("n1", k, k)
            for t in range(N_IN):
                act.wait_ge(tile_done, t + 1)
                split_hi(t + 2)
                if T_K <= t - 2 < T_P:
                    i = t - 2 - T_K
                    act.wait_ge(nat_mm, i + 1)
                    if i == 0:
                        act.wait_ge(xt_mm, TB)
                    if i < 8:
                        if i:
                            act.wait_ge(k_out, 32 * i)
                        dst, c = k_stage, 0
                    else:
                        dst, c = v_nat, (i - 8) * P
                    a.copy(dst[:, 0:4, c:c + P], pair[2][:, 0, :].rearrange("p (b c) -> p b c", c=P)).then_inc(nat_ev, 1)
                    a.copy(dst[0:NS, 4, c:c + P], pair[2][0:NS, 1, 0:P]).then_inc(nat_ev, 1)
                if t < T_K:
                    if t == 0:
                        act.wait_ge(xT_saved, 16)
                        act.wait_ge(n_lo["n1"], KD)
                    a.mul(as_halves(main[:, t, :]), halves(t % 2), HD ** -0.5).then_inc(out_act, 1)
                elif t >= T_G:
                    n = t - T_G
                    if n < 2:
                        act.wait_ge(nat_mm, 16)
                    else:
                        act.wait_ge(gate_out[n % 2], 16 * (n // 2))
                    a.activation(as_halves(tmp[:, n % 2, :]), halves(t % 2), ACT.Sigmoid,
                                 bias=bgate_c[:, n:n + 1]).then_inc(out_act, 1)
            act.wait_ge(pool_t_mm, 1)
            a.copy(stT[:, :, :], pair[0][:, :, :].rearrange("p a (k t) -> p (a k) t", t=P)[:, :, 0:DB * PSTATE]).then_inc(pool_t_ev, 1)
            act.wait_ge(pool_t_mm, 2)
            a.copy(pool_rows[0:PSTATE, 0, :], pair[1][0:PSTATE, :, :].rearrange("p a c -> p (a c)")).then_inc(pool_t_ev, 1)
            act.wait_ge(pool_t_mm, 3)
            a.copy(pool_rows[0:NS, 1, :], pair[2][0:NS, :, :].rearrange("p a c -> p (a c)")).then_inc(pool_t_ev, 1)
            act.wait_ge(pool_out, 16 * (2 + DB))
            act.wait_ge(pool_d, 4)

            def take_aT(u):
                nk = u % 4 + 1
                act.wait_ge(pa_tmm, u + 1)
                if u >= 2:
                    act.wait_ge(pa_o, u - 1)
                a.copy(paT[u % 2][:, 0:nk, :],
                       pair[2][:, u % 2, 0:nk * P].rearrange("p (k q) -> p k q", q=P)).then_inc(pa_tev, 1)

            for u in range(4 * H):
                nk = (u % 4 + 1) * P
                act.wait_ge(pa_max, u + 1)
                if u >= 2:
                    act.wait_ge(pa_a, u - 1)
                for c in range(2):
                    a.activation(pp[u % 2][:, c, 0:nk], pair[u % 2][:, c, 0:nk], ACT.Exp,
                                 bias=p_stat[:, u % 2, 2 + c:3 + c],
                                 accum_out=p_stat[:, u % 2, 4 + c:5 + c]).then_inc(pa_exp, 1)
                if u:
                    take_aT(u - 1)
            take_aT(4 * H - 1)

            for b in range(DB):
                for g in range(PAGES):
                    n, s = b * PAGES + g, b * (PAGES + 1) + g
                    act.wait_ge(sa_tmm, n + 1)
                    if n >= 2:
                        act.wait_ge(sa_s, n - 1)
                    a.copy(kT_page[n % 2][:, 0:4, :], pair[s % 2][:, 0, :].rearrange("p (h k) -> p h k", k=P)).then_inc(sa_tev_a, 1)
                act.wait_ge(sa_max, b + 1)
                if b:
                    act.wait_ge(sa_ptmm, b)
                a.activation(sp_[:, 0:1024], pair[2][:, :, :].rearrange("p a k -> p (a k)"), ACT.Exp,
                             bias=s_stat[:, 3:4], accum_out=s_stat[:, 4:5]).then_inc(sa_exp, 1)
                a.activation(sp_[:, 1024:1024 + NS], pair[3][:, 0, 0:NS], ACT.Exp,
                             bias=s_stat[:, 3:4], accum_out=s_stat[:, 5:6]).then_inc(sa_exp, 1)
                act.wait_ge(sa_ptmm, b + 1)
                if b:
                    act.wait_ge(sa_o, b)
                s = b * (PAGES + 1) + PAGES
                pt = pair[s % 2][:, :, :].rearrange("p a (g h c t) -> p (a g) h c t", h=H, c=2, t=DT)
                for bank in range(2):
                    half = pair[s % 2][:, bank, :].rearrange("p (g c t) -> p g c t", c=2, t=DT)
                    a.copy(s_aT[:, 4 * bank:4 * bank + 4, :].rearrange("p g (h t) -> p (g h) t", t=DT),
                           half[:, :, 0, :]).then_inc(sa_cp, 1)
                a.copy(s_aTn[:, :].rearrange("p (h t) -> p h t", t=DT),
                       pair[3][0:NS, 0, P:2 * P].rearrange("p (h c t) -> p h c t", c=2, t=DT)[:, :, 0, :]).then_inc(sa_cp, 1)
            act.wait_ge(sa_oev, DB)
            act.wait_ge(pa_oev, 4 * H)
            squares("sub", 0, 1)
            for h in range(H):
                if h + 1 < H:
                    act.wait_ge(sq_used["sub"], h + 1)
                    act.wait_ge(n_lo["sub"], h) if h else None
                root("sub", h + 1)
                norm_hi("sub", h, h)
                if h + 1 < H:
                    act.wait_ge(n_lo["sub"], h + 1)
                    squares("sub", h + 1, 1, first=h + 1)
            for i in range(8):
                act.wait_ge(pw_mm, i + 1)
                if i < 2:
                    split = None
                    act.wait_ge(n_lo["sub"], H)
                else:
                    act.wait_ge(pw_ev, i - 1)
                a.mul(as_halves(tmp[:, i % 2, :]), halves(i % 2), pscale_c[:, i:i + 1]).then_inc(pw_val, 1)
                act.wait_ge(pw_val, i + 1)
                a.copy(act_hi[:, 8 + i, :], tmp[:, i % 2, :]).then_inc(pw_hi, 1)
            for d in range(N_BR):
                act.wait_ge(tile_done, G_BR + d + 1)
                split_hi(G_BR + d + 2)
            for k in range(KD):
                act.wait_ge(merged_sum, k + 1)
                a.copy(act_hi[:, k, :], main[:, k, :]).then_inc(mg_hi, 1)
            for m in range(N_OUT):
                act.wait_ge(tile_done, G_OUT + m + 1)
                split_hi(G_OUT + m + 2)
            act.wait_ge(out_dve, 24 + N_OUT)
            squares("n2", 0, KD)
            root("n2", 1)
            for k in range(KD):
                norm_hi("n2", k, k)

            def take_scores(t):
                act.wait_ge(sc_mm, t + 1)
                if t >= 2:
                    act.wait_ge(top_done, t - 1)
                ps = pair[2 + t % 2]
                a.copy(s_ev[:, t % 2, 0:4, :], ps[:, 0, :].rearrange("p (b k) -> p b k", k=P)).then_inc(sc_ev, 1)
                a.copy(s_ev[0:NS, t % 2, 4, :], ps[0:NS, 1, 0:P]).then_inc(sc_ev, 1)

            for t in range(N_PQ):
                act.wait_ge(tile_done, G_PQ + t + 1)
                if G_PQ + t + 2 < G_U:
                    split_hi(G_PQ + t + 2)
                act.wait_ge(sk_tmm, t + 1)
                if t >= 2:
                    act.wait_ge(sc_mm, t - 1)
                a.copy(skT[:, t % 2, :], pair[2 + t % 2][:, 1, P:2 * P]).then_inc(sk_tev, 1)
                if t:
                    take_scores(t - 1)
            take_scores(N_PQ - 1)
            def u_high(n, s, first=False):
                for i in range(2):
                    act.wait_ge(u_tmm, n * 2 + (i + 1))
                    if i == 0 and not first:
                        act.wait_ge(a_done, n - 1)
                    a.copy(w_hi[s][:, 8 * i:8 * i + 8, :],
                           pair[2][:, :, :].rearrange("p a (k e) -> p (a k) e", e=P)).then_inc(u_hi, 1)

            def gelu(n, s, first=False):
                act.wait_ge(a_done, n + 1)
                if not first:
                    act.wait_ge(a_out[s], (n - s) * 8)
                a.activation(as_halves(tmp[:, s, :]), halves(s), ACT.Gelu).then_inc(a_gelu, 1)

            def gate_exp(tb):
                w = tokens(tb)
                act.wait_ge(gx_in, tb + 1)
                a.activation(sel[0:w, 2, :], sel[0:w, 2, :], ACT.Exp).then_inc(gx_exp, 1)

            def take_selected(tb):
                w = tokens(tb)
                act.wait_ge(sel_tmm, tb + 1)
                for i, dst in enumerate((iaT, ibT, gT)):
                    a.copy(dst[:, tb * P:tb * P + w], pair[3][:, 0, i * P:i * P + w]).then_inc(sel_tev, 1)

            def take_gates(g, t0):
                act.wait_ge(gm_mm, g + 1)
                at = slice(t0, t0 + NTOK_G) if isinstance(t0, int) else bass.ds(t0, NTOK_G)
                a.copy(gmat[:, :, at], pair[3][:, :, :].rearrange("p a (t j) -> p j (a t)", j=PK)).then_inc(gm_ev, 1)

            u_high(0, 0, True)
            for n in range(G_FIRST):
                u_high(n + 1, (n + 1) % 2, n == 0)
                gelu(n, n % 2, n < 2)
                tb, i = divmod(n, SEL_TILES)
                if i == SEL_TILES - 1:
                    gate_exp(tb)
                if tb and i == 1:
                    take_selected(tb - 1)
            take_selected(TB - 1)
            act.wait_ge(hT_saved, 16)
            def gate_block(blk, first=False):
                for i in range(GB // NTOK_G):
                    n = blk * 8 + (G_FIRST + i)
                    u_high(n + 1, (i + 1) % 2)
                    gelu(n, i % 2)
                    if i == 0 and not first:
                        act.wait_ge(gm_out, blk * 16)
                    take_gates(blk * 8 + i, i * NTOK_G)

            gate_block(0, True)
            with act.Fori(1, T // GB) as blk:
                gate_block(blk)
            with act.Fori(0, (N_U - G_FIRST - N_G) // 2 - 1) as hh:
                for s in range(2):
                    n = hh * 2 + (G_FIRST + N_G + s)
                    u_high(n + 1, 1 - s)
                    gelu(n, s)
            u_high(N_U - 1, 1)
            gelu(N_U - 2, 0)
            gelu(N_U - 1, 1)

            def value_high(n, i, first):
                s = i % 2
                act.wait_ge(v_in[s], 16 * (i // 2) + (n - i) * 8 + 16)
                if not first:
                    act.wait_ge(acc_ps, (n - i) * 8 + 16 * (i // 2) - 16)
                a.copy(v_hi[i][:, :], v_raw[s][:, :]).then_inc(v_hid, 1)
                act.wait_ge(wx_val, n + 1)
                a.copy(wx_hi[i][:, :], wx[s][:, :]).then_inc(wx_hid, 1)

            for i in range(4):
                value_high(i, i, True)
            with act.Fori(1, N_U // 4) as q:
                for i in range(4):
                    value_high(q * 4 + i, i, False)
            act.wait_ge(acc_done, N_U // 2 * KD)
            squares("nf", 0, KD)
            root("nf", 1)
            for k in range(KD):
                act.wait_ge(yt_mm, k + 1)
                ps = pair[2 + k % 2]
                c = slice(k * P, (k + 1) * P)
                a.copy(y_rows[:, 0:4, c], ps[:, 0, :].rearrange("p (b c) -> p b c", c=P)).then_inc(yt_ev, 1)
                a.copy(y_rows[0:NS, 4, c], ps[0:NS, 1, 0:P]).then_inc(yt_ev, 1)

        @block.vector
        def _(dve):
            v = nc.vector
            count = [0]

            def link(*ops):
                for op in ops:
                    op.then_inc(chain, 1)
                count[0] += len(ops)
                dve.wait_ge(chain, count[0])

            dve.wait_ge(pool_const, 7)
            link(v.tensor_copy(iota_f[:, :], iota_i[:, :]),
                 v.tensor_copy(col_f[:, 0:1], col_i[:, 0:1]),
                 v.tensor_single_scalar(col_i[:, 1:2], col_i[:, 0:1], 7, ALU.bitwise_and),
                 v.tensor_single_scalar(col_i[:, 2:3], col_i[:, 0:1], 3, ALU.logical_shift_right))
            link(v.tensor_single_scalar(col_i[:, 3:4], col_i[:, 2:3], 1, ALU.bitwise_and))
            link(v.tensor_copy(col_f[:, 1:3], col_i[:, 1:4:2]))
            link(v.tensor_scalar_add(col_f[:, 3:4], col_f[:, 1:2], 56.0))
            v.tensor_scalar(mask_new[:, :], iota_f[:, 0:120], col_f[:, 3:4], NEG, ALU.is_gt, ALU.mult).then_inc(vec_const, 1)
            for g, w in enumerate(WINDOWS):
                link(v.tensor_scalar(cinv[:, g, :], iota_f[:, 0:16], 1.0, float(w), ALU.add, ALU.min))
            link(v.reciprocal(cinv[:, :, :], cinv[:, :, :]))
            dve.wait_ge(const_in, 16 * 11)
            v.tensor_scalar(page_rows[:, :], page_i[:, :], float(P), col_f[:, 0:1], ALU.mult, ALU.add).then_inc(vec_const, 1)
            v.tensor_scalar_mul(subgc8[:, :], subgc[:, :], 1.0 - LAM_INIT).then_inc(vec_const, 1)
            for i in range(2):
                op = v.tensor_tensor_reduce(out=lam_raw[:, 4, :], in0=lam_raw[:, 2 * i, :], in1=lam_raw[:, 2 * i + 1, :],
                                            scale=1.0, scalar=0.0, op0=ALU.mult, op1=ALU.add, accum_out=lam_v[:, i:i + 1])
                if i:
                    op.then_inc(lam_dots, 1)
                else:
                    link(op)
            for tb in range(TB):
                dve.wait_ge(xt_mm, tb + 1)
                w = tokens(tb)
                v.tensor_copy(main[:, 8:16, tb * P:tb * P + w],
                              pair[2 * (tb % 2) + 1][:, :, :].rearrange("p a (k t) -> p (a k) t", t=P)[:, :, 0:w]).then_inc(xt_ev_dve, 1)
            dve.wait_ge(lam_exp, 1)
            link(v.tensor_scalar_add(lam_c[:, 0:1], lam_v[:, 2:3], LAM_INIT))
            link(v.tensor_sub(lam_c[:, 0:1], lam_c[:, 0:1], lam_v[:, 3:4]))
            link(v.tensor_scalar_mul(lam_c[:, 1:2], lam_c[:, 0:1], -1.0),
                 v.tensor_scalar_add(col_f[:, 4:5], lam_c[:, 0:1], 1.0))
            link(v.tensor_mul(col_f[:, 5:6], col_f[:, 4:5], col_f[:, 2:3]))
            link(v.tensor_scalar(col_f[:, 6:7], col_f[:, 5:6], -1.0, 1.0, ALU.mult, ALU.add))

            def split_lo(g):
                dve.wait_ge(hi_done, g + 1)
                v.tensor_sub(w_lo[g % 2][:, :, :], w_raw[g % 2][:, :, :], w_hi[g % 2][:, :, :].bitcast(F)).then_inc(lo_done, 1)

            def variance(key, n, ps, width, eps):
                dve.wait_ge(sq_used[key], n)
                v.tensor_scalar(as_halves(rstd[:, :]), halves(ps), 1.0 / width, eps, ALU.mult, ALU.add).then_inc(n_var[key], 1)

            def inverse(key, n):
                dve.wait_ge(n_sqrt[key], n)
                link(v.reciprocal(rstd[:, :], rstd[:, :]))

            def norm_value(key, src, gain, c):
                if c >= 2:
                    dve.wait_ge(n_lo[key], c - 1)
                v.scalar_tensor_tensor(tmp[:, c % 2, :], main[:, src, :], gain, rstd[:, :], ALU.mult, ALU.mult).then_inc(n_val[key], 1)

            def norm_lo(key, dst, c):
                dve.wait_ge(n_hi[key], c + 1)
                v.tensor_sub(act_lo[:, dst, :], tmp[:, c % 2, :], act_hi[:, dst, :].bitcast(F)).then_inc(n_lo[key], 1)

            def norm_all(key, gains, eps):
                variance(key, KD, 0, D, eps)
                inverse(key, 1)
                for k in range(KD):
                    norm_value(key, k, gains[:, k:k + 1], k)
                    if k:
                        norm_lo(key, k - 1, k - 1)
                norm_lo(key, KD - 1, KD - 1)

            split_lo(0)
            split_lo(1)
            norm_all("n1", g1c, NORM_EPS)
            for t in range(N_IN):
                dve.wait_ge(tile_done, t + 1)
                split_lo(t + 2)
                if T_K <= t < T_V:
                    v.tensor_copy(as_halves(main[:, 8 + t - T_K, :]), halves(t % 2)).then_inc(out_dve, 1)
                elif T_V <= t < T_P:
                    i = t - T_V
                    if i >= 2:
                        dve.wait_ge(nat_mm, 8 + i - 1)
                    v.tensor_copy(as_halves(tmp[:, i % 2, :]), halves(t % 2)).then_inc(out_dve, 1)
                elif T_P <= t < T_G:
                    v.tensor_copy(as_halves(pT[:, t - T_P, :]), halves(t % 2)).then_inc(out_dve, 1)
            dve.wait_ge(tile_done, N_IN)
            dve.wait_ge(out_dve, 24)
            dve.wait_ge(pool_t_ev, 3)
            L0 = PSTATE + SEQ
            for g, w in enumerate(WINDOWS):
                e, f = ex
                def new(b):
                    return b[:, :, L0:].rearrange("p k (s x) -> p k s x", x=SEG)
                p2 = pT[:, 2 * g:2 * g + 2, :]
                ops = [v.memset(e[:, :, 0:PSTATE], 0.0), v.tensor_copy(e[:, :, PSTATE:L0], p2[:, :, 0:SEQ])]
                for k in range(2):
                    ops += [v.tensor_copy(new(e)[:, k, :, 0:PSTATE],
                                          stT[:, 2 * g + k, :].rearrange("p (s x) -> p s x", x=PSTATE)),
                            v.tensor_copy(new(e)[:, k, :, PSTATE:], p2[:, k, SEQ:].rearrange("p (s x) -> p s x", x=DT))]
                link(*ops)
                step = 1
                while step < w:
                    link(v.tensor_copy(f[:, :, 0:step], e[:, :, 0:step]),
                         v.tensor_add(f[:, :, step:], e[:, :, step:], e[:, :, 0:EXL - step]))
                    e, f = f, e
                    step *= 2
                for k in range(2):
                    link(v.tensor_mul(f[:, k, 0:16], e[:, k, PSTATE:PSTATE + 16], cinv[:, g, :]))
                    link(v.tensor_sub(f[:, k, 0:16], f[:, k, 0:16], p2[:, k, 0:16]))
                    link(v.scalar_tensor_tensor(p2[:, k, 0:SEQ], e[:, k, PSTATE:L0], 1.0 / w, p2[:, k, 0:SEQ], ALU.mult, ALU.subtract),
                         v.scalar_tensor_tensor(p2[:, k, SEQ:].rearrange("p (s x) -> p s x", x=DT), new(e)[:, k, :, PSTATE:],
                                                1.0 / w, p2[:, k, SEQ:].rearrange("p (s x) -> p s x", x=DT), ALU.mult, ALU.subtract))
                    link(v.tensor_copy(p2[:, k, 0:16], f[:, k, 0:16]))
                v.nop() if False else None
                v.tensor_copy(col_f[:, 7:8], col_f[:, 0:1]).then_inc(pool_d, 1)
            dve.wait_ge(pool_out, 16 * (2 + DB))
            dve.wait_ge(pool_d, 4)

            def row_max(u):
                nk = (u % 4 + 1) * P
                dve.wait_ge(pa_s, u + 1)
                ps, st = pair[u % 2], p_stat[:, u % 2, :]
                link(*[v.tensor_add(ps[:, c, nk - P:nk], ps[:, c, nk - P:nk], mask_diag[:, :]) for c in range(2)])
                if u >= 2:
                    dve.wait_ge(pa_a, u - 1)
                link(v.tensor_reduce(out=st[:, 0:2], in_=ps[:, :, 0:nk], axis=AX.X, op=ALU.max))
                v.tensor_scalar_mul(st[:, 2:4], st[:, 0:2], -1.0).then_inc(pa_max, 1)

            def weights(u):
                nk = (u % 4 + 1) * P
                s, st = pp[u % 2], p_stat[:, u % 2, :]
                dve.wait_ge(pa_exp, 2 * (u + 1))
                link(v.reciprocal(st[:, 6:8], st[:, 4:6]))
                if u >= 2:
                    dve.wait_ge(pa_tmm, u - 1)
                link(v.tensor_scalar_mul(pa_buf[u % 2][:, 0:nk], s[:, 0, 0:nk], st[:, 6:7]),
                     v.tensor_mul(st[:, 7:8], st[:, 7:8], lam_c[:, 1:2]))
                v.scalar_tensor_tensor(pa_buf[u % 2][:, 0:nk], s[:, 1, 0:nk], st[:, 7:8], pa_buf[u % 2][:, 0:nk],
                                       ALU.mult, ALU.add).then_inc(pa_a, 1)

            def take_o(u):
                h, qb = divmod(u, 4)
                dve.wait_ge(pa_o, u + 1)
                v.tensor_copy(main[:, h, qb * P:(qb + 1) * P], pair[3][:, u % 2, 0:P]).then_inc(pa_oev, 1)

            for u in range(4 * H + 2):
                if u < 4 * H:
                    row_max(u)
                if 1 <= u <= 4 * H:
                    weights(u - 1)
                if u >= 2:
                    take_o(u - 2)

            dve.wait_ge(pool_const, 8)
            link(v.memset(qd[:, :], 0.0))
            for b in range(DB):
                if b:
                    dve.wait_ge(sa_s, PAGES * b + b)
                for c in range(2):
                    r_ = slice(c * HD, (c + 1) * HD)
                    v.tensor_copy(qd[r_, :].rearrange("p (h x) -> p h x", x=144)[:, :, c * DT:(c + 1) * DT],
                                  main[r_, 0:H, SEQ + b * DT:SEQ + (b + 1) * DT]).then_inc(sa_qd, 1)
                for g in range(PAGES):
                    n, s = b * PAGES + g, b * (PAGES + 1) + g
                    dve.wait_ge(sa_tmm, n + 1)
                    if n >= 2:
                        dve.wait_ge(sa_s, (n - 2) + (n - 2) // PAGES + 1)
                    v.tensor_copy(kT_page[n % 2][:, 4:8, :], pair[s % 2][:, 1, :].rearrange("p (h k) -> p h k", k=P)).then_inc(sa_tev_d, 1)
                dve.wait_ge(sa_s, (PAGES + 1) * (b + 1))
                if b:
                    dve.wait_ge(sa_exp, 2 * b)
                link(v.tensor_add(pair[3][:, 0, 0:NS], pair[3][:, 0, 0:NS], mask_new[:, 56 - 8 * b:56 - 8 * b + NS]))
                link(v.tensor_reduce(out=s_stat[:, 0:1], in_=pair[2][:, :, :], axis=AX.XY, op=ALU.max),
                     v.tensor_reduce(out=s_stat[:, 1:2], in_=pair[3][:, 0, 0:NS], axis=AX.X, op=ALU.max))
                link(v.tensor_max(s_stat[:, 2:3], s_stat[:, 0:1], s_stat[:, 1:2]))
                v.tensor_scalar_mul(s_stat[:, 3:4], s_stat[:, 2:3], -1.0).then_inc(sa_max, 1)
                dve.wait_ge(sa_exp, 2 * (b + 1))
                link(v.tensor_add(s_stat[:, 6:7], s_stat[:, 4:5], s_stat[:, 5:6]))
                link(v.reciprocal(s_stat[:, 6:7], s_stat[:, 6:7]))
                link(v.tensor_mul(s_stat[:, 7:8], s_stat[:, 6:7], col_f[:, 6:7]))
                v.tensor_scalar_mul(sp_[:, :], sp_[:, :], s_stat[:, 7:8]).then_inc(sa_p, 1)
                dve.wait_ge(sa_cp, 3 * (b + 1))
                s = b * (PAGES + 1) + PAGES
                for bank in range(2):
                    half = pair[s % 2][:, bank, :].rearrange("p (g c t) -> p g c t", c=2, t=DT)
                    o = s_aT[:, 4 * bank:4 * bank + 4, :].rearrange("p g (h t) -> p (g h) t", t=DT)
                    v.tensor_add(o, half[:, :, 1, :], o).then_inc(sa_aT, 1)
                o = s_aTn[:, :].rearrange("p (h t) -> p h t", t=DT)
                v.tensor_add(o, pair[3][0:NS, 0, P:2 * P].rearrange("p (h c t) -> p h c t", c=2, t=DT)[:, :, 1, :], o).then_inc(sa_aT, 1)
                dve.wait_ge(sa_o, b + 1)
                v.tensor_copy(main[:, 0:H, SEQ + b * DT:SEQ + (b + 1) * DT],
                              pair[3][:, 1, 0:NS].rearrange("p (h t) -> p h t", t=DT)).then_inc(sa_oev, 1)
            dve.wait_ge(sa_oev, DB)
            for h in range(H):
                variance("sub", h + 1, h % 2, VD, SUBLN_EPS)
                inverse("sub", h + 1)
                norm_value("sub", h, subgc8[:, :], h)
                norm_lo("sub", h, h)
            for i in range(8):
                dve.wait_ge(pw_hi, i + 1)
                v.tensor_sub(act_lo[:, 8 + i, :], tmp[:, i % 2, :], act_hi[:, 8 + i, :].bitcast(F)).then_inc(pw_ev, 1)
            dve.wait_ge(pw_ev, 8)
            for d in range(N_BR):
                dve.wait_ge(tile_done, G_BR + d + 1)
                split_lo(G_BR + d + 2)
                dve.wait_ge(back_in[d % 2], 32 * (d // 2 + 1))
                if d:
                    dve.wait_ge(merged_sum, d)
                pa_, pb_ = (0, 1) if d % 2 == 0 else (2, 3)
                link(v.tensor_mul(as_halves(mtmp[:, 0, :]), halves(pa_), as_halves(back[:, d % 2, :])),
                     v.tensor_mul(as_halves(mtmp[:, 1, :]), halves(pb_), as_halves(back[:, 2 + d % 2, :])))
                v.tensor_add(main[:, d, :], mtmp[:, 0, :], mtmp[:, 1, :]).then_inc(merged_sum, 1)
            for k in range(KD):
                dve.wait_ge(mg_hi, k + 1)
                v.tensor_sub(act_lo[:, k, :], main[:, k, :], act_hi[:, k, :].bitcast(F)).then_inc(mg_lo, 1)
            dve.wait_ge(mg_lo, KD)
            for m in range(N_OUT):
                dve.wait_ge(tile_done, G_OUT + m + 1)
                split_lo(G_OUT + m + 2)
                dve.wait_ge(back_in[m % 2], 32 * (N_BR // 2) + 16 * (m // 2 + 1))
                v.tensor_add(as_halves(main[:, m, :]), halves(m % 2), as_halves(back[:, m % 2, :])).then_inc(out_dve, 1)
            norm_all("n2", g2c, NORM_EPS)

            def best(t):
                dve.wait_ge(sc_ev, 2 * (t + 1))
                s = t % 2
                rows = [(tb, tokens(tb)) for tb in range(TB)]
                link(*[v.max(out=sv[0:w, tb, t, 0:8], in_=s_ev[0:w, s, tb, :]) for tb, w in rows])
                link(*[v.max_index(out=si[0:w, tb, t, 0:8], in_max=sv[0:w, tb, t, 0:8], in_values=s_ev[0:w, s, tb, :]) for tb, w in rows])
                link(*[v.match_replace(out=s_ev[0:w, s, tb, :], in_to_replace=sv[0:w, tb, t, 0:8],
                                       in_values=s_ev[0:w, s, tb, :], imm_value=-3e38) for tb, w in rows])
                link(*[v.max(out=sv[0:w, tb, t, 8:16], in_=s_ev[0:w, s, tb, :]) for tb, w in rows])
                for tb, w in rows:
                    op = v.max_index(out=si[0:w, tb, t, 8:16], in_max=sv[0:w, tb, t, 8:16], in_values=s_ev[0:w, s, tb, :])
                op.then_inc(top_done, 1)

            for t in range(N_PQ):
                dve.wait_ge(tile_done, G_PQ + t + 1)
                if G_PQ + t + 2 < G_U:
                    split_lo(G_PQ + t + 2)
                if t >= 2:
                    dve.wait_ge(sc_mm, t - 1)
                v.tensor_copy(as_halves(q_ev[:, t % 2, :]), halves(t % 2)).then_inc(q_evd, 1)
                if t:
                    best(t - 1)
            best(N_PQ - 1)
            dve.wait_ge(top_done, N_PQ)

            def u_low(n, s, halves_=range(2)):
                for i in halves_:
                    dve.wait_ge(u_hi, n * 2 + (i + 1))
                    v.tensor_sub(w_lo[s][:, 8 * i:8 * i + 8, :],
                                 pair[2][:, :, :].rearrange("p a (k e) -> p (a k) e", e=P),
                                 w_hi[s][:, 8 * i:8 * i + 8, :].bitcast(F)).then_inc(u_lo, 1)

            def sel_sums(tb, w):
                svh = sv[0:w, tb, :, :].rearrange("p (h c) a -> p h c a", c=2)
                full = [w, PH, TOPK, TOPK]
                link(v.tensor_copy(si_f[0:w], si[0:w, tb, :, :]),
                     v.tensor_tensor(cand[0:w].rearrange("p h (a b) -> p h a b", b=TOPK),
                                     svh[:, :, 0, :].unsqueeze(3).broadcast_to(full),
                                     svh[:, :, 1, :].unsqueeze(2).broadcast_to(full), ALU.add))
                link(*[v.max(out=ts[0:w, h, 0:8], in_=cand[0:w, h, :]) for h in range(PH)])

            def sel_first(tb, w):
                link(*[v.max_index(out=tp[0:w, h, 0:8], in_max=ts[0:w, h, 0:8], in_values=cand[0:w, h, :]) for h in range(PH)])
                link(*[v.match_replace(out=cand[0:w, h, :], in_to_replace=ts[0:w, h, 0:8], in_values=cand[0:w, h, :],
                                       imm_value=-3e38) for h in range(PH)])

            def sel_second(tb, w):
                link(*[v.max(out=ts[0:w, h, 8:16], in_=cand[0:w, h, :]) for h in range(PH)])
                link(*[v.max_index(out=tp[0:w, h, 8:16], in_max=ts[0:w, h, 8:16], in_values=cand[0:w, h, :]) for h in range(PH)])
                tpw = tp[0:w].rearrange("p h k -> p (h k)")
                link(v.tensor_single_scalar(tpa[0:w, 0, :], tpw, 4, ALU.logical_shift_right),
                     v.tensor_single_scalar(tpa[0:w, 1, :], tpw, 15, ALU.bitwise_and))
                link(v.tensor_copy(tpf[0:w], tpa[0:w]))

            def sel_key(tb, w, c):
                full = [w, PH, TOPK, TOPK]
                link(v.tensor_tensor(oh[0:w], tpf[0:w, c, :].unsqueeze(2).broadcast_to([w, PH * TOPK, 16]),
                                     iota_f[0:w, 0:16].unsqueeze(1).broadcast_to([w, PH * TOPK, 16]), ALU.is_equal))
                ohk = oh[0:w].rearrange("p (h k) a -> p h k a", k=TOPK)
                sih = si_f[0:w].rearrange("p (h c) a -> p h c a", c=2)[:, :, c, :]
                link(v.tensor_tensor(ohk, ohk, sih.unsqueeze(2).broadcast_to(full), ALU.mult))
                if c == 0 and tb:
                    dve.wait_ge(sel_tmm, tb)
                link(v.tensor_reduce(out=sel[0:w, c, :], in_=oh[0:w], axis=AX.X, op=ALU.add))

            def sel_gate_in(tb, w):
                v.tensor_tensor(sel[0:w, 2, :].rearrange("p (h k) -> p h k", k=TOPK), ts[0:w],
                                ts[0:w, :, 0:1].broadcast_to([w, PH, TOPK]), ALU.subtract).then_inc(gx_in, 1)

            def sel_gate_out(tb, w):
                sel2 = sel[0:w, 2, :].rearrange("p (h k) -> p h k", k=TOPK)
                dve.wait_ge(gx_exp, tb + 1)
                link(v.tensor_reduce(out=ssum[0:w, 0, :], in_=sel2, axis=AX.X, op=ALU.add))
                link(v.reciprocal(ssum[0:w, 1, :], ssum[0:w, 0, :]))
                v.tensor_tensor(sel2, sel2, ssum[0:w, 1, :].unsqueeze(2).broadcast_to([w, PH, TOPK]), ALU.mult).then_inc(sel_done, 1)

            u_low(0, 0)
            for tb in range(TB):
                w = tokens(tb)
                n = SEL_TILES * tb + 1
                sel_sums(tb, w)
                u_low(n, 1)
                sel_first(tb, w)
                u_low(n + 1, 0)
                sel_second(tb, w)
                u_low(n + 2, 1)
                sel_key(tb, w, 0)
                u_low(n + 3, 0)
                sel_key(tb, w, 1)
                sel_gate_in(tb, w)
                u_low(n + 4, 1)
                u_low(n + 5, 0)
                sel_gate_out(tb, w)
            dve.wait_ge(sel_tev, 3 * TB)
            link(v.tensor_copy(gTh[:, :], gT[:, :]))
            link(v.tensor_sub(gT[:, :], gT[:, :], gTh[:, :].bitcast(F)))

            def one_hots(g, s, t0, part, first=False):
                if part == 0 and not first:
                    dve.wait_ge(gm_mm, g - 1)
                for n in range(part * 4, part * 4 + 4):
                    def col(x):
                        return x[:, t0 + n:t0 + n + 1] if isinstance(t0, int) else x[:, bass.ds(t0 + n, 1)]
                    v.tensor_scalar(oi[s][:, n, :], iota_f[:, :], col(iaT), None, ALU.is_equal)
                    v.tensor_scalar(jh[s][:, n, :], iota_f[:, :], col(ibT), col(gTh[:, :].bitcast(F)), ALU.is_equal, ALU.mult)
                    op = v.tensor_scalar(jl[s][:, n, :], iota_f[:, :], col(ibT), col(gT), ALU.is_equal, ALU.mult)
                if part == 1:
                    op.then_inc(oh_v, 1)

            for g in range(2):
                for part in range(2):
                    one_hots(g, g, g * NTOK_G, part, True)
                    u_low(G_FIRST + 1 + g, (1 + g) % 2, [part])
            with dve.Fori(1, N_G // 2) as gg:
                for s in range(2):
                    for part in range(2):
                        one_hots(gg * 2 + s, s, gg * (2 * NTOK_G) + s * NTOK_G, part)
                        u_low(gg * 2 + (G_FIRST + 1 + s), 1 - s, [part])
            with dve.Fori(0, (N_U - G_FIRST - N_G) // 2 - 1) as hh:
                for s in range(2):
                    u_low(hh * 2 + (G_FIRST + N_G + 1 + s), 1 - s)
            u_low(N_U - 1, 1)

            def value_pair(n, i, first):
                for m in range(2):
                    dve.wait_ge(wx_hid, n + (m + 1))
                    v.tensor_sub(wx_lo[i + m][:, :], wx[(i + m) % 2][:, :], wx_hi[i + m][:, :].bitcast(F)).then_inc(wx_lod, 1)

            def take_sums(at, ds):
                for d in ds:
                    dve.wait_ge(acc_ps, at + (d + 1))
                    v.tensor_add(as_halves(main[:, d, :]), halves(d % 4), as_halves(main[:, d, :])).then_inc(acc_done, 1)

            FRONT, BACK = range(12), range(12, KD)
            value_pair(0, 0, True)
            dve.wait_ge(hT_back, 16)
            take_sums(0, FRONT)
            value_pair(2, 2, True)
            take_sums(0, BACK)
            take_sums(16, FRONT)
            with dve.Fori(1, N_U // 4) as q:
                value_pair(q * 4, 0, False)
                take_sums(q * 32 - 16, BACK)
                take_sums(q * 32, FRONT)
                value_pair(q * 4 + 2, 2, False)
                take_sums(q * 32, BACK)
                take_sums(q * 32 + 16, FRONT)
            take_sums(N_U // 2 * KD - KD, BACK)
            variance("nf", KD, 0, D, NORM_EPS)
            inverse("nf", 1)
            for k in range(KD):
                if k >= 2:
                    dve.wait_ge(yt_mm, k - 1)
                v.scalar_tensor_tensor(tmp[:, k % 2, :], main[:, k, :], gfc[:, k:k + 1], rstd[:, :], ALU.mult, ALU.mult).then_inc(n_val["nf"], 1)

        @block.tensor
        def _(pe):
            m_ = nc.tensor.matmul

            def tr(out, in_):
                n = in_.shape[0]
                return nc.tensor.transpose(out, in_, ident[0:n, 0:n])

            pe.wait_ge(pool_const, 7)
            for tb in range(TB):
                pe.wait_ge(x_loaded[tb % 2], 16 * (tb // 2 + 1))
                if tb >= 2:
                    pe.wait_ge(xt_ev_act, tb - 1)
                    pe.wait_ge(xt_ev_dve, tb - 1)
                w = tokens(tb)
                for k in range(KD):
                    ps = pair[2 * (tb % 2) + k // 8]
                    i = tr(ps[:, k // 4 % 2, (k % 4) * P:(k % 4) * P + w], x_in[0:w, tb % 2, k * P:(k + 1) * P])
                i.then_inc(xt_mm, 1)

            def sum_squares(key, c0, n, ps):
                for i in range(n):
                    pe.wait_ge(sq_done[key], c0 + i + 1)
                    for hf in range(2):
                        op = m_(pair[ps][:, hf, 0:TH], ones[:, :], tmp[:, (c0 + i) % 2, hf * TH:(hf + 1) * TH],
                                start=(i == 0), stop=(i == n - 1))
                    op.then_inc(sq_used[key], 1)

            def tile(whi, wlo, out, ks=range(KD), wait=None, starts=True, ends=True):
                ks = list(ks)
                for k in ks:
                    if wait:
                        wait(k)
                    for i, (w, x) in enumerate(((whi, act_hi), (whi, act_lo), (wlo, act_hi))):
                        for hf in range(2):
                            op = m_(pair[out][:, hf, 0:TH], w[:, k, :], x[:, k, hf * TH:(hf + 1) * TH],
                                    start=(starts and k == ks[0] and i == 0), stop=(ends and k == ks[-1] and i == 2))
                return op

            pe.wait_ge(xt_ev_act, TB)
            pe.wait_ge(xt_ev_dve, TB)
            sum_squares("n1", 0, KD, 0)

            def to_rows(i):
                if i < 8:
                    pe.wait_ge(out_dve, i + 1)
                    src = main[:, 8 + i, :]
                else:
                    pe.wait_ge(out_dve, i + 1)
                    src = tmp[:, i % 2, :]
                if i:
                    pe.wait_ge(nat_ev, 2 * i)
                for tb in range(TB):
                    w = tokens(tb)
                    op = tr(pair[2][0:w, tb // 4, (tb % 4) * P:(tb % 4 + 1) * P], src[:, tb * P:tb * P + w])
                op.then_inc(nat_mm, 1)

            for t in range(N_IN):
                pe.wait_ge(lo_done, t + 1)
                if t >= 2:
                    wait_w_in_out(pe, t - 2)
                if t == 0:
                    pe.wait_ge(n_var["n1"], 1)
                tile(w_hi[t % 2], w_lo[t % 2], t % 2,
                     wait=(lambda k: pe.wait_ge(n_lo["n1"], k + 1)) if t == 0 else None).then_inc(tile_done, 1)
                if T_K <= t - 1 < T_P:
                    to_rows(t - 1 - T_K)
            pe.wait_ge(out_act, 40)
            pe.wait_ge(nat_ev, 32)
            pe.wait_ge(pool_in, 16)
            n = DB * PSTATE
            for k in range(8):
                op = tr(pair[0][:, k // 4, (k % 4) * P:(k % 4) * P + n], st_rows[0:n, k * P:(k + 1) * P])
            op.then_inc(pool_t_mm, 1)
            for k in range(8):
                op = tr(pair[1][0:PSTATE, k // 4, (k % 4) * P:(k % 4 + 1) * P], pT[:, k, SEQ - PSTATE:SEQ])
            op.then_inc(pool_t_mm, 1)
            for k in range(8):
                op = tr(pair[2][0:NS, k // 4, (k % 4) * P:(k % 4 + 1) * P], pT[:, k, SEQ:T])
            op.then_inc(pool_t_mm, 1)
            pe.wait_ge(pool_t_ev, 3)

            def scores(u):
                h, qb = divmod(u, 4)
                nk = (qb + 1) * P
                if u >= 2:
                    pe.wait_ge(pa_exp, 2 * (u - 1))
                for c in range(2):
                    r_ = slice(c * HD, (c + 1) * HD)
                    op = m_(pair[u % 2][:, c, 0:nk], main[r_, h, qb * P:(qb + 1) * P], main[r_, 8 + h, 0:nk],
                            start=True, stop=True)
                op.then_inc(pa_s, 1)

            def turn(u):
                nk = u % 4 + 1
                pe.wait_ge(pa_a, u + 1)
                if u >= 2:
                    pe.wait_ge(pa_tev, u - 1)
                for k in range(nk):
                    op = tr(pair[2][:, u % 2, k * P:(k + 1) * P], pa_buf[u % 2][:, k * P:(k + 1) * P])
                op.then_inc(pa_tmm, 1)

            def output(u):
                h, nk = u // 4, u % 4 + 1
                pe.wait_ge(pa_tev, u + 1)
                if u >= 2:
                    pe.wait_ge(pa_oev, u - 1)
                for k in range(nk):
                    op = m_(pair[3][:, u % 2, 0:P], v_nat[:, k, h * VD:(h + 1) * VD], paT[u % 2][:, k, :],
                            start=(k == 0), stop=(k == nk - 1))
                op.then_inc(pa_o, 1)

            scores(0)
            for u in range(4 * H):
                if u + 1 < 4 * H:
                    scores(u + 1)
                turn(u)
                if u:
                    output(u - 1)
            output(4 * H - 1)

            pe.wait_ge(pa_oev, 4 * H)

            def page_T(n):
                b, g = divmod(n, PAGES)
                s = b * (PAGES + 1) + g
                pe.wait_ge(kp_in[n % K_RING], 16 * (n // K_RING + 1))
                if n >= 2:
                    pe.wait_ge(sa_tev_a, n - 1)
                    pe.wait_ge(sa_tev_d, n - 1)
                if b and g < 2:
                    pe.wait_ge(sa_aT, 3 * b)
                for h in range(H):
                    op = tr(pair[s % 2][:, h // 4, (h % 4) * P:(h % 4 + 1) * P], k_page[n % K_RING][:, h * P:(h + 1) * P])
                op.then_inc(sa_tmm, 1)

            page_T(0)
            for b in range(DB):
                pe.wait_ge(sa_qd, 2 * (b + 1))
                if b:
                    pe.wait_ge(sa_exp, 2 * b)
                for g in range(PAGES):
                    n = b * PAGES + g
                    if g + 1 < PAGES:
                        page_T(n + 1)
                    pe.wait_ge(sa_tev_a, n + 1)
                    pe.wait_ge(sa_tev_d, n + 1)
                    for h in range(H):
                        op = m_(pair[2][:, g // 4, (g % 4) * P:(g % 4 + 1) * P], qd[:, h * P:(h + 1) * P],
                                kT_page[n % 2][:, h, :], start=(h == 0), stop=(h == H - 1))
                    op.then_inc(sa_s, 1)
                if b:
                    pe.wait_ge(sa_aT, 3 * b)
                for h in range(H):
                    op = m_(pair[3][:, 0, 0:NS], qd[:, h * P:(h + 1) * P], main[:, 8 + h, SEQ:T],
                            start=(h == 0), stop=(h == H - 1))
                op.then_inc(sa_s, 1)
                s = b * (PAGES + 1) + PAGES
                pe.wait_ge(sa_p, b + 1)
                for g in range(PAGES):
                    tr(pair[s % 2][:, g // 4, (g % 4) * P:(g % 4 + 1) * P], sp_[:, g * P:(g + 1) * P])
                tr(pair[3][0:NS, 0, P:2 * P], sp_[:, 1024:1024 + NS]).then_inc(sa_ptmm, 1)
                if (b + 1) < DB:
                    page_T((b + 1) * PAGES)
                pe.wait_ge(sa_aT, 3 * (b + 1))
                if b:
                    pe.wait_ge(sa_oev, b)
                for g in range(PAGES):
                    pe.wait_ge(vp_in[g], 16 * (b + 1))
                for h in range(H):
                    for g in range(PAGES):
                        m_(pair[3][:, 1, h * DT:(h + 1) * DT], v_page[g][:, h * VD:(h + 1) * VD],
                           s_aT[:, g, h * DT:(h + 1) * DT], start=(g == 0), stop=False)
                    op = m_(pair[3][:, 1, h * DT:(h + 1) * DT], v_nat[0:NS, 4, h * VD:(h + 1) * VD],
                            s_aTn[:, h * DT:(h + 1) * DT], start=False, stop=True)
                op.then_inc(sa_o, 1)
            for h in range(H):
                if h >= 2:
                    pe.wait_ge(n_var["sub"], h - 1)
                sum_squares("sub", h, 1, h % 2)
            pe.wait_ge(n_var["sub"], H)
            for g in range(4):
                pe.wait_ge(pw_in, 16 * (g + 1))
                for o in range(2):
                    i = 2 * g + o
                    if i >= 2:
                        pe.wait_ge(pw_val, i - 1)
                    for k in range(2):
                        for hf in range(2):
                            op = m_(pair[i % 2][:, hf, 0:TH], pw[:, k, o * P:(o + 1) * P],
                                    pT[:, 2 * g + k, hf * TH:(hf + 1) * TH], start=(k == 0), stop=(k == 1))
                    op.then_inc(pw_mm, 1)
            pe.wait_ge(pw_ev, 8)
            for d in range(N_BR):
                g = G_BR + d
                pe.wait_ge(lo_done, g + 1)
                if d >= 2:
                    pe.wait_ge(merged_sum, d - 1)
                o = 0 if d % 2 == 0 else 2
                tile(w_hi[g % 2], w_lo[g % 2], o, range(8))
                tile(w_hi[g % 2], w_lo[g % 2], o + 1, range(8, 16)).then_inc(tile_done, 1)
            for t in range(N_OUT):
                g = G_OUT + t
                pe.wait_ge(lo_done, g + 1)
                if t >= 2:
                    pe.wait_ge(out_dve, 24 + t - 1)
                tile(w_hi[g % 2], w_lo[g % 2], t % 2,
                     wait=(lambda k: pe.wait_ge(mg_lo, k + 1)) if t == 0 else None).then_inc(tile_done, 1)
            pe.wait_ge(out_dve, 24 + N_OUT)
            sum_squares("n2", 0, KD, 0)
            pe.wait_ge(n_var["n2"], 1)

            def key_scores(t):
                pe.wait_ge(q_evd, t + 1)
                pe.wait_ge(sk_tev, t + 1)
                if t >= 2:
                    pe.wait_ge(sc_ev, 2 * (t - 1))
                for tb in range(TB):
                    w = tokens(tb)
                    op = m_(pair[2 + t % 2][0:w, tb // 4, (tb % 4) * P:(tb % 4 + 1) * P],
                            q_ev[:, t % 2, tb * P:tb * P + w], skT[:, t % 2, :], start=True, stop=True)
                op.then_inc(sc_mm, 1)

            for t in range(N_PQ):
                g = G_PQ + t
                pe.wait_ge(lo_done, g + 1)
                if t >= 2:
                    pe.wait_ge(q_evd, t - 1)
                tile(w_hi[g % 2], w_lo[g % 2], t % 2,
                     wait=(lambda k: pe.wait_ge(n_lo["n2"], k + 1)) if t == 0 else None).then_inc(tile_done, 1)
                pe.wait_ge(sk_in[t % 2], 16 * (t // 2 + 1))
                if t >= 2:
                    pe.wait_ge(sc_ev, 2 * (t - 1))
                tr(pair[2 + t % 2][:, 1, P:2 * P], sk_raw[:, t % 2, :]).then_inc(sk_tmm, 1)
                if t:
                    key_scores(t - 1)
            key_scores(N_PQ - 1)
            def turn_u(n, s, i, first=False):
                if i == 0:
                    pe.wait_ge(u_in[s], (n - s) * 8 + 16)
                if not first:
                    pe.wait_ge(u_lo, n * 2 + i)
                raw = w_raw[s][:, :, :].rearrange("p k c -> p (k c)")
                for k in range(8):
                    op = tr(pair[2][:, k // 4, (k % 4) * P:(k % 4 + 1) * P], raw[:, (8 * i + k) * P:(8 * i + k + 1) * P])
                op.then_inc(u_tmm, 1)

            def expert_tile(n, s, first=False, last=False):
                pe.wait_ge(u_lo, n * 2 + 2)
                if not first:
                    pe.wait_ge(a_gelu, n - 1)
                if not last:
                    turn_u(n + 1, 1 - s, 0)
                tile(w_hi[s], w_lo[s], s, range(8), ends=False)
                if not last:
                    turn_u(n + 1, 1 - s, 1)
                tile(w_hi[s], w_lo[s], s, range(8, KD), starts=False).then_inc(a_done, 1)

            def turn_selected(tb):
                w = tokens(tb)
                pe.wait_ge(sel_done, tb + 1)
                if tb:
                    pe.wait_ge(sel_tev, 3 * tb)
                else:
                    pe.wait_ge(sc_ev, 2 * N_PQ)
                for i in range(3):
                    op = tr(pair[3][:, 0, i * P:i * P + w], sel[0:w, i, :])
                op.then_inc(sel_tmm, 1)

            def gate_matrix(g, s, first=False):
                pe.wait_ge(oh_v, g + 1)
                if not first:
                    pe.wait_ge(gm_ev, g)
                for n in range(NTOK_G):
                    out = pair[3][:, n // 4, (n % 4) * PK:(n % 4 + 1) * PK]
                    m_(out, oi[s][:, n, :], jh[s][:, n, :], start=True, stop=False)
                    op = m_(out, oi[s][:, n, :], jl[s][:, n, :], start=False, stop=True)
                op.then_inc(gm_mm, 1)

            pe.wait_ge(sc_ev, 2 * N_PQ)
            pe.wait_ge(q_evd, N_PQ)
            turn_u(0, 0, 0, True)
            turn_u(0, 0, 1)
            for n in range(2):
                expert_tile(n, n, True)
            with pe.Fori(1, SEL_TILES // 2) as hh:
                for s in range(2):
                    expert_tile(hh * 2 + s, s)
            for tb in range(1, TB):
                for s in range(2):
                    expert_tile(tb * SEL_TILES + s, s)
                turn_selected(tb - 1)
                with pe.Fori(tb * SEL_TILES // 2 + 1, (tb + 1) * SEL_TILES // 2) as hh:
                    for s in range(2):
                        expert_tile(hh * 2 + s, s)
            turn_selected(TB - 1)
            pe.wait_ge(sel_tev, 3 * TB)
            for s in range(2):
                expert_tile(G_FIRST + s, s)
                gate_matrix(s, s, s == 0)
            with pe.Fori(1, N_G // 2) as gg:
                for s in range(2):
                    expert_tile(gg * 2 + (G_FIRST + s), s)
                    gate_matrix(gg * 2 + s, s)
            with pe.Fori(0, (N_U - G_FIRST - N_G) // 2 - 1) as hh:
                for s in range(2):
                    expert_tile(hh * 2 + (G_FIRST + N_G + s), s)
            expert_tile(N_U - 2, 0)
            expert_tile(N_U - 1, 1, last=True)
            pe.wait_ge(a_gelu, N_U)
            pe.wait_ge(gm_ev, N_G)

            def value_sums(n, i, at, first):
                pe.wait_ge(v_lod, n + 2)
                pe.wait_ge(wx_lod, n + 2)
                for d in range(KD):
                    if not first or d >= 4:
                        pe.wait_ge(acc_done, at + (d - 3))
                    c = slice(d * P, (d + 1) * P)
                    terms = [(w[m], x[m]) for m in (i, i + 1) for w, x in ((v_hi, wx_hi), (v_hi, wx_lo), (v_lo, wx_hi))]
                    for j, (w, x) in enumerate(terms):
                        for hf in range(2):
                            op = m_(pair[d % 4][:, hf, 0:TH], w[:, c], x[:, hf * TH:(hf + 1) * TH],
                                    start=(j == 0), stop=(j == 5))
                    op.then_inc(acc_ps, 1)

            value_sums(0, 0, 0, True)
            value_sums(2, 2, KD, False)
            with pe.Fori(1, N_U // 4) as q:
                value_sums(q * 4, 0, q * 32, False)
                value_sums(q * 4 + 2, 2, q * 32 + 16, False)
            pe.wait_ge(acc_done, N_U // 2 * KD)
            sum_squares("nf", 0, KD, 0)
            for k in range(KD):
                pe.wait_ge(n_val["nf"], k + 1)
                if k >= 2:
                    pe.wait_ge(yt_ev, 2 * (k - 1))
                for tb in range(TB):
                    w = tokens(tb)
                    op = tr(pair[2 + k % 2][0:w, tb // 4, (tb % 4) * P:(tb % 4 + 1) * P], tmp[:, k % 2, tb * P:tb * P + w])
                op.then_inc(yt_mm, 1)


_INS = ["x_prompt", "x_sample", "cache_k", "cache_v", "state_pool", "page_table", "norm1_g", "w_in", "b_gate",
        "lambda_q1", "lambda_k1", "lambda_q2", "lambda_k2", "subln_g", "w_attn_branch", "pool_w", "pool_scale",
        "w_pool_branch", "w_out", "norm2_g", "w_peer_q", "peer_sub_keys", "peer_u", "peer_v", "norm_f_g"]
_OUTS = [(1, SEQ, D), (DB, DT, D), (1, 1, SEQ, H, 2, HD), (1, 1, SEQ, H, VD), (1, 1, PSTATE, POOLW),
         (1, DB, DT, H, 2, HD), (1, DB, DT, H, VD), (1, DB, PSTATE, POOLW)]


def kernel(**inputs):
    import numpy as _np
    import concourse.bacc as _bacc
    from concourse import mybir as _mybir
    from concourse.bass_utils import run_bass_kernel_spmd as _run

    nc = _bacc.Bacc("TRN2", target_bir_lowering=False, num_devices=1)
    arrays, args = {}, []
    for name in _INS:
        a = _np.ascontiguousarray(inputs[name])
        arrays[f"in_{name}_dram"] = a
        args.append(nc.dram_tensor(f"in_{name}_dram", a.shape, _mybir.dt.from_np(a.dtype), kind="ExternalInput").ap())
    for i, shape in enumerate(_OUTS):
        args.append(nc.dram_tensor(f"out_{i}_dram", shape, _mybir.dt.float32, kind="ExternalOutput").ap())
    hybrid_step(nc, *args)
    r = _run(nc, [arrays], core_ids=[0])
    return tuple(r.results[0][f"out_{i}_dram"] for i in range(len(_OUTS)))
```

```python
import math

import numpy as np
import concourse.bass as bass
from concourse import mybir
from contextlib import ExitStack

F = mybir.dt.float32
R = mybir.dt.float32r
I32 = mybir.dt.int32
U32 = mybir.dt.uint32
ALU = mybir.AluOpType
ACT = mybir.ActivationFunctionType
AX = mybir.AxisListType

P = 128
D = 2048
KD = D // P
SEQ, DB, DT = 512, 8, 8
NS = DB * DT
T = SEQ + NS
TH = T // 2
TB = 5
H, HD, VD = 8, 64, 128
PAGES = 8
POOLW, PSTATE = 1024, 15
WINDOWS = (2, 4, 8, 16)
PH, PK, TOPK = 8, 128, 16
NEG = -1e30
SUBLN_EPS, NORM_EPS = 1e-5, 1e-6
LAM_INIT = 0.8 - 0.6 * math.exp(0.0)

T_P, T_Q, T_K, T_V, T_G = 0, 8, 16, 24, 32
N_IN = 64
QUARTERS = 4
N_BR, N_OUT, N_PQ = 16, 16, 16
G_BR = N_IN
G_OUT = G_BR + N_BR
G_PQ = G_OUT + N_OUT
G_U = G_PQ + N_PQ
N_W = G_U
N_U = PK
NTOK_G = 8
SEL_TILES = 6
G_FIRST = SEL_TILES * TB
N_G = T // NTOK_G
GB = 64


def tokens(tb):
    return P if tb < TB - 1 else NS


def hybrid_step(nc, x_prompt, x_sample, cache_k, cache_v, state_pool, page_table, norm1_g, w_in, b_gate,
                lambda_q1, lambda_k1, lambda_q2, lambda_k2, subln_g, w_attn_branch, pool_w, pool_scale,
                w_pool_branch, w_out, norm2_g, w_peer_q, peer_sub_keys, peer_u, peer_v, norm_f_g,
                y_prompt, y_sample, k_prompt, v_prompt, pool_prompt, k_sample, v_sample, pool_sample):
    ctx = ExitStack()
    with ctx:
        ctx.enter_context(nc.allow_non_contiguous_dma("columns of gains and biases"))
        BASE = (nc.sbuf_base + 63) // 64 * 64
        U = KD * T * 4
        A_ACT, A_MAIN = 0, 2 * U
        A_RING = 3 * U
        A_CONST = A_RING + 6 * KD * P * 4
        A_X = A_CONST + 4352

        class Region:
            def __init__(self, at, end):
                self.at, self.end = BASE + at, BASE + end

            def __call__(self, name, shape, dt=F):
                size = int(np.prod(shape[1:])) * 4
                t = nc.alloc_sbuf_tensor_at(name, shape, dt, offset=self.at)
                self.at += (size + 31) // 32 * 32
                assert self.at <= self.end, (name, self.at - self.end)
                return t

        END = nc.sbuf_usable_end // 32 * 32 - BASE
        r = Region(A_ACT, A_MAIN)
        act_hi = r("act_hi", [P, KD, T], R)
        act_lo = r("act_lo", [P, KD, T], R)
        main = Region(A_MAIN, A_RING)("main", [P, KD, T])
        r = Region(A_RING, A_CONST)
        w_raw = [r(f"w_raw{s}", [P, KD, P]) for s in range(2)]
        w_hi = [r(f"w_hi{s}", [P, KD, P], R) for s in range(2)]
        w_lo = [r(f"w_lo{s}", [P, KD, P], R) for s in range(2)]
        r = Region(A_CONST, A_X)
        ident = r("ident", [P, P])
        ones = r("ones", [P, P])
        mask_diag = r("mask_diag", [P, P])
        mask_new = r("mask_new", [P, 120])
        iota_f = r("iota_f", [P, P])
        iota_i = r("iota_i", [P, P], I32)
        g1c, g2c, gfc = r("g1c", [P, KD]), r("g2c", [P, KD]), r("gfc", [P, KD])
        subgc = r("subgc", [P, 1])
        subgc8 = r("subgc8", [P, 1])
        pscale_c = r("pscale_c", [P, 8])
        bgate_c = r("bgate_c", [P, 32])
        cinv = r("cinv", [P, 4, 16])
        page_i = r("page_i", [P, DB * PAGES], I32)
        page_rows = r("page_rows", [P, DB * PAGES], U32)
        col_i = r("col_i", [P, 4], I32)
        col_f = r("col_f", [P, 8])
        lam_v = r("lam_v", [P, 4])
        lam_c = r("lam_c", [P, 2])
        r = Region(A_X, END)
        tmp = r("tmp", [P, 2, T])
        rstd = r("rstd", [P, T])
        v_nat = r("v_nat", [P, TB, H * VD])
        pT = r("pT", [P, 8, T])
        k_stage = r("k_stage", [P, TB, P])
        r = Region(A_X, END)
        r("tmp_", [P, 3, T])
        x_in = r("x_in", [P, 2, D])
        r = Region(A_ACT, A_MAIN)
        lam_raw = r("lam_raw", [P, 5, HD])
        x_sq = [r(f"x_sq{s}", [P, KD, P]) for s in range(2)]
        SEG = PSTATE + DT
        EXL = PSTATE + SEQ + DB * SEG
        r = Region(A_X + 3 * T * 4, END)
        ex = [r(f"ex{s}", [P, 2, EXL]) for s in range(2)]
        stT = r("stT", [P, 8, DB * PSTATE])
        st_at = r.at - BASE
        st_rows = r("st_rows", [P, POOLW])
        pw = r("pw", [P, 2, P])
        assert r.at - BASE <= A_X + 3 * T * 4 + TB * H * VD * 4
        pool_rows = Region(st_at, END)("pool_rows", [NS, POOLW])
        A_ATT = A_X + 3 * T * 4 + TB * H * VD * 4
        r = Region(A_ATT, END)
        pp = [r(f"pp{s}", [P, 2, SEQ]) for s in range(2)]
        pa_buf = [r(f"pa{s}", [P, SEQ]) for s in range(2)]
        paT = [r(f"paT{s}", [P, 4, P]) for s in range(2)]
        p_stat = r("p_stat", [P, 2, 8])
        r = Region(A_ATT, END)
        qd = r("qd", [P, 8 * 144])
        kT_page = [r(f"kT_page{s}", [P, H, P]) for s in range(2)]
        sp_ = r("sp_", [P, 1024 + NS])
        s_aT = r("s_aT", [P, PAGES, NS])
        s_aTn = r("s_aTn", [NS, NS])
        s_stat = r("s_stat", [P, 8])
        k_new = Region(A_X + 2 * T * 4, END)("k_new", [P, H, NS])
        K_RING = V_RING = 4
        r = Region(A_MAIN + U // 2, A_RING)
        k_page = [r(f"k_page{s}", [P, H * P]) for s in range(K_RING)]
        r = Region(A_X + 3 * T * 4, A_ATT)
        v_page = [r(f"v_page{s}", [P, H * VD]) for s in range(V_RING)]
        r = Region(A_X, END)
        r("tmp__", [P, 3, T])
        back = r("back", [P, 4, T])
        mtmp = r("mtmp", [P, 2, T])
        head_col = r("head_col", [P, 2 * H])
        head_row = r("head_row", [H, H, P])
        r = Region(A_X, END)
        r("tmp___", [P, 2, T])
        iaT = r("iaT", [P, T])
        ibT = r("ibT", [P, T])
        gT = r("gT", [P, T])
        x2 = r.at - BASE
        sv = r("sv", [P, TB, 16, 16])
        si = r("si", [P, TB, 16, 16], U32)
        q_ev = r("q_ev", [P, 2, T])
        sk_raw = r("sk_raw", [P, 2, P])
        skT = r("skT", [P, 2, P])
        s_ev = r("s_ev", [P, 2, TB, PK])
        r = Region(x2, END)
        r("keep_sv", [P, 2, TB, 16, 16])
        si_f = r("si_f", [P, 16, 16])
        cand = r("cand", [P, PH, 256])
        ts = r("ts", [P, PH, TOPK])
        tp = r("tp", [P, PH, TOPK], U32)
        tpa = r("tpa", [P, 2, PH * TOPK], U32)
        tpf = r("tpf", [P, 2, PH * TOPK])
        oh = r("oh", [P, PH * TOPK, 16])
        sel = r("sel", [P, 3, PH * TOPK])
        ssum = r("ssum", [P, 2, PH])
        r = Region(x2, END)
        one_i = [r(f"one_i{s}", [P, NTOK_G, PK]) for s in range(2)]
        gate_j = [r(f"gate_j{s}", [P, NTOK_G, PK]) for s in range(2)]
        gmat = Region(A_MAIN, A_RING)("gmat", [P, PK, GB])
        r = Region(A_ACT, A_MAIN)
        v_hi = [r(f"v_hi{s}", [P, D], R) for s in range(4)]
        v_lo = [r(f"v_lo{s}", [P, D], R) for s in range(4)]
        r = Region(A_RING, A_CONST)
        v_raw = [r(f"v_raw{s}", [P, D]) for s in range(2)]
        wx_hi = [r(f"wx_hi{s}", [P, T], R) for s in range(4)]
        wx_lo = [r(f"wx_lo{s}", [P, T], R) for s in range(4)]
        r = Region(A_X, END)
        wx = [r(f"wx{s}", [P, T]) for s in range(2)]
        a_back = [r(f"a_back{s}", [P, T]) for s in range(2)]
        g_back = [r(f"g_back{s}", [P, T // GB, GB]) for s in range(2)]
        y_rows = Region(A_ACT, A_MAIN)("y_rows", [P, TB, D])

        pair = [ctx.enter_context(nc.psum_tensor(f"pair{i}", [P, 2, 512], F)) for i in range(4)]

        def halves(n):
            return pair[n][:, :, 0:TH]

        def as_halves(t):
            return t.rearrange("p (a t) -> p a t", a=2)

        xT_dram = nc.dram_tensor("xT_dram", [KD, P, T], F).ap()
        hT_dram = nc.dram_tensor("hT_dram", [KD, P, T], F).ap()
        pool_dram = nc.dram_tensor("pool_dram", [8, P, T], F).ap()
        gate_dram = nc.dram_tensor("gate_dram", [32, P, T], F).ap()
        gmat_dram = nc.dram_tensor("gmat_dram", [T // GB, P, PK, GB], F).ap()
        gelu_dram = nc.dram_tensor("gelu_dram", [N_U, P, T], F).ap()
        ck = cache_k.rearrange("l n s h c d -> (l n s) (h c d)")
        cv = cache_v.rearrange("l n s h e -> (l n s) (h e)")
        u_tiles = peer_u.rearrange("l (i j) d -> (l i) j d", j=PK)
        v_tiles = peer_v.rearrange("l (i j) d -> (l i) j d", j=PK)

        def sem(name):
            return ctx.enter_context(nc.semaphore(name))

        const_in = sem("const_in")
        pool_const = sem("pool_const")
        vec_const = sem("vec_const")
        lam_exp, lam_dots = sem("lam_exp"), sem("lam_dots")
        chain = sem("chain")
        x_loaded = [sem(f"x_loaded{s}") for s in range(2)]
        xt_mm, xt_ev_act, xt_ev_dve = sem("xt_mm"), sem("xt_ev_act"), sem("xt_ev_dve")
        xT_saved = sem("xT_saved")
        raw_in = [sem(f"raw_in{s}") for s in range(2)]
        hi_done, lo_done, tile_done = sem("hi_done"), sem("lo_done"), sem("tile_done")
        out_act, out_dve = sem("out_act"), sem("out_dve")
        nat_mm, nat_ev = sem("nat_mm"), sem("nat_ev")
        k_out, v_out = sem("k_out"), sem("v_out")
        gate_out = [sem(f"gate_out{s}") for s in range(2)]
        pool_in, pool_t_mm, pool_t_ev = sem("pool_in"), sem("pool_t_mm"), sem("pool_t_ev")
        pool_d = sem("pool_d")
        pool_out = sem("pool_out")
        pw_in, pw_mm, pw_val, pl_hi, pl_lo = (sem(n) for n in ("pw_in", "pw_mm", "pw_val", "pl_hi", "pl_lo"))
        pw_out = [sem(f"pw_out{s}") for s in range(2)]
        pl_in = [sem(f"pl_in{s}") for s in range(4)]
        st_out, kn_done = sem("st_out"), sem("kn_done")
        pa_s, pa_max, pa_exp, pa_a, pa_tmm, pa_tev, pa_o, pa_oev = (
            sem(n) for n in ("pa_s", "pa_max", "pa_exp", "pa_a", "pa_tmm", "pa_tev", "pa_o", "pa_oev"))
        kp_in = [sem(f"kp_in{s}") for s in range(K_RING)]
        vp_in = [sem(f"vp_in{s}") for s in range(V_RING)]
        sa_qd, sa_tmm, sa_tev_a, sa_tev_d, sa_s, sa_max, sa_exp, sa_p, sa_ptmm, sa_cp, sa_aT, sa_half, sa_o, sa_oev = (
            sem(n) for n in ("sa_qd", "sa_tmm", "sa_tev_a", "sa_tev_d", "sa_s", "sa_max", "sa_exp", "sa_p",
                             "sa_ptmm", "sa_cp", "sa_aT", "sa_half", "sa_o", "sa_oev"))
        NORMS = ("n1", "sub", "n2", "nf")
        sq_done, sq_used, n_var, n_sqrt, n_val, n_hi, n_lo = (
            {k: sem(f"{n}_{k}") for k in NORMS} for n in ("sq_done", "sq_used", "n_var", "n_sqrt", "n_val", "n_hi", "n_lo"))
        back_in = [sem(f"back_in{s}") for s in range(2)]
        merged_sum, mg_hi, mg_lo = sem("merged_sum"), sem("mg_hi"), sem("mg_lo")
        sk_in = [sem(f"sk_in{s}") for s in range(2)]
        sk_tmm, sk_tev, q_evd, sc_mm, sc_ev, top_done = (
            sem(n) for n in ("sk_tmm", "sk_tev", "q_evd", "sc_mm", "sc_ev", "top_done"))
        gx_in, gx_exp, sel_done, sel_tmm, sel_tev = (
            sem(n) for n in ("gx_in", "gx_exp", "sel_done", "sel_tmm", "sel_tev"))
        hT_saved, hT_back = sem("hT_saved"), sem("hT_back")
        oh_v, gm_mm, gm_ev, gm_out = (sem(n) for n in ("oh_v", "gm_mm", "gm_ev", "gm_out"))
        u_in = [sem(f"u_in{s}") for s in range(2)]
        u_tmm, u_hi, u_lo, a_done, a_gelu = (sem(n) for n in ("u_tmm", "u_hi", "u_lo", "a_done", "a_gelu"))
        a_out = [sem(f"a_out{s}") for s in range(2)]
        v_in = [sem(f"v_in{s}") for s in range(2)]
        ag_in = [sem(f"ag_in{s}") for s in range(2)]
        v_hid, v_lod, wx_val, wx_hid, wx_lod, acc_ps, acc_done = (
            sem(n) for n in ("v_hid", "v_lod", "wx_val", "wx_hid", "wx_lod", "acc_ps", "acc_done"))
        sub_sel, sub_inv, sub_all = sem("sub_sel"), sem("sub_inv"), sem("sub_all")
        sq_summed = sem("sq_summed")
        yt_mm, yt_ev, y_out = sem("yt_mm"), sem("yt_ev"), sem("y_out")

        block = ctx.enter_context(nc.Block())

        def col_view(a, n):
            return a.rearrange("l (k p) -> p (l k)", p=P) if len(a.shape) == 2 else a.rearrange("(k p) -> p k", p=P)

        def ring_source(g):
            if g < G_BR:
                g = 24 + g if g < T_Q else g - 8 if g < T_G else g
                return [(w_in[0, :, g * P:(g + 1) * P].rearrange("(k p) c -> p k c", p=P), 0, KD)]
            if g < G_OUT:
                c = slice((g - G_BR) * P, (g - G_BR + 1) * P)
                return [(w_attn_branch[0, :, c].rearrange("(k p) c -> p k c", p=P), 0, 8),
                        (w_pool_branch[0, :, c].rearrange("(k p) c -> p k c", p=P), 8, 8)]
            w, g = (w_out, g - G_OUT) if g < G_PQ else (w_peer_q, g - G_PQ)
            return [(w[0, :, g * P:(g + 1) * P].rearrange("(k p) c -> p k c", p=P), 0, KD)]

        def raw_count(g):
            n = sum(2 if G_BR <= m < G_OUT else 1 for m in range(g % 2, g + 1, 2))
            return 16 * n

        OUT_ACT = [t for t in range(N_IN) if T_Q <= t < T_K or t >= T_G]
        OUT_DVE = [t for t in range(N_IN) if t < T_Q or T_K <= t < T_G]

        def wait_w_in_out(eng, t):
            if t in OUT_ACT:
                eng.wait_ge(out_act, OUT_ACT.index(t) + 1)
            else:
                eng.wait_ge(out_dve, OUT_DVE.index(t) + 1)


        @block.sync
        def _(sp):
            for s in range(2):
                sp.dma_start(x_in[:, s, :], x_prompt[0, s * P:(s + 1) * P, :]).then_inc(x_loaded[s], 16)

            def load_tile(g):
                if g >= 2:
                    sp.wait_ge(lo_done, g - 1)
                for src, k0, n in ring_source(g):
                    sp.dma_start(w_raw[g % 2][:, k0:k0 + n, :], src).then_inc(raw_in[g % 2], 16)

            for i, v in enumerate((lambda_q1, lambda_k1, lambda_q2, lambda_k2)):
                sp.dma_start(lam_raw[:, i, :], v.broadcast_to([P, HD])).then_inc(const_in, 16)
            for dst, src in ((g1c, norm1_g), (g2c, norm2_g), (gfc, norm_f_g), (subgc, subln_g),
                             (pscale_c, pool_scale), (bgate_c, b_gate)):
                sp.dma_start(dst[:, :], col_view(src, P)).then_inc(const_in, 16)
            sp.dma_start(page_i[:, :], page_table.rearrange("b g -> (b g)").unsqueeze(0)
                         .broadcast_to([P, DB * PAGES])).then_inc(const_in, 16)
            for tb in range(2, TB):
                if tb == TB - 1:
                    load_tile(0)
                sp.wait_ge(xt_mm, tb - 1)
                src = x_prompt[0, tb * P:(tb + 1) * P, :] if tb < 4 else x_sample.rearrange("b t d -> (b t) d")
                sp.dma_start(x_in[0:tokens(tb), tb % 2, :], src).then_inc(x_loaded[tb % 2], 16)
            load_tile(1)
            for g in range(2, G_U):
                load_tile(g)
                if T_G <= g - 3 < N_IN:
                    n = g - 3 - T_G
                    sp.wait_ge(out_act, 8 + n + 1)
                    sp.dma_start(gate_dram[n], tmp[:, n % 2, :]).then_inc(gate_out[n % 2], 16)
            def load_u(n, s):
                src = u_tiles[:, n, :] if isinstance(n, int) else u_tiles[:, bass.ds(n, 1), :].rearrange("p a d -> p (a d)")
                sp.dma_start(w_raw[s][:, :, :].rearrange("p k c -> p (k c)"), src).then_inc(u_in[s], 16)

            def store_gelu(n, s):
                sp.wait_ge(a_gelu, n + 1)
                dst = gelu_dram[n] if isinstance(n, int) else gelu_dram[bass.ds(n, 1)].rearrange("a p t -> p (a t)")
                sp.dma_start(dst, tmp[:, s, :]).then_inc(a_out[s], 16)

            sp.wait_ge(lo_done, N_W)
            load_u(0, 0)
            load_u(1, 1)
            for n in range(2, 4):
                sp.wait_ge(u_tmm, 2 * (n - 1))
                load_u(n, n % 2)
                if n == 3:
                    store_gelu(0, 0)
            with sp.Fori(2, N_U // 2) as hh:
                for s in range(2):
                    sp.wait_ge(u_tmm, hh * 4 + 2 * (s - 1))
                    load_u(hh * 2 + s, s)
                    store_gelu(hh * 2 + (s - 3), 1 - s)
            def one(ap, m):
                return ap[:, m, :] if isinstance(m, int) else ap[:, bass.ds(m, 1), :].rearrange("p a d -> p (a d)")

            def load_v(n, s):
                sp.dma_start(v_raw[s][:, :], one(v_tiles, n)).then_inc(v_in[s], 16)

            def load_weights(n, s):
                sp.dma_start(a_back[s][:, :], one(gelu_dram.rearrange("j i t -> i j t"), n)).then_inc(ag_in[s], 16)
                g = gmat_dram.rearrange("b i j t -> i b j t")
                g = g[:, :, n, :] if isinstance(n, int) else g[:, :, bass.ds(n, 1), :].rearrange("i b j t -> i b (j t)")
                sp.dma_start(g_back[s][:, :, :], g).then_inc(ag_in[s], 16)

            sp.wait_ge(gm_out, 16 * (T // GB))
            sp.wait_ge(hT_saved, 16)
            sp.dma_start(main[:, :, :], hT_dram.rearrange("k p t -> p k t")).then_inc(hT_back, 16)
            store_gelu(N_U - 3, 1)
            for s in range(2):
                sp.wait_ge(a_out[s], 16)
                load_weights(s, s)
            for s in range(2):
                sp.wait_ge(u_tmm, 2 * (N_U - 1 + s))
                load_v(s, s)
                store_gelu(N_U - 2 + s, s)
            for s in range(2):
                sp.wait_ge(a_out[s], 16 * N_U // 2)
            for i in range(2, 4):
                sp.wait_ge(v_lod, i - 1)
                sp.wait_ge(wx_val, i - 1)
                load_v(i, i % 2)
                load_weights(i, i % 2)
            with sp.Fori(1, N_U // 4) as q:
                for i in range(4):
                    sp.wait_ge(v_lod, q * 4 + (i - 1))
                    sp.wait_ge(wx_val, q * 4 + (i - 1))
                    load_v(q * 4 + i, i % 2)
                    load_weights(q * 4 + i, i % 2)
            for n in range(4):
                c = slice(n * D // 4, (n + 1) * D // 4)
                sp.wait_ge(yt_ev, 2 * KD * (n + 1) // 4)
                sp.dma_start(y_prompt[0].rearrange("(b p) d -> p b d", p=P)[:, :, c], y_rows[:, 0:4, c]).then_inc(y_out, 16)
                sp.dma_start(y_sample.rearrange("b t d -> (b t) d")[:, c], y_rows[0:NS, 4, c]).then_inc(y_out, 16)
            sp.wait_ge(y_out, 4 * 32)

        @block.gpsimd
        def _(pool):
            g = nc.gpsimd
            g.memset(ident[:, :], 0.0).then_inc(pool_const, 1)
            g.memset(ones[:, :], 1.0).then_inc(pool_const, 1)
            g.memset(mask_diag[:, :], 0.0).then_inc(pool_const, 1)
            g.iota(iota_i[:, :], pattern=[[1, P]], base=0, channel_multiplier=0).then_inc(pool_const, 1)
            g.iota(col_i[:, 0:1], pattern=[[1, 1]], base=0, channel_multiplier=1).then_inc(pool_const, 1)
            pool.wait_ge(pool_const, 5)
            g.affine_select(out=ident[:, :], in_=ident[:, :], compare_op=ALU.not_equal, fill=1.0, base=0,
                            pattern=[[-1, P]], channel_multiplier=1).then_inc(pool_const, 1)
            g.affine_select(out=mask_diag[:, :], in_=mask_diag[:, :], compare_op=ALU.is_ge, fill=NEG, base=0,
                            pattern=[[-1, P]], channel_multiplier=1).then_inc(pool_const, 1)
            pool.wait_ge(vec_const, 1)
            g.affine_select(out=mask_new[:, :], in_=mask_new[:, :], compare_op=ALU.is_ge, fill=NEG, base=-56,
                            pattern=[[1, 120]], channel_multiplier=0).then_inc(pool_const, 1)
            pool.wait_ge(xt_ev_act, TB)
            pool.wait_ge(xt_ev_dve, TB)
            pool.dma_start(xT_dram.rearrange("k p t -> p k t"), main[:, :, :]).then_inc(xT_saved, 16)
            pool.wait_ge(xt_mm, TB)
            pool.dma_start(st_rows[0:DB * PSTATE, :], state_pool.rearrange("l b s c -> (l b s) c")).then_inc(pool_in, 16)
            pool.dma_start(pw[:, :, :], pool_w[0, 0].rearrange("(k p) d -> p k d", p=P)[:, :, 0:P]).then_inc(pw_in, 16)
            pool.dma_start(pool_sample[0, :, 0:PSTATE - DT, :], state_pool[0, :, DT:PSTATE, :]).then_inc(pool_out, 16)
            pool.wait_ge(pool_t_ev, 2)
            pool.dma_start(pool_prompt[0, 0], pool_rows[0:PSTATE, :]).then_inc(st_out, 16)
            pool.wait_ge(pool_t_ev, 3)
            for b in range(DB):
                pool.dma_start(pool_sample[0, b, PSTATE - DT:PSTATE, :],
                               pool_rows[b * DT:(b + 1) * DT, :]).then_inc(pool_out, 16)

            def store_k(h):
                pool.wait_ge(nat_ev, 2 * (h + 1))
                pool.dma_start(k_prompt[0, 0].rearrange("(b p) h c d -> p b h (c d)", p=P)[:, :, h, :],
                               k_stage[:, 0:4, :]).then_inc(k_out, 16)
                pool.dma_start(k_sample[0].rearrange("b t h c d -> (b t) h (c d)")[:, h, :],
                               k_stage[0:NS, 4, :]).then_inc(k_out, 16)

            for i in range(8):
                pool.wait_ge(pw_val, i + 1)
                pool.dma_start(pool_dram[i], tmp[:, i % 2, :]).then_inc(pw_out[i % 2], 16)
                if i < 7:
                    c = slice((i + 1) % 2 * P, (i + 1) % 2 * P + P)
                    pool.dma_start(pw[:, :, :], pool_w[0, (i + 1) // 2].rearrange("(k p) d -> p k d", p=P)[:, :, c]).then_inc(pw_in, 16)
                if i:
                    store_k(i - 1)
            store_k(7)
            pool.wait_ge(nat_ev, 32)
            pool.dma_start(v_prompt[0, 0].rearrange("(b p) h e -> p b (h e)", p=P), v_nat[:, 0:4, :]).then_inc(v_out, 16)
            pool.dma_start(v_sample[0].rearrange("b t h e -> (b t) (h e)"), v_nat[0:NS, 4, :]).then_inc(v_out, 16)

            def gather(dst, cache, n, s):
                pool.indirect_dma_start(out=dst[:, :], out_offset=None, in_=cache,
                                        in_offset=bass.IndirectOffsetOnAxis(ap=page_rows[:, n:n + 1], axis=0)
                                        ).then_inc(s, 16)

            pool.wait_ge(vec_const, 3)
            pool.wait_ge(pa_oev, 4 * H)
            pool.wait_ge(kn_done, 1)
            pool.wait_ge(v_out, 32)
            for n in range(K_RING):
                gather(k_page[n], ck, n, kp_in[n])
            for b in range(DB):
                for g_ in range(PAGES):
                    n = b * PAGES + g_
                    if g_ >= V_RING:
                        pool.wait_ge(sa_half, b + 1)
                    elif b:
                        pool.wait_ge(sa_o, b)
                    gather(v_page[g_ % V_RING], cv, n, vp_in[g_ % V_RING])
                    if g_ == V_RING - 1:
                        for m in range(b * PAGES + K_RING, min((b + 1) * PAGES + K_RING, DB * PAGES)):
                            pool.wait_ge(sa_tmm, m - K_RING + 1)
                            gather(k_page[m % K_RING], ck, m, kp_in[m % K_RING])
            pool.wait_ge(sa_o, DB)
            for i in range(8):
                if i < 2:
                    pool.wait_ge(pw_out[i], 16 * 4)
                if i >= 4:
                    pool.wait_ge(pl_lo, i - 3)
                pool.dma_start(back[:, i % 4, :], pool_dram[i]).then_inc(pl_in[i % 4], 16)
            for s in range(2):
                pool.wait_ge(gate_out[s], 16 * 16)
            pool.wait_ge(pl_lo, 8)
            for n in range(N_BR):
                if n >= 2:
                    pool.wait_ge(merged_sum, n - 1)
                pool.dma_start(back[:, n % 2, :], gate_dram[n]).then_inc(back_in[n % 2], 16)
                pool.dma_start(back[:, 2 + n % 2, :], gate_dram[KD + n]).then_inc(back_in[n % 2], 16)
            pool.wait_ge(xT_saved, 16)
            for m in range(N_OUT):
                if m < 2:
                    pool.wait_ge(merged_sum, N_BR - 1 + m)
                else:
                    pool.wait_ge(out_dve, 24 + m - 1)
                pool.dma_start(back[:, m % 2, :], xT_dram[m]).then_inc(back_in[m % 2], 16)
            pool.wait_ge(out_dve, 24 + N_OUT)
            for t in range(N_PQ):
                if t >= 2:
                    pool.wait_ge(sk_tmm, t - 1)
                pool.dma_start(sk_raw[:, t % 2, :], peer_sub_keys[0, t // 2, t % 2]).then_inc(sk_in[t % 2], 16)
            pool.wait_ge(n_lo["n2"], KD)
            pool.dma_start(hT_dram.rearrange("k p t -> p k t"), main[:, :, :]).then_inc(hT_saved, 16)
            for b in range(T // GB):
                pool.wait_ge(gm_ev, (b + 1) * (GB // NTOK_G))
                pool.dma_start(gmat_dram[b], gmat[:, :, :]).then_inc(gm_out, 16)
            def value_tile(n, i, first):
                s = i % 2
                if not first or i >= 2:
                    pool.wait_ge(wx_lod, n - 1)
                else:
                    pool.wait_ge(a_out[s], 16 * N_U // 2)
                pool.wait_ge(ag_in[s], 32 * (i // 2) + (n - i) * 16 + 32)
                g.tensor_tensor(wx[s][:, :], a_back[s][:, :], g_back[s][:, :, :].rearrange("p b t -> p (b t)"),
                                ALU.mult).then_inc(wx_val, 1)
                if first and i < 2:
                    return
                if first and i == 2:
                    pool.wait_ge(v_lod, 2)
                pool.wait_ge(v_hid, n + 1)
                g.tensor_tensor(v_lo[i][:, :], v_raw[s][:, :], v_hi[i][:, :].bitcast(F), ALU.subtract).then_inc(v_lod, 1)

            for i in range(4):
                value_tile(i, i, True)
            with pool.Fori(1, N_U // 4) as q:
                for i in range(4):
                    value_tile(q * 4 + i, i, False)
            pool.wait_ge(k_out, 32 * H)
            pool.wait_ge(v_out, 32)
            pool.wait_ge(pool_out, 16 * (1 + DB))
            pool.wait_ge(st_out, 16)

        @block.scalar
        def _(act):
            a = nc.scalar
            for tb in range(TB + 1):
                if tb < TB:
                    act.wait_ge(xt_mm, tb + 1)
                    w = tokens(tb)
                    a.copy(main[:, 0:8, tb * P:tb * P + w],
                           pair[2 * (tb % 2)][:, :, :].rearrange("p a (k t) -> p (a k) t", t=P)[:, :, 0:w]).then_inc(xt_ev_act, 1)
                if tb:
                    c = tb - 1
                    w = tokens(c)
                    act.wait_ge(xt_ev_act, c + 1)
                    act.wait_ge(xt_ev_dve, c + 1)
                    if c >= 2:
                        act.wait_ge(sq_summed, c - 1)
                    a.activation(x_sq[c % 2][:, :, 0:w], main[:, :, c * P:c * P + w], ACT.Square).then_inc(sq_done["n1"], 1)

            def split_hi(g):
                act.wait_ge(raw_in[g % 2], raw_count(g))
                if g >= 2:
                    act.wait_ge(tile_done, g - 1)
                a.copy(w_hi[g % 2][:, :, :], w_raw[g % 2][:, :, :]).then_inc(hi_done, 1)

            split_hi(0)
            split_hi(1)
            def root(key, n):
                act.wait_ge(n_var[key], n)
                a.activation(rstd[:, :], rstd[:, :], ACT.Sqrt).then_inc(n_sqrt[key], 1)

            def norm_hi(key, dst, c):
                act.wait_ge(n_val[key], c + 1)
                a.copy(act_hi[:, dst, :], tmp[:, c % 2, :]).then_inc(n_hi[key], 1)

            root("n1", 1)
            act.wait_ge(lam_dots, 1)
            for k in range(KD):
                norm_hi("n1", k, k)
            a.activation(lam_v[:, 2:4], lam_v[:, 0:2], ACT.Exp).then_inc(lam_exp, 1)

            def take_rows(i):
                act.wait_ge(nat_mm, i + 1)
                if i < 8:
                    if i:
                        act.wait_ge(k_out, 32 * i)
                    dst, c = k_stage, 0
                else:
                    if i == 8:
                        act.wait_ge(pw_mm, 8)
                        act.wait_ge(pool_out, 16 * (1 + DB))
                        act.wait_ge(st_out, 16)
                    dst, c = v_nat, (i - 8) * P
                a.copy(dst[:, 0:4, c:c + P], pair[2][:, 0, :].rearrange("p (b c) -> p b c", c=P)).then_inc(nat_ev, 1)
                a.copy(dst[0:NS, 4, c:c + P], pair[2][0:NS, 1, 0:P]).then_inc(nat_ev, 1)

            def take_pooled(i):
                act.wait_ge(pw_mm, i + 1)
                if i >= 2:
                    act.wait_ge(pw_out[i % 2], 16 * (i // 2))
                else:
                    act.wait_ge(n_lo["n1"], KD)
                a.mul(as_halves(tmp[:, i % 2, :]), halves(3), pscale_c[:, i:i + 1]).then_inc(pw_val, 1)

            for t in range(T_G):
                act.wait_ge(tile_done, t + 1)
                split_hi(t + 2)
                if T_Q <= t < T_K:
                    if t == T_Q:
                        act.wait_ge(xT_saved, 16)
                        act.wait_ge(n_lo["n1"], KD)
                    a.mul(as_halves(main[:, t - T_Q, :]), halves(t % 2), HD ** -0.5).then_inc(out_act, 1)
                if t == T_Q:
                    act.wait_ge(pool_t_mm, 1)
                    a.copy(stT[:, :, :], pair[2][:, :, :].rearrange("p a (k t) -> p (a k) t", t=P)[:, :, 0:DB * PSTATE]).then_inc(pool_t_ev, 1)
                    act.wait_ge(pool_t_mm, 2)
                    a.copy(pool_rows[0:PSTATE, :], pair[3][0:PSTATE, :, :].rearrange("p a c -> p (a c)")).then_inc(pool_t_ev, 1)
                if t == T_Q + 1:
                    act.wait_ge(pool_t_mm, 3)
                    act.wait_ge(st_out, 16)
                    a.copy(pool_rows[0:NS, :], pair[2][0:NS, :, :].rearrange("p a c -> p (a c)")).then_inc(pool_t_ev, 1)
                if T_K <= t < T_V:
                    take_pooled(t - T_K)
                if T_K <= t - 1:
                    take_rows(t - 1 - T_K)
            take_rows(15)

            def gate_tile(n, split=True):
                act.wait_ge(tile_done, T_G + n + 1)
                if n < 2:
                    act.wait_ge(nat_mm, 16)
                else:
                    act.wait_ge(gate_out[n % 2], 16 * (n // 2))
                a.activation(as_halves(tmp[:, n % 2, :]), halves(1), ACT.Sigmoid,
                             bias=bgate_c[:, n:n + 1]).then_inc(out_act, 1)
                if split:
                    split_hi(T_G + n + 2)

            def take_aT(u):
                nk = u % 4 + 1
                act.wait_ge(pa_tmm, u + 1)
                if u >= 2:
                    act.wait_ge(pa_o, u - 1)
                a.copy(paT[u % 2][:, 0:nk, :],
                       pair[2][:, 0, 0:nk * P].rearrange("p (k q) -> p k q", q=P)).then_inc(pa_tev, 1)

            for u in range(4 * H):
                nk = (u % 4 + 1) * P
                act.wait_ge(pa_max, u + 1)
                if u == 0:
                    act.wait_ge(k_out, 32 * H)
                if u >= 2:
                    act.wait_ge(pa_a, u - 1)
                for c in range(2):
                    a.activation(pp[u % 2][:, c, 0:nk], pair[3 * (u % 2)][:, c, 0:nk], ACT.Exp,
                                 bias=p_stat[:, u % 2, 2 + c:3 + c],
                                 accum_out=p_stat[:, u % 2, 4 + c:5 + c]).then_inc(pa_exp, 1)
                if u and u % 4 == 0:
                    gate_tile(u // 4 - 1, False)
                if u:
                    take_aT(u - 1)
                if u and u % 4 == 0:
                    split_hi(T_G + u // 4 + 1)
            take_aT(4 * H - 1)
            gate_tile(7)

            def take_page(n):
                act.wait_ge(sa_tmm, n + 1)
                if n == 0:
                    act.wait_ge(pa_oev, 4 * H)
                if n >= 2:
                    act.wait_ge(sa_s, (n - 2) + (n - 2) // PAGES + 1)
                a.copy(kT_page[n % 2][:, 0:4, :], pair[0][:, 0, :].rearrange("p (h k) -> p h k", k=P)).then_inc(sa_tev_a, 1)

            take_page(0)
            for b in range(DB):
                j = 8 + 3 * b
                for g in range(1, PAGES):
                    take_page(b * PAGES + g)
                    if g == 4:
                        gate_tile(j)
                gate_tile(j + 1)
                act.wait_ge(sa_max, b + 1)
                if b:
                    act.wait_ge(sa_ptmm, b)
                a.activation(sp_[:, 0:1024], pair[2][:, :, :].rearrange("p a k -> p (a k)"), ACT.Exp,
                             bias=s_stat[:, 3:4], accum_out=s_stat[:, 4:5]).then_inc(sa_exp, 1)
                a.activation(sp_[:, 1024:1024 + NS], pair[3][:, 0, 0:NS], ACT.Exp,
                             bias=s_stat[:, 3:4], accum_out=s_stat[:, 5:6]).then_inc(sa_exp, 1)
                act.wait_ge(sa_ptmm, b + 1)
                if b:
                    act.wait_ge(sa_o, b)
                for bank in range(2):
                    half = pair[0][:, bank, :].rearrange("p (g c t) -> p g c t", c=2, t=DT)
                    a.copy(s_aT[:, 4 * bank:4 * bank + 4, :].rearrange("p g (h t) -> p (g h) t", t=DT),
                           half[:, :, 0, :]).then_inc(sa_cp, 1)
                a.copy(s_aTn[:, :].rearrange("p (h t) -> p h t", t=DT),
                       pair[3][0:NS, 0, P:2 * P].rearrange("p (h c t) -> p h c t", c=2, t=DT)[:, :, 0, :]).then_inc(sa_cp, 1)
                if b + 1 < DB:
                    take_page((b + 1) * PAGES)
                gate_tile(j + 2)
            act.wait_ge(sa_oev, DB)
            act.wait_ge(sa_o, DB)
            for i in range(H):
                if i >= 2:
                    act.wait_ge(sq_used["sub"], i - 1)
                a.activation(mtmp[:, i % 2, :], main[:, i, :], ACT.Square).then_inc(sq_done["sub"], 1)
                act.wait_ge(pl_in[i % 4], 16 * (i // 4 + 1))
                a.copy(act_hi[:, 8 + i, :], back[:, i % 4, :]).then_inc(pl_hi, 1)
            act.wait_ge(n_var["sub"], 1)
            a.activation(rstd[0:H, :], rstd[0:H, :], ACT.Sqrt).then_inc(n_sqrt["sub"], 1)
            for h in range(H):
                norm_hi("sub", h, h)
            for d in range(N_BR):
                act.wait_ge(tile_done, G_BR + d + 1)
                split_hi(G_BR + d + 2)
            for k in range(KD):
                act.wait_ge(merged_sum, k + 1)
                a.copy(act_hi[:, k, :], main[:, k, :]).then_inc(mg_hi, 1)
            for m in range(N_OUT):
                act.wait_ge(tile_done, G_OUT + m + 1)
                split_hi(G_OUT + m + 2)
            root("n2", 1)
            for k in range(KD):
                norm_hi("n2", k, k)

            def take_scores(t):
                act.wait_ge(sc_mm, t + 1)
                if t >= 2:
                    act.wait_ge(top_done, t - 1)
                ps = pair[2 + t % 2]
                a.copy(s_ev[:, t % 2, 0:4, :], ps[:, 0, :].rearrange("p (b k) -> p b k", k=P)).then_inc(sc_ev, 1)
                a.copy(s_ev[0:NS, t % 2, 4, :], ps[0:NS, 1, 0:P]).then_inc(sc_ev, 1)

            for t in range(N_PQ):
                act.wait_ge(tile_done, G_PQ + t + 1)
                if G_PQ + t + 2 < G_U:
                    split_hi(G_PQ + t + 2)
                act.wait_ge(sk_tmm, t + 1)
                if t >= 2:
                    act.wait_ge(sc_mm, t - 1)
                a.copy(skT[:, t % 2, :], pair[2 + t % 2][:, 1, P:2 * P]).then_inc(sk_tev, 1)
                if t:
                    take_scores(t - 1)
            take_scores(N_PQ - 1)
            def u_high(n, s, first=False):
                for i in range(2):
                    act.wait_ge(u_tmm, n * 2 + (i + 1))
                    if i == 0 and not first:
                        act.wait_ge(a_done, n - 1)
                    a.copy(w_hi[s][:, 8 * i:8 * i + 8, :],
                           pair[2][:, :, :].rearrange("p a (k e) -> p (a k) e", e=P)).then_inc(u_hi, 1)

            def gelu(n, s, first=False):
                act.wait_ge(a_done, n + 1)
                if not first:
                    act.wait_ge(a_out[s], (n - s) * 8)
                a.activation(as_halves(tmp[:, s, :]), halves(s), ACT.Gelu).then_inc(a_gelu, 1)

            def gate_exp(tb):
                w = tokens(tb)
                act.wait_ge(gx_in, tb + 1)
                a.activation(sel[0:w, 2, :], sel[0:w, 2, :], ACT.Exp).then_inc(gx_exp, 1)

            def take_selected(tb):
                w = tokens(tb)
                act.wait_ge(sel_tmm, tb + 1)
                for i, dst in enumerate((iaT, ibT, gT)):
                    a.copy(dst[:, tb * P:tb * P + w], pair[3][:, 0, i * P:i * P + w]).then_inc(sel_tev, 1)

            def take_gates(g, t0):
                act.wait_ge(gm_mm, g + 1)
                at = slice(t0, t0 + NTOK_G) if isinstance(t0, int) else bass.ds(t0, NTOK_G)
                a.copy(gmat[:, :, at], pair[3][:, :, :].rearrange("p a (t j) -> p j (a t)", j=PK)).then_inc(gm_ev, 1)

            u_high(0, 0, True)
            for n in range(G_FIRST):
                u_high(n + 1, (n + 1) % 2, n == 0)
                tb, i = divmod(n, SEL_TILES)
                if i == SEL_TILES - 1:
                    gate_exp(tb)
                gelu(n, n % 2, n < 2)
                if tb and i == 1:
                    take_selected(tb - 1)
            take_selected(TB - 1)
            act.wait_ge(hT_saved, 16)
            def gate_block(blk, first=False):
                for i in range(GB // NTOK_G):
                    n = blk * 8 + (G_FIRST + i)
                    u_high(n + 1, (i + 1) % 2)
                    gelu(n, i % 2)
                    if i == 0 and not first:
                        act.wait_ge(gm_out, blk * 16)
                    take_gates(blk * 8 + i, i * NTOK_G)

            gate_block(0, True)
            with act.Fori(1, T // GB) as blk:
                gate_block(blk)
            with act.Fori(0, (N_U - G_FIRST - N_G) // 2 - 1) as hh:
                for s in range(2):
                    n = hh * 2 + (G_FIRST + N_G + s)
                    u_high(n + 1, 1 - s)
                    gelu(n, s)
            u_high(N_U - 1, 1)
            gelu(N_U - 2, 0)
            gelu(N_U - 1, 1)

            def value_high(n, i, first):
                s = i % 2
                act.wait_ge(v_in[s], 16 * (i // 2) + (n - i) * 8 + 16)
                if not first:
                    act.wait_ge(acc_ps, (n - i) * 8 + 16 * (i // 2) - 16)
                a.copy(v_hi[i][:, :], v_raw[s][:, :]).then_inc(v_hid, 1)
                act.wait_ge(wx_val, n + 1)
                a.copy(wx_hi[i][:, :], wx[s][:, :]).then_inc(wx_hid, 1)

            for i in range(4):
                value_high(i, i, True)
            with act.Fori(1, N_U // 4) as q:
                for i in range(4):
                    value_high(q * 4 + i, i, False)
            act.wait_ge(wx_val, N_U)
            for k in range(KD):
                act.wait_ge(acc_done, (N_U // 2 - 1) * KD + k + 1)
                if k >= 2:
                    act.wait_ge(sq_summed, TB + k - 1)
                a.activation(a_back[k % 2][:, :], main[:, k, :], ACT.Square).then_inc(sq_done["nf"], 1)
            root("nf", 1)
            for k in range(KD):
                act.wait_ge(yt_mm, k + 1)
                ps = pair[2 + k % 2]
                c = slice(k * P, (k + 1) * P)
                a.copy(y_rows[:, 0:4, c], ps[:, 0, :].rearrange("p (b c) -> p b c", c=P)).then_inc(yt_ev, 1)
                a.copy(y_rows[0:NS, 4, c], ps[0:NS, 1, 0:P]).then_inc(yt_ev, 1)

        @block.vector
        def _(dve):
            v = nc.vector
            count = [0]

            def link(*ops):
                for op in ops:
                    op.then_inc(chain, 1)
                count[0] += len(ops)
                dve.wait_ge(chain, count[0])

            dve.wait_ge(pool_const, 7)
            link(v.tensor_copy(iota_f[:, :], iota_i[:, :]),
                 v.tensor_copy(col_f[:, 0:1], col_i[:, 0:1]),
                 v.tensor_single_scalar(col_i[:, 1:2], col_i[:, 0:1], 7, ALU.bitwise_and),
                 v.tensor_single_scalar(col_i[:, 2:3], col_i[:, 0:1], 3, ALU.logical_shift_right))
            link(v.tensor_single_scalar(col_i[:, 3:4], col_i[:, 2:3], 1, ALU.bitwise_and))
            link(v.tensor_copy(col_f[:, 1:3], col_i[:, 1:4:2]))
            link(v.tensor_scalar_add(col_f[:, 3:4], col_f[:, 1:2], 56.0))
            v.tensor_scalar(mask_new[:, :], iota_f[:, 0:120], col_f[:, 3:4], NEG, ALU.is_gt, ALU.mult).then_inc(vec_const, 1)
            for g, w in enumerate(WINDOWS):
                link(v.tensor_scalar(cinv[:, g, :], iota_f[:, 0:16], 1.0, float(w), ALU.add, ALU.min))
            link(v.reciprocal(cinv[:, :, :], cinv[:, :, :]))
            for tb in range(TB + 1):
                if tb < TB:
                    dve.wait_ge(xt_mm, tb + 1)
                    w = tokens(tb)
                    v.tensor_copy(main[:, 8:16, tb * P:tb * P + w],
                                  pair[2 * (tb % 2) + 1][:, :, :].rearrange("p a (k t) -> p (a k) t", t=P)[:, :, 0:w]).then_inc(xt_ev_dve, 1)
                if tb:
                    c = tb - 1
                    w = tokens(c)
                    dve.wait_ge(sq_done["n1"], c + 1)
                    v.tensor_reduce(out=tmp[:, 0, c * P:c * P + w], in_=x_sq[c % 2][:, :, 0:w].rearrange("p k t -> p t k"),
                                    axis=AX.X, op=ALU.add).then_inc(sq_summed, 1)

            dve.wait_ge(const_in, 16 * 11)
            v.tensor_scalar(page_rows[:, :], page_i[:, :], float(P), col_f[:, 0:1], ALU.mult, ALU.add).then_inc(vec_const, 1)
            v.tensor_scalar_mul(subgc8[:, :], subgc[:, :], 1.0 - LAM_INIT).then_inc(vec_const, 1)
            for i in range(2):
                op = v.tensor_tensor_reduce(out=lam_raw[:, 4, :], in0=lam_raw[:, 2 * i, :], in1=lam_raw[:, 2 * i + 1, :],
                                            scale=1.0, scalar=0.0, op0=ALU.mult, op1=ALU.add, accum_out=lam_v[:, i:i + 1])
                if i:
                    op.then_inc(lam_dots, 1)
                else:
                    link(op)

            def split_lo(g):
                dve.wait_ge(hi_done, g + 1)
                v.tensor_sub(w_lo[g % 2][:, :, :], w_raw[g % 2][:, :, :], w_hi[g % 2][:, :, :].bitcast(F)).then_inc(lo_done, 1)

            def variance(key, n, ps, width, eps):
                dve.wait_ge(sq_used[key], n)
                v.tensor_scalar(as_halves(rstd[:, :]), halves(ps), 1.0 / width, eps, ALU.mult, ALU.add).then_inc(n_var[key], 1)

            split_lo(0)
            variance("n1", 1, 0, D, NORM_EPS)
            def inverse(key, n):
                dve.wait_ge(n_sqrt[key], n)
                link(v.reciprocal(rstd[:, :], rstd[:, :]))

            def norm_value(key, src, gain, c):
                if c >= 2:
                    dve.wait_ge(n_lo[key], c - 1)
                v.scalar_tensor_tensor(tmp[:, c % 2, :], main[:, src, :], gain, rstd[:, :], ALU.mult, ALU.mult).then_inc(n_val[key], 1)

            def norm_lo(key, dst, c):
                dve.wait_ge(n_hi[key], c + 1)
                v.tensor_sub(act_lo[:, dst, :], tmp[:, c % 2, :], act_hi[:, dst, :].bitcast(F)).then_inc(n_lo[key], 1)

            def norm_all(key, gains):
                inverse(key, 1)
                for k in range(KD):
                    norm_value(key, k, gains[:, k:k + 1], k)
                    if k:
                        norm_lo(key, k - 1, k - 1)
                norm_lo(key, KD - 1, KD - 1)

            split_lo(1)
            norm_all("n1", g1c)
            dve.wait_ge(lam_exp, 1)
            link(v.tensor_scalar_add(lam_c[:, 0:1], lam_v[:, 2:3], LAM_INIT))
            link(v.tensor_sub(lam_c[:, 0:1], lam_c[:, 0:1], lam_v[:, 3:4]))
            link(v.tensor_scalar_mul(lam_c[:, 1:2], lam_c[:, 0:1], -1.0),
                 v.tensor_scalar_add(col_f[:, 4:5], lam_c[:, 0:1], 1.0))
            link(v.tensor_mul(col_f[:, 5:6], col_f[:, 4:5], col_f[:, 2:3]))
            link(v.tensor_scalar(col_f[:, 6:7], col_f[:, 5:6], -1.0, 1.0, ALU.mult, ALU.add))
            L0 = PSTATE + SEQ

            def new(b):
                return b[:, :, L0:].rearrange("p k (s x) -> p k s x", x=SEG)

            def window_sums(g, w):
                e, f = ex
                p2 = pT[:, 2 * g:2 * g + 2, :]
                ops = [v.memset(e[:, :, 0:PSTATE], 0.0), v.tensor_copy(e[:, :, PSTATE:L0], p2[:, :, 0:SEQ])]
                for k in range(2):
                    ops += [v.tensor_copy(new(e)[:, k, :, 0:PSTATE],
                                          stT[:, 2 * g + k, :].rearrange("p (s x) -> p s x", x=PSTATE)),
                            v.tensor_copy(new(e)[:, k, :, PSTATE:], p2[:, k, SEQ:].rearrange("p (s x) -> p s x", x=DT))]
                link(*ops)
                step = 1
                while step < w:
                    link(v.tensor_copy(f[:, :, 0:step], e[:, :, 0:step]),
                         v.tensor_add(f[:, :, step:], e[:, :, step:], e[:, :, 0:EXL - step]))
                    e, f = f, e
                    step *= 2

            def window_means(g, w):
                e, f = ex if g % 2 else ex[::-1]
                p2 = pT[:, 2 * g:2 * g + 2, :]
                link(*[v.tensor_mul(f[:, k, 0:16], e[:, k, PSTATE:PSTATE + 16], cinv[:, g, :]) for k in range(2)])
                link(*[v.tensor_sub(f[:, k, 0:16], f[:, k, 0:16], p2[:, k, 0:16]) for k in range(2)])
                for k in range(2):
                    v.scalar_tensor_tensor(p2[:, k, SEQ:].rearrange("p (s x) -> p s x", x=DT), new(e)[:, k, :, PSTATE:],
                                           1.0 / w, p2[:, k, SEQ:].rearrange("p (s x) -> p s x", x=DT), ALU.mult, ALU.subtract)
                link(*[v.scalar_tensor_tensor(p2[:, k, 0:SEQ], e[:, k, PSTATE:L0], 1.0 / w, p2[:, k, 0:SEQ],
                                              ALU.mult, ALU.subtract) for k in range(2)])
                v.tensor_copy(p2[:, :, 0:16], f[:, :, 0:16]).then_inc(pool_d, 1)

            for t in range(T_G):
                dve.wait_ge(tile_done, t + 1)
                split_lo(t + 2)
                if t < T_Q:
                    v.tensor_copy(as_halves(pT[:, t, :]), halves(t % 2)).then_inc(out_dve, 1)
                elif T_K <= t < T_V:
                    v.tensor_copy(as_halves(main[:, 8 + t - T_K, :]), halves(t % 2)).then_inc(out_dve, 1)
                elif T_V <= t:
                    i = t - T_V
                    if i >= 2:
                        dve.wait_ge(nat_mm, 8 + i - 1)
                    else:
                        dve.wait_ge(pw_out[i], 16 * 4)
                    v.tensor_copy(as_halves(tmp[:, i % 2, :]), halves(t % 2)).then_inc(out_dve, 1)
                if t == T_Q + 2:
                    dve.wait_ge(out_dve, 8)
                    dve.wait_ge(pool_t_ev, 3)
                if T_Q + 2 <= t < T_Q + 10:
                    g, part = divmod(t - T_Q - 2, 2)
                    (window_means if part else window_sums)(g, WINDOWS[g])
                    if part:
                        dve.wait_ge(pool_d, g + 1)

            def gate_tile(n):
                dve.wait_ge(tile_done, T_G + n + 1)
                split_lo(T_G + n + 2)

            def gate_tile_part(n, i):
                g = T_G + n + 2
                ks = slice((0, 5, 10)[i], (5, 10, KD)[i])
                dve.wait_ge(hi_done, g + 1)
                op = v.tensor_sub(w_lo[g % 2][:, ks, :], w_raw[g % 2][:, ks, :], w_hi[g % 2][:, ks, :].bitcast(F))
                if i == 2:
                    op.then_inc(lo_done, 1)

            dve.wait_ge(k_out, 32 * H)
            dve.wait_ge(pw_mm, 8)

            def row_max(u):
                nk = (u % 4 + 1) * P
                dve.wait_ge(pa_s, u + 1)
                ps, st = pair[3 * (u % 2)], p_stat[:, u % 2, :]
                link(*[v.tensor_add(ps[:, c, nk - P:nk], ps[:, c, nk - P:nk], mask_diag[:, :]) for c in range(2)])
                if u >= 2:
                    dve.wait_ge(pa_a, u - 1)
                link(v.tensor_reduce(out=st[:, 0:2], in_=ps[:, :, 0:nk], axis=AX.X, op=ALU.max))
                v.tensor_scalar_mul(st[:, 2:4], st[:, 0:2], -1.0).then_inc(pa_max, 1)

            def weights(u):
                nk = (u % 4 + 1) * P
                s, st = pp[u % 2], p_stat[:, u % 2, :]
                dve.wait_ge(pa_exp, 2 * (u + 1))
                link(v.reciprocal(st[:, 6:8], st[:, 4:6]))
                if u >= 2:
                    dve.wait_ge(pa_tmm, u - 1)
                link(v.tensor_scalar_mul(pa_buf[u % 2][:, 0:nk], s[:, 0, 0:nk], st[:, 6:7]),
                     v.tensor_mul(st[:, 7:8], st[:, 7:8], lam_c[:, 1:2]))
                v.scalar_tensor_tensor(pa_buf[u % 2][:, 0:nk], s[:, 1, 0:nk], st[:, 7:8], pa_buf[u % 2][:, 0:nk],
                                       ALU.mult, ALU.add).then_inc(pa_a, 1)

            def take_o(u):
                h, qb = divmod(u, 4)
                dve.wait_ge(pa_o, u + 1)
                v.tensor_copy(main[:, h, qb * P:(qb + 1) * P], pair[2][:, 1, 0:P]).then_inc(pa_oev, 1)

            for u in range(4 * H + 2):
                if u < 4 * H:
                    row_max(u)
                if 1 <= u <= 4 * H:
                    weights(u - 1)
                if u >= 2:
                    take_o(u - 2)
                if 4 <= u < 4 * H and u % 4 < 3:
                    gate_tile_part(u // 4 - 1, u % 4)
            dve.wait_ge(pa_oev, 4 * H)
            v.tensor_copy(k_new[:, :, :], main[:, 8:16, SEQ:T]).then_inc(kn_done, 1)
            gate_tile(7)

            dve.wait_ge(pool_const, 8)
            link(v.memset(qd[:, :], 0.0))

            def queries(b):
                for c in range(2):
                    r_ = slice(c * HD, (c + 1) * HD)
                    v.tensor_copy(qd[r_, :].rearrange("p (h x) -> p h x", x=144)[:, :, c * DT:(c + 1) * DT],
                                  main[r_, 0:H, SEQ + b * DT:SEQ + (b + 1) * DT]).then_inc(sa_qd, 1)

            def take_page(n):
                dve.wait_ge(sa_tmm, n + 1)
                if n >= 2:
                    dve.wait_ge(sa_s, (n - 2) + (n - 2) // PAGES + 1)
                v.tensor_copy(kT_page[n % 2][:, 4:8, :], pair[0][:, 1, :].rearrange("p (h k) -> p h k", k=P)).then_inc(sa_tev_d, 1)

            queries(0)
            take_page(0)
            for b in range(DB):
                j = 8 + 3 * b
                for g in range(1, PAGES):
                    take_page(b * PAGES + g)
                    if g == 4:
                        gate_tile(j)
                dve.wait_ge(sa_s, (PAGES + 1) * (b + 1))
                if b:
                    dve.wait_ge(sa_exp, 2 * b)
                link(v.tensor_add(pair[3][:, 0, 0:NS], pair[3][:, 0, 0:NS], mask_new[:, 56 - 8 * b:56 - 8 * b + NS]))
                if b:
                    dve.wait_ge(sa_p, b)
                link(v.tensor_reduce(out=s_stat[:, 0:1], in_=pair[2][:, :, :], axis=AX.XY, op=ALU.max),
                     v.tensor_reduce(out=s_stat[:, 1:2], in_=pair[3][:, 0, 0:NS], axis=AX.X, op=ALU.max))
                link(v.tensor_max(s_stat[:, 2:3], s_stat[:, 0:1], s_stat[:, 1:2]))
                v.tensor_scalar_mul(s_stat[:, 3:4], s_stat[:, 2:3], -1.0).then_inc(sa_max, 1)
                if b + 1 < DB:
                    queries(b + 1)
                gate_tile(j + 1)
                dve.wait_ge(sa_exp, 2 * (b + 1))
                link(v.tensor_add(s_stat[:, 6:7], s_stat[:, 4:5], s_stat[:, 5:6]))
                link(v.reciprocal(s_stat[:, 6:7], s_stat[:, 6:7]))
                link(v.tensor_mul(s_stat[:, 7:8], s_stat[:, 6:7], col_f[:, 6:7]))
                v.tensor_scalar_mul(sp_[:, :], sp_[:, :], s_stat[:, 7:8]).then_inc(sa_p, 1)
                dve.wait_ge(sa_cp, 3 * (b + 1))
                for bank in range(2):
                    half = pair[0][:, bank, :].rearrange("p (g c t) -> p g c t", c=2, t=DT)
                    o = s_aT[:, 4 * bank:4 * bank + 4, :].rearrange("p g (h t) -> p (g h) t", t=DT)
                    v.tensor_add(o, half[:, :, 1, :], o).then_inc(sa_aT, 1)
                o = s_aTn[:, :].rearrange("p (h t) -> p h t", t=DT)
                v.tensor_add(o, pair[3][0:NS, 0, P:2 * P].rearrange("p (h c t) -> p h c t", c=2, t=DT)[:, :, 1, :], o).then_inc(sa_aT, 1)
                if b + 1 < DB:
                    take_page((b + 1) * PAGES)
                gate_tile(j + 2)
                dve.wait_ge(sa_o, b + 1)
                v.tensor_copy(main[:, 0:H, SEQ + b * DT:SEQ + (b + 1) * DT],
                              pair[3][:, 1, 0:NS].rearrange("p (h t) -> p h t", t=DT)).then_inc(sa_oev, 1)
            dve.wait_ge(sa_oev, DB)
            for s_ in range(2):
                dve.wait_ge(gate_out[s_], 16 * (N_IN - T_G) // 2)
            v.memset(head_col[:, 0:H], 0.0).then_inc(sub_sel, 1)
            v.memset(head_col[:, H + 1:], 0.0).then_inc(sub_sel, 1)
            v.memset(head_col[:, H:H + 1], 1.0).then_inc(sub_sel, 1)
            v.tensor_copy(head_row[:, :, :], ident[0:H, 0:H].unsqueeze(2).broadcast_to([H, H, P])).then_inc(sub_sel, 1)
            for i in range(8):
                dve.wait_ge(pl_hi, i + 1)
                v.tensor_sub(act_lo[:, 8 + i, :], back[:, i % 4, :], act_hi[:, 8 + i, :].bitcast(F)).then_inc(pl_lo, 1)
            dve.wait_ge(sq_used["sub"], H)
            v.tensor_scalar(as_halves(rstd[0:H, :]), pair[0][0:H, :, 0:TH], 1.0 / VD, SUBLN_EPS,
                            ALU.mult, ALU.add).then_inc(n_var["sub"], 1)
            dve.wait_ge(n_sqrt["sub"], 1)
            v.reciprocal(rstd[0:H, :], rstd[0:H, :]).then_inc(sub_inv, 1)
            for h in range(H + 1):
                if h < H:
                    dve.wait_ge(sub_all, h + 1)
                    if h >= 2:
                        dve.wait_ge(n_lo["sub"], h - 1)
                    v.scalar_tensor_tensor(as_halves(tmp[:, h % 2, :]), as_halves(main[:, h, :]), subgc8[:, :],
                                           halves(2 + h % 2), ALU.mult, ALU.mult).then_inc(n_val["sub"], 1)
                if h:
                    norm_lo("sub", h - 1, h - 1)
            dve.wait_ge(pl_lo, 8)
            for d in range(N_BR):
                dve.wait_ge(tile_done, G_BR + d + 1)
                split_lo(G_BR + d + 2)
                dve.wait_ge(back_in[d % 2], 32 * (d // 2 + 1))
                if d:
                    dve.wait_ge(merged_sum, d)
                pa_, pb_ = (0, 1) if d % 2 == 0 else (2, 3)
                link(v.tensor_mul(as_halves(mtmp[:, 0, :]), halves(pa_), as_halves(back[:, d % 2, :])),
                     v.tensor_mul(as_halves(mtmp[:, 1, :]), halves(pb_), as_halves(back[:, 2 + d % 2, :])))
                v.tensor_add(main[:, d, :], mtmp[:, 0, :], mtmp[:, 1, :]).then_inc(merged_sum, 1)
            for k in range(KD):
                dve.wait_ge(mg_hi, k + 1)
                v.tensor_sub(act_lo[:, k, :], main[:, k, :], act_hi[:, k, :].bitcast(F)).then_inc(mg_lo, 1)
            dve.wait_ge(mg_lo, KD)
            for m in range(N_OUT):
                dve.wait_ge(tile_done, G_OUT + m + 1)
                split_lo(G_OUT + m + 2)
                dve.wait_ge(back_in[m % 2], 32 * (N_BR // 2) + 16 * (m // 2 + 1))
                v.tensor_add(as_halves(main[:, m, :]), halves(m % 2), as_halves(back[:, m % 2, :])).then_inc(out_dve, 1)
                dve.wait_ge(out_dve, 24 + m + 1)
                op = v.tensor_mul(mtmp[:, 1 if m == 0 else 0, :], main[:, m, :], main[:, m, :])
                if m:
                    link(op)
                    op = v.tensor_add(mtmp[:, 1, :], mtmp[:, 1, :], mtmp[:, 0, :])
                if m < N_OUT - 1:
                    link(op)
                else:
                    op.then_inc(sq_done["n2"], 1)
            variance("n2", 1, 0, D, NORM_EPS)
            norm_all("n2", g2c)

            def best(t):
                dve.wait_ge(sc_ev, 2 * (t + 1))
                s = t % 2
                rows = [(tb, tokens(tb)) for tb in range(TB)]
                link(*[v.max(out=sv[0:w, tb, t, 0:8], in_=s_ev[0:w, s, tb, :]) for tb, w in rows])
                link(*[v.max_index(out=si[0:w, tb, t, 0:8], in_max=sv[0:w, tb, t, 0:8], in_values=s_ev[0:w, s, tb, :]) for tb, w in rows])
                link(*[v.match_replace(out=s_ev[0:w, s, tb, :], in_to_replace=sv[0:w, tb, t, 0:8],
                                       in_values=s_ev[0:w, s, tb, :], imm_value=-3e38) for tb, w in rows])
                link(*[v.max(out=sv[0:w, tb, t, 8:16], in_=s_ev[0:w, s, tb, :]) for tb, w in rows])
                for tb, w in rows:
                    op = v.max_index(out=si[0:w, tb, t, 8:16], in_max=sv[0:w, tb, t, 8:16], in_values=s_ev[0:w, s, tb, :])
                op.then_inc(top_done, 1)

            for t in range(N_PQ):
                dve.wait_ge(tile_done, G_PQ + t + 1)
                if G_PQ + t + 2 < G_U:
                    split_lo(G_PQ + t + 2)
                if t >= 2:
                    dve.wait_ge(sc_mm, t - 1)
                v.tensor_copy(as_halves(q_ev[:, t % 2, :]), halves(t % 2)).then_inc(q_evd, 1)
                if 0 < t < N_PQ - 1:
                    best(t - 1)
            def u_low(n, s, halves_=range(2)):
                for i in halves_:
                    dve.wait_ge(u_hi, n * 2 + (i + 1))
                    v.tensor_sub(w_lo[s][:, 8 * i:8 * i + 8, :],
                                 pair[2][:, :, :].rearrange("p a (k e) -> p (a k) e", e=P),
                                 w_hi[s][:, 8 * i:8 * i + 8, :].bitcast(F)).then_inc(u_lo, 1)

            def sel_sums(tb, w):
                svh = sv[0:w, tb, :, :].rearrange("p (h c) a -> p h c a", c=2)
                full = [w, PH, TOPK, TOPK]
                link(v.tensor_copy(si_f[0:w], si[0:w, tb, :, :]),
                     v.tensor_tensor(cand[0:w].rearrange("p h (a b) -> p h a b", b=TOPK),
                                     svh[:, :, 0, :].unsqueeze(3).broadcast_to(full),
                                     svh[:, :, 1, :].unsqueeze(2).broadcast_to(full), ALU.add))

            def sel_max(tb, w, at):
                link(*[v.max(out=ts[0:w, h, at:at + 8], in_=cand[0:w, h, :]) for h in range(PH)])

            def sel_place(tb, w, at):
                link(*[v.max_index(out=tp[0:w, h, at:at + 8], in_max=ts[0:w, h, at:at + 8], in_values=cand[0:w, h, :])
                       for h in range(PH)])

            def sel_strike(tb, w):
                link(*[v.match_replace(out=cand[0:w, h, :], in_to_replace=ts[0:w, h, 0:8], in_values=cand[0:w, h, :],
                                       imm_value=-3e38) for h in range(PH)])

            def sel_split(tb, w):
                tpw = tp[0:w].rearrange("p h k -> p (h k)")
                link(v.tensor_single_scalar(tpa[0:w, 0, :], tpw, 4, ALU.logical_shift_right),
                     v.tensor_single_scalar(tpa[0:w, 1, :], tpw, 15, ALU.bitwise_and))
                link(v.tensor_copy(tpf[0:w], tpa[0:w]))

            def sel_mark(tb, w, c):
                link(v.tensor_tensor(oh[0:w], tpf[0:w, c, :].unsqueeze(2).broadcast_to([w, PH * TOPK, 16]),
                                     iota_f[0:w, 0:16].unsqueeze(1).broadcast_to([w, PH * TOPK, 16]), ALU.is_equal))

            def sel_key(tb, w, c):
                full = [w, PH, TOPK, TOPK]
                ohk = oh[0:w].rearrange("p (h k) a -> p h k a", k=TOPK)
                sih = si_f[0:w].rearrange("p (h c) a -> p h c a", c=2)[:, :, c, :]
                link(v.tensor_tensor(ohk, ohk, sih.unsqueeze(2).broadcast_to(full), ALU.mult))
                if c == 0 and tb:
                    dve.wait_ge(sel_tmm, tb)
                link(v.tensor_reduce(out=sel[0:w, c, :], in_=oh[0:w], axis=AX.X, op=ALU.add))

            def sel_gate_in(tb, w):
                v.tensor_tensor(sel[0:w, 2, :].rearrange("p (h k) -> p h k", k=TOPK), ts[0:w],
                                ts[0:w, :, 0:1].broadcast_to([w, PH, TOPK]), ALU.subtract).then_inc(gx_in, 1)

            def sel_gate_out(tb, w):
                sel2 = sel[0:w, 2, :].rearrange("p (h k) -> p h k", k=TOPK)
                dve.wait_ge(gx_exp, tb + 1)
                link(v.tensor_reduce(out=ssum[0:w, 0, :], in_=sel2, axis=AX.X, op=ALU.add))
                link(v.reciprocal(ssum[0:w, 1, :], ssum[0:w, 0, :]))
                v.tensor_tensor(sel2, sel2, ssum[0:w, 1, :].unsqueeze(2).broadcast_to([w, PH, TOPK]), ALU.mult).then_inc(sel_done, 1)

            u_low(0, 0)
            for tb in range(TB):
                w = tokens(tb)

                def low_half(i):
                    u_low(SEL_TILES * tb + 1 + i // 2, (1 + i // 2) % 2, [i % 2])

                if tb == 0:
                    best(N_PQ - 2)
                low_half(0)
                if tb == 0:
                    best(N_PQ - 1)
                    dve.wait_ge(top_done, N_PQ)
                low_half(1)
                sel_sums(tb, w)
                low_half(2)
                sel_max(tb, w, 0)
                low_half(3)
                sel_place(tb, w, 0)
                low_half(4)
                sel_strike(tb, w)
                low_half(5)
                sel_max(tb, w, 8)
                low_half(6)
                sel_place(tb, w, 8)
                low_half(7)
                sel_split(tb, w)
                sel_mark(tb, w, 0)
                low_half(8)
                sel_key(tb, w, 0)
                low_half(9)
                sel_mark(tb, w, 1)
                low_half(10)
                sel_key(tb, w, 1)
                sel_gate_in(tb, w)
                low_half(11)
                sel_gate_out(tb, w)
            dve.wait_ge(sel_tev, 3 * TB)

            def one_hots(g, s, t0, part, first=False):
                if part == 0 and not first:
                    dve.wait_ge(gm_mm, g - 1)
                for n in range(part * 4, part * 4 + 4):
                    def col(x):
                        return x[:, t0 + n:t0 + n + 1] if isinstance(t0, int) else x[:, bass.ds(t0 + n, 1)]
                    v.tensor_scalar(one_i[s][:, n, :], iota_f[:, :], col(iaT), None, ALU.is_equal)
                    op = v.tensor_scalar(gate_j[s][:, n, :], iota_f[:, :], col(ibT), col(gT), ALU.is_equal, ALU.mult)
                if part == 1:
                    op.then_inc(oh_v, 1)

            for g in range(2):
                for part in range(2):
                    one_hots(g, g, g * NTOK_G, part, True)
                    u_low(G_FIRST + 1 + g, (1 + g) % 2, [part])
            with dve.Fori(1, N_G // 2) as gg:
                for s in range(2):
                    for part in range(2):
                        one_hots(gg * 2 + s, s, gg * (2 * NTOK_G) + s * NTOK_G, part)
                        u_low(gg * 2 + (G_FIRST + 1 + s), 1 - s, [part])
            with dve.Fori(0, (N_U - G_FIRST - N_G) // 2 - 1) as hh:
                for s in range(2):
                    u_low(hh * 2 + (G_FIRST + N_G + 1 + s), 1 - s)
            u_low(N_U - 1, 1)

            def value_pair(n, i, first):
                for m in range(2):
                    if first and i == 0:
                        dve.wait_ge(v_hid, m + 1)
                        v.tensor_sub(v_lo[m][:, :], v_raw[m][:, :], v_hi[m][:, :].bitcast(F)).then_inc(v_lod, 1)
                    dve.wait_ge(wx_hid, n + (m + 1))
                    v.tensor_sub(wx_lo[i + m][:, :], wx[(i + m) % 2][:, :], wx_hi[i + m][:, :].bitcast(F)).then_inc(wx_lod, 1)

            def take_sums(at, ds):
                for d in ds:
                    dve.wait_ge(acc_ps, at + (d + 1))
                    v.tensor_add(as_halves(main[:, d, :]), halves(d % 4), as_halves(main[:, d, :])).then_inc(acc_done, 1)

            FRONT, BACK = range(12), range(12, KD)
            value_pair(0, 0, True)
            dve.wait_ge(hT_back, 16)
            take_sums(0, FRONT)
            value_pair(2, 2, True)
            take_sums(0, BACK)
            take_sums(16, FRONT)
            with dve.Fori(1, N_U // 4) as q:
                value_pair(q * 4, 0, False)
                take_sums(q * 32 - 16, BACK)
                take_sums(q * 32, FRONT)
                value_pair(q * 4 + 2, 2, False)
                take_sums(q * 32, BACK)
                take_sums(q * 32 + 16, FRONT)
            dve.wait_ge(wx_hid, N_U)
            added = 0
            for d in list(BACK) + [None]:
                if d is not None:
                    take_sums(N_U // 2 * KD - KD, [d])
                while added < (KD if d is None else d - 2 - 2 * (KD - 1 - d)):
                    dve.wait_ge(sq_done["nf"], added + 1)
                    if added == 0:
                        op = v.tensor_copy(wx[0][:, :], a_back[0][:, :])
                    else:
                        dve.wait_ge(sq_summed, TB + added)
                        op = v.tensor_add(wx[0][:, :], wx[0][:, :], a_back[added % 2][:, :])
                    op.then_inc(sq_summed, 1)
                    added += 1
            variance("nf", 1, 0, D, NORM_EPS)
            inverse("nf", 1)
            for k in range(KD):
                if k >= 2:
                    dve.wait_ge(yt_mm, k - 1)
                v.scalar_tensor_tensor(tmp[:, k % 2, :], main[:, k, :], gfc[:, k:k + 1], rstd[:, :], ALU.mult, ALU.mult).then_inc(n_val["nf"], 1)

        @block.tensor
        def _(pe):
            m_ = nc.tensor.matmul

            def tr(out, in_):
                n = in_.shape[0]
                return nc.tensor.transpose(out, in_, ident[0:n, 0:n])

            pe.wait_ge(pool_const, 7)
            for tb in range(TB):
                pe.wait_ge(x_loaded[tb % 2], 16 * (tb // 2 + 1))
                if tb >= 2:
                    pe.wait_ge(xt_ev_act, tb - 1)
                    pe.wait_ge(xt_ev_dve, tb - 1)
                w = tokens(tb)
                for k in range(KD):
                    ps = pair[2 * (tb % 2) + k // 8]
                    i = tr(ps[:, k // 4 % 2, (k % 4) * P:(k % 4) * P + w], x_in[0:w, tb % 2, k * P:(k + 1) * P])
                i.then_inc(xt_mm, 1)

            def sum_squares(key, sums):
                for hf in range(2):
                    op = m_(pair[0][:, hf, 0:TH], ones[:, :], sums[:, hf * TH:(hf + 1) * TH], start=True, stop=True)
                op.then_inc(sq_used[key], 1)

            def tile(whi, wlo, out, ks=range(KD), wait=None, starts=True, ends=True):
                ks = list(ks)
                for k in ks:
                    if wait:
                        wait(k)
                    for i, (w, x) in enumerate(((whi, act_hi), (whi, act_lo), (wlo, act_hi))):
                        for hf in range(2):
                            op = m_(pair[out][:, hf, 0:TH], w[:, k, :], x[:, k, hf * TH:(hf + 1) * TH],
                                    start=(starts and k == ks[0] and i == 0), stop=(ends and k == ks[-1] and i == 2))
                return op

            pe.wait_ge(xt_ev_act, TB)
            pe.wait_ge(xt_ev_dve, TB)
            pe.wait_ge(sq_summed, TB)
            sum_squares("n1", tmp[:, 0, :])

            def to_rows(i):
                if i < 8:
                    pe.wait_ge(out_dve, 8 + i + 1)
                    src = main[:, 8 + i, :]
                else:
                    pe.wait_ge(out_dve, 8 + i + 1)
                    src = tmp[:, i % 2, :]
                if i:
                    pe.wait_ge(nat_ev, 2 * i)
                else:
                    pe.wait_ge(pool_t_ev, 3)
                for tb in range(TB):
                    w = tokens(tb)
                    op = tr(pair[2][0:w, tb // 4, (tb % 4) * P:(tb % 4 + 1) * P], src[:, tb * P:tb * P + w])
                op.then_inc(nat_mm, 1)

            def first_tiles(g, key):
                pe.wait_ge(lo_done, g + 2)
                for k in range(KD):
                    pe.wait_ge(n_lo[key], k + 1)
                    op = tile(w_hi[0], w_lo[0], 0, [k], starts=(k == 0), ends=(k == KD - 1))
                    if k == KD - 1:
                        op.then_inc(tile_done, 1)
                    if k % 2:
                        tile(w_hi[1], w_lo[1], 1, [k // 2], starts=(k == 1), ends=False)
                tile(w_hi[1], w_lo[1], 1, range(KD // 2, KD), starts=False).then_inc(tile_done, 1)

            pe.wait_ge(n_var["n1"], 1)
            first_tiles(0, "n1")
            for t in range(2, T_G):
                pe.wait_ge(lo_done, t + 1)
                wait_w_in_out(pe, t - 2)
                tile(w_hi[t % 2], w_lo[t % 2], t % 2).then_inc(tile_done, 1)
                if t == T_Q:
                    n = DB * PSTATE
                    pe.wait_ge(pool_in, 16)
                    pe.wait_ge(out_dve, 8)
                    for k in range(8):
                        op = tr(pair[2][:, k // 4, (k % 4) * P:(k % 4) * P + n], st_rows[0:n, k * P:(k + 1) * P])
                    op.then_inc(pool_t_mm, 1)
                    for k in range(8):
                        op = tr(pair[3][0:PSTATE, k // 4, (k % 4) * P:(k % 4 + 1) * P], pT[:, k, SEQ - PSTATE:SEQ])
                    op.then_inc(pool_t_mm, 1)
                if t == T_Q + 1:
                    pe.wait_ge(pool_t_ev, 1)
                    for k in range(8):
                        op = tr(pair[2][0:NS, k // 4, (k % 4) * P:(k % 4 + 1) * P], pT[:, k, SEQ:T])
                    op.then_inc(pool_t_mm, 1)
                if T_K <= t < T_V:
                    i = t - T_K
                    pe.wait_ge(pw_in, 16 * (i + 1))
                    pe.wait_ge(pool_d, i // 2 + 1)
                    if i:
                        pe.wait_ge(pw_val, i)
                    else:
                        pe.wait_ge(pool_t_ev, 3)
                    for k in range(2):
                        for hf in range(2):
                            op = m_(pair[3][:, hf, 0:TH], pw[:, k, :],
                                    pT[:, 2 * (i // 2) + k, hf * TH:(hf + 1) * TH], start=(k == 0), stop=(k == 1))
                    op.then_inc(pw_mm, 1)
                if T_K <= t - 1:
                    to_rows(t - 1 - T_K)
            to_rows(15)

            def gate_quarter(n, i):
                g = T_G + n
                if i == 0:
                    pe.wait_ge(lo_done, g + 1)
                    wait_w_in_out(pe, g - 1)
                op = tile(w_hi[g % 2], w_lo[g % 2], 1, range(4 * i, 4 * i + 4), starts=(i == 0), ends=(i == 3))
                if i == 3:
                    op.then_inc(tile_done, 1)

            pe.wait_ge(out_act, 8)
            pe.wait_ge(out_dve, 24)
            pe.wait_ge(pw_val, 8)

            def scores(u):
                h, qb = divmod(u, 4)
                nk = (qb + 1) * P
                if u >= 2:
                    pe.wait_ge(pa_exp, 2 * (u - 1))
                for c in range(2):
                    r_ = slice(c * HD, (c + 1) * HD)
                    op = m_(pair[3 * (u % 2)][:, c, 0:nk], main[r_, h, qb * P:(qb + 1) * P], main[r_, 8 + h, 0:nk],
                            start=True, stop=True)
                op.then_inc(pa_s, 1)

            def turn(u):
                nk = u % 4 + 1
                pe.wait_ge(pa_a, u + 1)
                if u:
                    pe.wait_ge(pa_tev, u)
                else:
                    pe.wait_ge(nat_ev, 32)
                for k in range(nk):
                    op = tr(pair[2][:, 0, k * P:(k + 1) * P], pa_buf[u % 2][:, k * P:(k + 1) * P])
                op.then_inc(pa_tmm, 1)

            def output(u):
                h, nk = u // 4, u % 4 + 1
                pe.wait_ge(pa_tev, u + 1)
                if u:
                    pe.wait_ge(pa_oev, u)
                for k in range(nk):
                    op = m_(pair[2][:, 1, 0:P], v_nat[:, k, h * VD:(h + 1) * VD],
                            paT[u % 2][:, k, :], start=(k == 0), stop=(k == nk - 1))
                op.then_inc(pa_o, 1)

            scores(0)
            for u in range(4 * H):
                if u + 1 < 4 * H:
                    scores(u + 1)
                gate_quarter(u // 4, u % 4)
                turn(u)
                if u:
                    output(u - 1)
            output(4 * H - 1)

            def page_T(n):
                pe.wait_ge(kp_in[n % K_RING], 16 * (n // K_RING + 1))
                if n:
                    pe.wait_ge(sa_tev_a, n)
                    pe.wait_ge(sa_tev_d, n)
                if n % PAGES == 0 and n:
                    pe.wait_ge(sa_aT, 3 * (n // PAGES))
                for h in range(H):
                    op = tr(pair[0][:, h // 4, (h % 4) * P:(h % 4 + 1) * P], k_page[n % K_RING][:, h * P:(h + 1) * P])
                op.then_inc(sa_tmm, 1)

            def values(b, gs):
                for g in gs:
                    pe.wait_ge(vp_in[g % V_RING], 16 * (2 * b + g // V_RING + 1))
                    for h in range(H):
                        op = m_(pair[3][:, 1, h * DT:(h + 1) * DT], v_page[g % V_RING][:, h * VD:(h + 1) * VD],
                                s_aT[:, g, h * DT:(h + 1) * DT], start=(g == 0 and h == 0), stop=False, skip_group_check=True)
                return op

            for i in range(QUARTERS):
                gate_quarter(8, i)
            pe.wait_ge(pa_oev, 4 * H)
            page_T(0)
            for b in range(DB):
                j = 8 + 3 * b
                pe.wait_ge(sa_qd, 2 * (b + 1))
                pe.wait_ge(kn_done, 1)
                if b:
                    pe.wait_ge(sa_exp, 2 * b)
                for g in range(PAGES):
                    n = b * PAGES + g
                    if g + 1 < PAGES:
                        page_T(n + 1)
                    pe.wait_ge(sa_tev_a, n + 1)
                    pe.wait_ge(sa_tev_d, n + 1)
                    for h in range(H):
                        op = m_(pair[2][:, g // 4, (g % 4) * P:(g % 4 + 1) * P], qd[:, h * P:(h + 1) * P],
                                kT_page[n % 2][:, h, :], start=(h == 0), stop=(h == H - 1))
                    op.then_inc(sa_s, 1)
                    if b or g >= 4:
                        gate_quarter(j + g // 4, g % 4)
                if b:
                    pe.wait_ge(sa_aT, 3 * b)
                for h in range(H):
                    op = m_(pair[3][:, 0, 0:NS], qd[:, h * P:(h + 1) * P], k_new[:, h, :],
                            start=(h == 0), stop=(h == H - 1))
                op.then_inc(sa_s, 1)
                gate_quarter(j + 2, 0)
                gate_quarter(j + 2, 1)
                pe.wait_ge(sa_p, b + 1)
                for g in range(PAGES):
                    tr(pair[0][:, g // 4, (g % 4) * P:(g % 4 + 1) * P], sp_[:, g * P:(g + 1) * P])
                tr(pair[3][0:NS, 0, P:2 * P], sp_[:, 1024:1024 + NS]).then_inc(sa_ptmm, 1)
                gate_quarter(j + 2, 2)
                pe.wait_ge(sa_aT, 3 * (b + 1))
                if (b + 1) < DB:
                    page_T((b + 1) * PAGES)
                if b:
                    pe.wait_ge(sa_oev, b)
                values(b, range(V_RING)).then_inc(sa_half, 1)
                gate_quarter(j + 2, 3)
                values(b, range(V_RING, PAGES))
                for h in range(H):
                    op = m_(pair[3][:, 1, h * DT:(h + 1) * DT], v_nat[0:NS, 4, h * VD:(h + 1) * VD],
                            s_aTn[:, h * DT:(h + 1) * DT], start=False, stop=True, skip_group_check=True)
                op.then_inc(sa_o, 1)
            pe.wait_ge(out_act, 40)
            pe.wait_ge(sub_sel, 4)
            for h in range(H):
                pe.wait_ge(sq_done["sub"], h + 1)
                for hf in range(2):
                    op = m_(pair[0][0:H, hf, 0:TH], head_col[:, H - h:2 * H - h], mtmp[:, h % 2, hf * TH:(hf + 1) * TH],
                            start=(h == 0), stop=(h == H - 1))
                op.then_inc(sq_used["sub"], 1)

            def pool_part(d):
                g = G_BR + d
                pe.wait_ge(lo_done, g + 1)
                if d >= 2:
                    pe.wait_ge(merged_sum, d - 1)
                tile(w_hi[g % 2], w_lo[g % 2], 1 if d % 2 == 0 else 3, range(8, 16),
                     wait=(lambda k: pe.wait_ge(pl_lo, k - 7)) if d == 0 else None)

            pool_part(0)
            pe.wait_ge(sub_inv, 1)
            for h in range(H):
                if h >= 2:
                    pe.wait_ge(n_val["sub"], h - 1)
                for hf in range(2):
                    op = m_(pair[2 + h % 2][:, hf, 0:TH], head_row[:, h, :], rstd[0:H, hf * TH:(hf + 1) * TH], start=True, stop=True)
                op.then_inc(sub_all, 1)
            for d in range(N_BR):
                g = G_BR + d
                if d:
                    pool_part(d)
                tile(w_hi[g % 2], w_lo[g % 2], 0 if d % 2 == 0 else 2, range(8),
                     wait=(lambda k: pe.wait_ge(n_lo["sub"], k + 1)) if d == 0 else None).then_inc(tile_done, 1)
            for t in range(N_OUT):
                g = G_OUT + t
                pe.wait_ge(lo_done, g + 1)
                if t >= 2:
                    pe.wait_ge(out_dve, 24 + t - 1)
                tile(w_hi[g % 2], w_lo[g % 2], t % 2,
                     wait=(lambda k: pe.wait_ge(mg_lo, k + 1)) if t == 0 else None).then_inc(tile_done, 1)
            pe.wait_ge(out_dve, 24 + N_OUT)
            pe.wait_ge(sq_done["n2"], 1)
            sum_squares("n2", mtmp[:, 1, :])
            pe.wait_ge(n_var["n2"], 1)

            def key_scores(t):
                pe.wait_ge(q_evd, t + 1)
                pe.wait_ge(sk_tev, t + 1)
                if t >= 2:
                    pe.wait_ge(sc_ev, 2 * (t - 1))
                for tb in range(TB):
                    w = tokens(tb)
                    op = m_(pair[2 + t % 2][0:w, tb // 4, (tb % 4) * P:(tb % 4 + 1) * P],
                            q_ev[:, t % 2, tb * P:tb * P + w], skT[:, t % 2, :], start=True, stop=True)
                op.then_inc(sc_mm, 1)

            first_tiles(G_PQ, "n2")
            for t in range(N_PQ):
                g = G_PQ + t
                if t >= 2:
                    pe.wait_ge(lo_done, g + 1)
                    pe.wait_ge(q_evd, t - 1)
                    tile(w_hi[g % 2], w_lo[g % 2], t % 2).then_inc(tile_done, 1)
                pe.wait_ge(sk_in[t % 2], 16 * (t // 2 + 1))
                if t >= 2:
                    pe.wait_ge(sc_ev, 2 * (t - 1))
                tr(pair[2 + t % 2][:, 1, P:2 * P], sk_raw[:, t % 2, :]).then_inc(sk_tmm, 1)
                if t:
                    key_scores(t - 1)
            key_scores(N_PQ - 1)
            def turn_u(n, s, i, first=False):
                if i == 0:
                    pe.wait_ge(u_in[s], (n - s) * 8 + 16)
                if not first:
                    pe.wait_ge(u_lo, n * 2 + i)
                raw = w_raw[s][:, :, :].rearrange("p k c -> p (k c)")
                for k in range(8):
                    op = tr(pair[2][:, k // 4, (k % 4) * P:(k % 4 + 1) * P], raw[:, (8 * i + k) * P:(8 * i + k + 1) * P])
                op.then_inc(u_tmm, 1)

            def expert_tile(n, s, first=False, last=False):
                pe.wait_ge(u_lo, n * 2 + 2)
                if not first:
                    pe.wait_ge(a_gelu, n - 1)
                if not last:
                    turn_u(n + 1, 1 - s, 0)
                tile(w_hi[s], w_lo[s], s, range(8), ends=False)
                if not last:
                    turn_u(n + 1, 1 - s, 1)
                tile(w_hi[s], w_lo[s], s, range(8, KD), starts=False).then_inc(a_done, 1)

            def turn_selected(tb):
                w = tokens(tb)
                pe.wait_ge(sel_done, tb + 1)
                if tb:
                    pe.wait_ge(sel_tev, 3 * tb)
                else:
                    pe.wait_ge(sc_ev, 2 * N_PQ)
                for i in range(3):
                    op = tr(pair[3][:, 0, i * P:i * P + w], sel[0:w, i, :])
                op.then_inc(sel_tmm, 1)

            def gate_matrix(g, s, first=False):
                pe.wait_ge(oh_v, g + 1)
                if not first:
                    pe.wait_ge(gm_ev, g)
                for n in range(NTOK_G):
                    op = m_(pair[3][:, n // 4, (n % 4) * PK:(n % 4 + 1) * PK], one_i[s][:, n, :], gate_j[s][:, n, :],
                            start=True, stop=True)
                op.then_inc(gm_mm, 1)

            pe.wait_ge(sc_ev, 2 * N_PQ)
            pe.wait_ge(q_evd, N_PQ)
            turn_u(0, 0, 0, True)
            turn_u(0, 0, 1)
            for n in range(2):
                expert_tile(n, n, True)
            with pe.Fori(1, SEL_TILES // 2) as hh:
                for s in range(2):
                    expert_tile(hh * 2 + s, s)
            for tb in range(1, TB):
                for s in range(2):
                    expert_tile(tb * SEL_TILES + s, s)
                turn_selected(tb - 1)
                with pe.Fori(tb * SEL_TILES // 2 + 1, (tb + 1) * SEL_TILES // 2) as hh:
                    for s in range(2):
                        expert_tile(hh * 2 + s, s)
            turn_selected(TB - 1)
            pe.wait_ge(sel_tev, 3 * TB)
            for s in range(2):
                expert_tile(G_FIRST + s, s)
                gate_matrix(s, s, s == 0)
            with pe.Fori(1, N_G // 2) as gg:
                for s in range(2):
                    expert_tile(gg * 2 + (G_FIRST + s), s)
                    gate_matrix(gg * 2 + s, s)
            with pe.Fori(0, (N_U - G_FIRST - N_G) // 2 - 1) as hh:
                for s in range(2):
                    expert_tile(hh * 2 + (G_FIRST + N_G + s), s)
            expert_tile(N_U - 2, 0)
            expert_tile(N_U - 1, 1, last=True)
            pe.wait_ge(a_gelu, N_U)
            pe.wait_ge(gm_ev, N_G)

            def value_sums(n, i, at, first):
                pe.wait_ge(v_lod, n + 2)
                pe.wait_ge(wx_lod, n + 2)
                for d in range(KD):
                    if not first or d >= 4:
                        pe.wait_ge(acc_done, at + (d - 3))
                    c = slice(d * P, (d + 1) * P)
                    terms = [(w[m], x[m]) for m in (i, i + 1) for w, x in ((v_hi, wx_hi), (v_hi, wx_lo), (v_lo, wx_hi))]
                    for j, (w, x) in enumerate(terms):
                        for hf in range(2):
                            op = m_(pair[d % 4][:, hf, 0:TH], w[:, c], x[:, hf * TH:(hf + 1) * TH],
                                    start=(j == 0), stop=(j == 5))
                    op.then_inc(acc_ps, 1)

            value_sums(0, 0, 0, True)
            value_sums(2, 2, KD, False)
            with pe.Fori(1, N_U // 4) as q:
                value_sums(q * 4, 0, q * 32, False)
                value_sums(q * 4 + 2, 2, q * 32 + 16, False)
            pe.wait_ge(acc_done, N_U // 2 * KD)
            pe.wait_ge(sq_summed, TB + KD)
            sum_squares("nf", wx[0][:, :])
            for k in range(KD):
                pe.wait_ge(n_val["nf"], k + 1)
                if k >= 2:
                    pe.wait_ge(yt_ev, 2 * (k - 1))
                for tb in range(TB):
                    w = tokens(tb)
                    op = tr(pair[2 + k % 2][0:w, tb // 4, (tb % 4) * P:(tb % 4 + 1) * P], tmp[:, k % 2, tb * P:tb * P + w])
                op.then_inc(yt_mm, 1)


_INS = ["x_prompt", "x_sample", "cache_k", "cache_v", "state_pool", "page_table", "norm1_g", "w_in", "b_gate",
        "lambda_q1", "lambda_k1", "lambda_q2", "lambda_k2", "subln_g", "w_attn_branch", "pool_w", "pool_scale",
        "w_pool_branch", "w_out", "norm2_g", "w_peer_q", "peer_sub_keys", "peer_u", "peer_v", "norm_f_g"]
_OUTS = [(1, SEQ, D), (DB, DT, D), (1, 1, SEQ, H, 2, HD), (1, 1, SEQ, H, VD), (1, 1, PSTATE, POOLW),
         (1, DB, DT, H, 2, HD), (1, DB, DT, H, VD), (1, DB, PSTATE, POOLW)]


def kernel(**inputs):
    import numpy as _np
    import concourse.bacc as _bacc
    from concourse import mybir as _mybir
    from concourse.bass_utils import run_bass_kernel_spmd as _run

    nc = _bacc.Bacc("TRN2", target_bir_lowering=False, num_devices=1)
    arrays, args = {}, []
    for name in _INS:
        a = _np.ascontiguousarray(inputs[name])
        arrays[f"in_{name}_dram"] = a
        args.append(nc.dram_tensor(f"in_{name}_dram", a.shape, _mybir.dt.from_np(a.dtype), kind="ExternalInput").ap())
    for i, shape in enumerate(_OUTS):
        args.append(nc.dram_tensor(f"out_{i}_dram", shape, _mybir.dt.float32, kind="ExternalOutput").ap())
    hybrid_step(nc, *args)
    r = _run(nc, [arrays], core_ids=[0])
    return tuple(r.results[0][f"out_{i}_dram"] for i in range(len(_OUTS)))
```
